# Optimizing a Trainium2 kernel written in Bass

```python
import math
import jax, jax.numpy as jnp
from jax import lax
import numpy as np

D_MODEL = 1024
BATCH = 1
SEQ = 256
DEPTH = 2

CHUNK = 64
N_A = DEPTH // 2
N_B = DEPTH - N_A
N_DENSE = (DEPTH + 1) // 2
N_MOE = DEPTH // 2
GMLP_CHUNK = 128
A_FFN = 6 * D_MODEL
A_HALF = A_FFN // 2
A_GROUPS = 8
A_GROUP_DIM = A_HALF // A_GROUPS
B_HEAD_DIM = 64
B_HEADS = D_MODEL // B_HEAD_DIM
Q_BLOCK = 128
D_FF = ((8 * D_MODEL // 3 + 255) // 256) * 256
N_EXPERTS = 8
TOP_K = 2
D_EXPERT = 7 * D_MODEL // 2
RMS_EPS = 1e-6
NEG_INF = -1e30


def rms_norm(x, g):
    xf = x.astype(jnp.float32)
    y = xf * lax.rsqrt(jnp.mean(xf * xf, axis=-1, keepdims=True) + RMS_EPS)
    return (y * g.astype(jnp.float32)).astype(x.dtype)

def swiglu(x, w_in, w_out):
    a, b = jnp.split(x @ w_in, 2, axis=-1)
    return (jax.nn.silu(a) * b) @ w_out

def mixer_a(x, w_in, v_norm_g, w_spatial, b_spatial, w_out):
    B, S, _ = x.shape
    uv = jax.nn.gelu(x @ w_in, approximate=False)
    u, v = jnp.split(uv, 2, axis=-1)
    v = rms_norm(v, v_norm_g)
    v = v.reshape(B, S // GMLP_CHUNK, GMLP_CHUNK, A_GROUPS, A_GROUP_DIM)
    pos = jnp.arange(GMLP_CHUNK)
    mask = (pos[None, :] // CHUNK) <= (pos[:, None] // CHUNK)
    w = jnp.where(mask[None], w_spatial, jnp.zeros_like(w_spatial))
    v = jnp.einsum('gij,bcjgd->bcigd', w, v) + b_spatial.T[None, None, :, :, None]
    return (u * v.reshape(B, S, A_HALF)) @ w_out

def shared_kv(h, norm_g, w_kvf, b_f, k_norm_g):
    B, S, _ = h.shape
    s = rms_norm(h, norm_g)
    kvf = s @ w_kvf
    k = kvf[..., :D_MODEL].reshape(B, S, B_HEADS, B_HEAD_DIM)
    v = kvf[..., D_MODEL:2 * D_MODEL].reshape(B, S, B_HEADS, B_HEAD_DIM)
    f = kvf[..., 2 * D_MODEL:]
    k = rms_norm(k, k_norm_g).transpose(0, 2, 1, 3)
    v = v.transpose(0, 2, 1, 3)
    log_f = jax.nn.log_sigmoid((f + b_f).astype(jnp.float32))
    cum_log_f = jnp.cumsum(log_f, axis=1).transpose(0, 2, 1)
    return k, v, cum_log_f

def mixer_b(x, k, v, cum_log_f, w_in, q_norm_g, w_out):
    B, S, _ = x.shape
    qg = x @ w_in
    q, gate = jnp.split(qg, 2, axis=-1)
    q = rms_norm(q.reshape(B, S, B_HEADS, B_HEAD_DIM), q_norm_g).transpose(0, 2, 1, 3)
    scale = B_HEAD_DIM ** -0.5
    outs = []
    for blk in range(S // Q_BLOCK):
        qs, qe = blk * Q_BLOCK, (blk + 1) * Q_BLOCK
        logits = jnp.einsum('bhqd,bhkd->bhqk', q[:, :, qs:qe], k[:, :, :qe]).astype(jnp.float32) * scale
        logits = logits + cum_log_f[:, :, qs:qe, None] - cum_log_f[:, :, None, :qe]
        causal = jnp.arange(qs, qe)[:, None] >= jnp.arange(qe)[None, :]
        logits = jnp.where(causal[None, None], logits, NEG_INF)
        p = jax.nn.softmax(logits, axis=-1).astype(v.dtype)
        outs.append(jnp.einsum('bhqk,bhkd->bhqd', p, v[:, :, :qe]))
    o = jnp.concatenate(outs, axis=2).transpose(0, 2, 1, 3).reshape(B, S, D_MODEL)
    o = o * jax.nn.sigmoid(gate)
    return o @ w_out

def moe_swiglu(x, w_router, w_in, w_out):
    B, S, D = x.shape
    xt = x.reshape(B * S, D)
    logits = (xt @ w_router).astype(jnp.float32)
    top_v, top_i = lax.top_k(logits, TOP_K)
    top_w = jax.nn.softmax(top_v, axis=-1)
    gates = jnp.sum(jax.nn.one_hot(top_i, N_EXPERTS, dtype=jnp.float32) * top_w[..., None], axis=1)
    y = jnp.zeros_like(xt)
    for e in range(N_EXPERTS):
        y = y + gates[:, e:e + 1].astype(xt.dtype) * swiglu(xt, w_in[e], w_out[e])
    return y.reshape(B, S, D)

def first_inputs(seed: int = 0) -> dict:
    key = jax.random.key(seed)
    ks = jax.random.split(key, 24)

    def dense(k, shape, fan_in, s=1.0):
        return jax.random.normal(k, shape, jnp.float32) * (s * fan_in ** -0.5)

    def gain(k, shape):
        return 1.0 + 0.02 * jax.random.normal(k, shape, jnp.float32)

    return {
        "x": jax.random.normal(ks[0], (BATCH, SEQ, D_MODEL), jnp.float32),
        "a_norm_g": gain(ks[1], (N_A, D_MODEL)),
        "a_w_in": dense(ks[2], (N_A, D_MODEL, A_FFN), D_MODEL),
        "a_v_norm_g": gain(ks[3], (N_A, A_HALF)),
        "a_w_spatial": dense(ks[4], (N_A, A_GROUPS, GMLP_CHUNK, GMLP_CHUNK), GMLP_CHUNK, 0.5),
        "a_b_spatial": 1.0 + 0.1 * jax.random.normal(ks[5], (N_A, A_GROUPS, GMLP_CHUNK), jnp.float32),
        "a_w_out": dense(ks[6], (N_A, A_HALF, D_MODEL), A_HALF),
        "f_norm_g": gain(ks[7], (N_DENSE, D_MODEL)),
        "f_w_in": dense(ks[8], (N_DENSE, D_MODEL, 2 * D_FF), D_MODEL),
        "f_w_out": dense(ks[9], (N_DENSE, D_FF, D_MODEL), D_FF),
        "kv_norm_g": gain(ks[10], (D_MODEL,)),
        "kv_w": dense(ks[11], (D_MODEL, 2 * D_MODEL + B_HEADS), D_MODEL),
        "kv_b_f": 4.0 + 0.1 * jax.random.normal(ks[12], (B_HEADS,), jnp.float32),
        "k_norm_g": gain(ks[13], (B_HEAD_DIM,)),
        "b_norm_g": gain(ks[14], (N_B, D_MODEL)),
        "b_w_in": dense(ks[15], (N_B, D_MODEL, 2 * D_MODEL), D_MODEL),
        "q_norm_g": gain(ks[16], (N_B, B_HEAD_DIM)),
        "b_w_out": dense(ks[17], (N_B, D_MODEL, D_MODEL), D_MODEL),
        "m_norm_g": gain(ks[18], (N_MOE, D_MODEL)),
        "m_w_router": dense(ks[19], (N_MOE, D_MODEL, N_EXPERTS), D_MODEL),
        "m_w_in": dense(ks[20], (N_MOE, N_EXPERTS, D_MODEL, 2 * D_EXPERT), D_MODEL),
        "m_w_out": dense(ks[21], (N_MOE, N_EXPERTS, D_EXPERT, D_MODEL), D_EXPERT),
    }

def first_block(x, a_norm_g, a_w_in, a_v_norm_g, a_w_spatial, a_b_spatial, a_w_out,
              f_norm_g, f_w_in, f_w_out,
              kv_norm_g, kv_w, kv_b_f, k_norm_g,
              b_norm_g, b_w_in, q_norm_g, b_w_out,
              m_norm_g, m_w_router, m_w_in, m_w_out):
    h = x
    k = v = cum_log_f = None
    for layer in range(DEPTH):
        if layer < N_A:
            i = layer
            h = h + mixer_a(rms_norm(h, a_norm_g[i]), a_w_in[i], a_v_norm_g[i],
                            a_w_spatial[i], a_b_spatial[i], a_w_out[i])
        else:
            if layer == N_A:
                k, v, cum_log_f = shared_kv(h, kv_norm_g, kv_w, kv_b_f, k_norm_g)
            i = layer - N_A
            h = h + mixer_b(rms_norm(h, b_norm_g[i]), k, v, cum_log_f,
                            b_w_in[i], q_norm_g[i], b_w_out[i])
        if layer % 2 == 0:
            j = layer // 2
            h = h + swiglu(rms_norm(h, f_norm_g[j]), f_w_in[j], f_w_out[j])
        else:
            j = layer // 2
            h = h + moe_swiglu(rms_norm(h, m_norm_g[j]), m_w_router[j], m_w_in[j], m_w_out[j])
    return h


DEPTH_2 = 1

MIX_WIDTH = D_MODEL
ATT_HEADS = 8
ATT_HEAD_DIM = 64
ATT_W = ATT_HEADS * ATT_HEAD_DIM
ROPE_DIM = ATT_HEAD_DIM // 4
ROPE_THETA = 500000.0
MOBA_BLOCK = 256
MOBA_TOPK = 3
Q_BLOCK_2 = 64
MLSTM_HEADS = 4
MLSTM_QK_DIM = 64
MLSTM_V_DIM = 128
ML_QK_W = MLSTM_HEADS * MLSTM_QK_DIM
ML_V_W = MLSTM_HEADS * MLSTM_V_DIM
MLSTM_CHUNK = 64
D_FF_2 = 4 * D_MODEL
EPS = 1e-6
IN_SPLITS = (ATT_W, ATT_W, ATT_W, ML_QK_W, ML_QK_W, ML_V_W, ML_V_W, MLSTM_HEADS, MLSTM_HEADS)
IN_WIDTH = 3 * ATT_W + 2 * ML_QK_W + 2 * ML_V_W + 2 * MLSTM_HEADS


def rms_norm_2(x, g):
    xf = x.astype(jnp.float32)
    y = xf * lax.rsqrt(jnp.mean(xf * xf, axis=-1, keepdims=True) + EPS) * g.astype(jnp.float32)
    return y.astype(x.dtype)

def partial_rope(x, positions):
    inv_freq = ROPE_THETA ** (-jnp.arange(0, ROPE_DIM, 2, dtype=jnp.float32) / ROPE_DIM)
    ang = positions.astype(jnp.float32)[:, None, :, None] * inv_freq
    cos = jnp.cos(jnp.concatenate([ang, ang], axis=-1))
    sin = jnp.sin(jnp.concatenate([ang, ang], axis=-1))
    xr, xp = x[..., :ROPE_DIM], x[..., ROPE_DIM:]
    x1, x2 = xr[..., :ROPE_DIM // 2], xr[..., ROPE_DIM // 2:]
    xr = xr * cos + jnp.concatenate([-x2, x1], axis=-1) * sin
    return jnp.concatenate([xr, xp], axis=-1)

def moba_attention(q, k, v):
    B, H, S, Dh = q.shape
    nb = -(-S // MOBA_BLOCK)
    pad = nb * MOBA_BLOCK - S
    kp = jnp.pad(k, ((0, 0), (0, 0), (0, pad), (0, 0)))
    vp = jnp.pad(v, ((0, 0), (0, 0), (0, pad), (0, 0)))
    kb = kp.reshape(B, H, nb, MOBA_BLOCK, Dh)
    vb = vp.reshape(B, H, nb, MOBA_BLOCK, Dh)
    k_mean = jnp.mean(kb, axis=3)
    n_sel = min(MOBA_TOPK, nb)
    scale = Dh ** -0.5
    blk_ids = jnp.arange(nb)
    gather = jax.vmap(jax.vmap(lambda blocks, ids: blocks[ids]))

    def one_block(c):
        q0 = c * Q_BLOCK_2
        own = q0 // MOBA_BLOCK
        qc = lax.dynamic_slice_in_dim(q, q0, Q_BLOCK_2, axis=2)
        qpos = q0 + jnp.arange(Q_BLOCK_2)
        gate = jnp.einsum('bhqd,bhnd->bhqn', qc, k_mean)
        gate = jnp.where(blk_ids < own, gate, -jnp.inf)
        _, sel = lax.top_k(gate, n_sel)
        valid = sel < own
        k_sel = gather(kb, sel)
        v_sel = gather(vb, sel)
        s_sel = jnp.einsum('bhqd,bhqnkd->bhqnk', qc, k_sel) * scale
        s_sel = jnp.where(valid[..., None], s_sel, -jnp.inf).reshape(B, H, Q_BLOCK_2, n_sel * MOBA_BLOCK)
        k_own = lax.dynamic_slice_in_dim(kp, own * MOBA_BLOCK, MOBA_BLOCK, axis=2)
        v_own = lax.dynamic_slice_in_dim(vp, own * MOBA_BLOCK, MOBA_BLOCK, axis=2)
        kpos = own * MOBA_BLOCK + jnp.arange(MOBA_BLOCK)
        s_own = jnp.einsum('bhqd,bhkd->bhqk', qc, k_own) * scale
        s_own = jnp.where(kpos[None, :] <= qpos[:, None], s_own, -jnp.inf)
        p = jax.nn.softmax(jnp.concatenate([s_sel, s_own], axis=-1).astype(jnp.float32), axis=-1)
        p_sel = p[..., :n_sel * MOBA_BLOCK].reshape(B, H, Q_BLOCK_2, n_sel, MOBA_BLOCK)
        p_own = p[..., n_sel * MOBA_BLOCK:]
        return (jnp.einsum('bhqnk,bhqnkd->bhqd', p_sel, v_sel)
                + jnp.einsum('bhqk,bhkd->bhqd', p_own, v_own))

    out = lax.map(one_block, jnp.arange(S // Q_BLOCK_2))
    return jnp.transpose(out, (1, 2, 0, 3, 4)).reshape(B, H, S, Dh)

def mlstm_chunkwise(q, k, v, ig, lf):
    B, H, S, dk = q.shape
    dv = v.shape[-1]
    L = MLSTM_CHUNK
    nc = S // L

    def chunks(a):
        return jnp.moveaxis(a.reshape((B, H, nc, L) + a.shape[3:]), 2, 0)

    causal = jnp.tril(jnp.ones((L, L), dtype=bool))

    def step(carry, xs):
        C, n, m = carry
        qc, kc, vc, ic, fc = xs
        b = jnp.cumsum(fc, axis=-1)
        d = b[..., :, None] - b[..., None, :] + ic[..., None, :]
        d = jnp.where(causal, d, -jnp.inf)
        m_inter = b + m[..., None]
        m_t = jnp.maximum(m_inter, jnp.max(d, axis=-1))
        s = jnp.einsum('bhtd,bhsd->bhts', qc, kc) * jnp.exp(d - m_t[..., None])
        decay = jnp.exp(m_inter - m_t)
        num = (jnp.einsum('bhts,bhsv->bhtv', s, vc)
               + decay[..., None] * jnp.einsum('bhtd,bhdv->bhtv', qc, C))
        den = jnp.sum(s, axis=-1) + decay * jnp.einsum('bhtd,bhd->bht', qc, n)
        h = num / jnp.maximum(jnp.abs(den), jnp.exp(-m_t))[..., None]
        b_last = b[..., -1]
        g = b_last[..., None] - b + ic
        m_new = jnp.maximum(b_last + m, jnp.max(g, axis=-1))
        carry_decay = jnp.exp(b_last + m - m_new)
        wg = jnp.exp(g - m_new[..., None])
        C_new = carry_decay[..., None, None] * C + jnp.einsum('bhs,bhsd,bhsv->bhdv', wg, kc, vc)
        n_new = carry_decay[..., None] * n + jnp.einsum('bhs,bhsd->bhd', wg, kc)
        return (C_new, n_new, m_new), h

    init = (jnp.zeros((B, H, dk, dv), jnp.float32),
            jnp.zeros((B, H, dk), jnp.float32),
            jnp.zeros((B, H), jnp.float32))
    _, h = lax.scan(step, init, (chunks(q), chunks(k), chunks(v), chunks(ig), chunks(lf)))
    return jnp.moveaxis(h, 0, 2).reshape(B, H, S, dv)

def hybrid_layer(x, positions, g_mix_pre, w_in, b_igate, b_fgate, g_mlstm_out, w_out,
                 g_mix_post, g_mlp_pre, w_up, w_down, g_mlp_post):
    B, S, _ = x.shape
    hdn = rms_norm_2(x, g_mix_pre)
    proj = hdn @ w_in
    aq, ak, av, mq, mk, mv, mo, mi, mf = jnp.split(proj, [int(c) for c in np.cumsum(IN_SPLITS)[:-1]], axis=-1)

    def to_heads(t, nh):
        return t.reshape(B, S, nh, -1).transpose(0, 2, 1, 3).astype(jnp.float32)

    q_a = partial_rope(to_heads(aq, ATT_HEADS), positions)
    k_a = partial_rope(to_heads(ak, ATT_HEADS), positions)
    v_a = to_heads(av, ATT_HEADS)
    att = moba_attention(q_a, k_a, v_a)
    att = att.transpose(0, 2, 1, 3).reshape(B, S, ATT_W)

    q_m = to_heads(mq, MLSTM_HEADS)
    k_m = to_heads(mk, MLSTM_HEADS) * (MLSTM_QK_DIM ** -0.5)
    v_m = to_heads(mv, MLSTM_HEADS)
    ig = (mi.astype(jnp.float32) + b_igate.astype(jnp.float32)).transpose(0, 2, 1)
    lf = jax.nn.log_sigmoid(mf.astype(jnp.float32) + b_fgate.astype(jnp.float32)).transpose(0, 2, 1)
    hm = mlstm_chunkwise(q_m, k_m, v_m, ig, lf)
    hm = hm * lax.rsqrt(jnp.mean(hm * hm, axis=-1, keepdims=True) + EPS)
    hm = hm.transpose(0, 2, 1, 3).reshape(B, S, ML_V_W) * g_mlstm_out.astype(jnp.float32)
    hm = hm * jax.nn.sigmoid(mo.astype(jnp.float32))

    mixed = jnp.concatenate([att, hm], axis=-1).astype(x.dtype)
    x = x + rms_norm_2(mixed @ w_out, g_mix_post)

    u = rms_norm_2(x, g_mlp_pre) @ w_up
    u = jnp.square(jax.nn.relu(u))
    x = x + rms_norm_2(u @ w_down, g_mlp_post)
    return x

def second_inputs(seed: int = 0) -> dict:
    key = jax.random.key(seed)
    ks = jax.random.split(key, 14)
    f32 = jnp.float32

    def gain(k, n):
        return 1.0 + 0.02 * jax.random.normal(k, (DEPTH_2, n), f32)

    x = jax.random.normal(ks[0], (BATCH, SEQ, D_MODEL), f32)
    positions = jnp.broadcast_to(jnp.arange(SEQ, dtype=jnp.int32), (BATCH, SEQ))
    g_mix_pre = gain(ks[1], D_MODEL)
    w_in = jax.random.normal(ks[2], (DEPTH_2, D_MODEL, IN_WIDTH), f32) * D_MODEL ** -0.5
    b_igate = 0.1 * jax.random.normal(ks[3], (DEPTH_2, MLSTM_HEADS), f32)
    b_fgate = (jnp.linspace(3.0, 6.0, MLSTM_HEADS, dtype=f32)[None, :]
               + 0.1 * jax.random.normal(ks[4], (DEPTH_2, MLSTM_HEADS), f32))
    g_mlstm_out = gain(ks[5], ML_V_W)
    w_out = jax.random.normal(ks[6], (DEPTH_2, MIX_WIDTH, D_MODEL), f32) * MIX_WIDTH ** -0.5
    g_mix_post = gain(ks[7], D_MODEL)
    g_mlp_pre = gain(ks[8], D_MODEL)
    w_up = jax.random.normal(ks[9], (DEPTH_2, D_MODEL, D_FF_2), f32) * D_MODEL ** -0.5
    w_down = jax.random.normal(ks[10], (DEPTH_2, D_FF_2, D_MODEL), f32) * D_FF_2 ** -0.5
    g_mlp_post = gain(ks[11], D_MODEL)
    return {"x": x, "positions": positions, "g_mix_pre": g_mix_pre, "w_in": w_in,
            "b_igate": b_igate, "b_fgate": b_fgate, "g_mlstm_out": g_mlstm_out, "w_out": w_out,
            "g_mix_post": g_mix_post, "g_mlp_pre": g_mlp_pre, "w_up": w_up, "w_down": w_down,
            "g_mlp_post": g_mlp_post}

def second_block(x, positions, g_mix_pre, w_in, b_igate, b_fgate, g_mlstm_out, w_out,
              g_mix_post, g_mlp_pre, w_up, w_down, g_mlp_post):
    for layer in range(DEPTH_2):
        x = hybrid_layer(x, positions, g_mix_pre[layer], w_in[layer], b_igate[layer], b_fgate[layer],
                         g_mlstm_out[layer], w_out[layer], g_mix_post[layer], g_mlp_pre[layer],
                         w_up[layer], w_down[layer], g_mlp_post[layer])
    return x


def setup_inputs(seed=0):
    out = dict(first_inputs(seed))
    for name, value in second_inputs(seed + 1).items():
        if name != "x":
            out[name + "_2"] = value
    return out


def reference(
    x, a_norm_g, a_w_in, a_v_norm_g, a_w_spatial, a_b_spatial, a_w_out, f_norm_g, f_w_in,
    f_w_out, kv_norm_g, kv_w, kv_b_f, k_norm_g, b_norm_g, b_w_in, q_norm_g, b_w_out, m_norm_g,
    m_w_router, m_w_in, m_w_out, positions_2, g_mix_pre_2, w_in_2, b_igate_2, b_fgate_2,
    g_mlstm_out_2, w_out_2, g_mix_post_2, g_mlp_pre_2, w_up_2, w_down_2, g_mlp_post_2,
):
    x = first_block(
        x, a_norm_g, a_w_in, a_v_norm_g, a_w_spatial, a_b_spatial, a_w_out, f_norm_g, f_w_in,
        f_w_out, kv_norm_g, kv_w, kv_b_f, k_norm_g, b_norm_g, b_w_in, q_norm_g, b_w_out,
        m_norm_g, m_w_router, m_w_in, m_w_out,
    )
    return second_block(
        x, positions_2, g_mix_pre_2, w_in_2, b_igate_2, b_fgate_2, g_mlstm_out_2, w_out_2,
        g_mix_post_2, g_mlp_pre_2, w_up_2, w_down_2, g_mlp_post_2,
    )


_drawn_inputs = setup_inputs


def setup_inputs(seed=0):
    import zlib

    import numpy as np

    out = dict(_drawn_inputs(seed))
    spreads = {}
    factors = {'kv_norm_g': 8.0,
     'kv_b_f': 2.775,
     'k_norm_g': 2.831,
     'b_norm_g': 3.402,
     'q_norm_g': 8.0,
     'b_igate_2': 64.0,
     'g_mlstm_out_2': 66.917,
     'g_mix_post_2': 54.525,
     'g_mlp_pre_2': 55.826,
     'g_mlp_post_2': 84.64,
     'm_norm_g': 4.067}
    for name, (base, spread) in spreads.items():
        noise = np.random.default_rng([zlib.crc32(name.encode()), seed]).standard_normal(out[name].shape)
        drawn = base * np.exp(spread * noise) if base else spread * noise
        out[name] = __import__('jax').numpy.asarray(drawn.astype(out[name].dtype))
    for name, factor in factors.items():
        out[name] = (out[name] * factor).astype(out[name].dtype)
    return out
```

```python
from contextlib import ExitStack
import math

import numpy as np

import concourse.bass as bass
from concourse import mybir

ALU = mybir.AluOpType
ACT = mybir.ActivationFunctionType
F32 = mybir.dt.float32
I32 = mybir.dt.int32
U32 = mybir.dt.uint32
F32R = mybir.dt.float32r
AX_X = mybir.AxisListType.X

P = 128
S = 256
NT = S // P
D = 1024
KD = D // P
BANK = 512
SLAB = KD * BANK
SLOTS = 7
EPS = 1e-6
MASKED = -1e30

A_HALF = 3072
GROUPS = 8
GDIM = A_HALF // GROUPS
GCH = GDIM // P
A_CHUNKS = A_HALF // P
D_FF = 2816
PAIR = BANK // 2
FF_SLABS = D_FF // PAIR
FF_CHUNKS = D_FF // P
HEADS = 16
HD = 64
AUG = HD + 2
KA, QA = 0, HEADS * AUG
VA, GA = 2 * HEADS * AUG, 2 * HEADS * AUG + D
ROW = GA + D
E = 8
D_EXP = 3584
UPS = D_EXP // PAIR
DOWNS = D_EXP // (4 * P)
ATT_H = 8
ML_H = 4
ML_V = 128
Q2, K2, V2, MQ, MK, MV, MO = 0, 512, 1024, 1536, 1792, 2048, 2560
PROJ = 3072
ROPE_HALF = 8
ROPE_THETA = 500000.0
D_FF2 = 4096
FF2_SLABS = D_FF2 // BANK
FF2_CHUNKS = D_FF2 // P

ORDER = [("up", 0), ("up", 1)]
for _p in range(DOWNS - 1):
    ORDER += [("up", 2 * _p + 2), ("up", 2 * _p + 3), ("down", _p)]
ORDER.append(("down", DOWNS - 1))
UNIT = SLAB // 2
UNITS = 2 * len(ORDER)
RAW_E = 7
HI_AT = [7, 12, 13, 8, 9, 10]
HI_E = len(HI_AT)
LEAD = 2
assert len(ORDER) == UPS + DOWNS and UNITS % RAW_E == 0 and UNITS % HI_E == 0
TURNS = ["route" if _g == 1 else (_g if _g == 0 else _g - 1) for _g in range(DOWNS + 1)]
TURN_OF = {what: g for g, what in enumerate(TURNS)}


class Steps:

    def __init__(self, eng, sem):
        self.eng, self.sem, self.n, self.offset = eng, sem, 0, 0

    def then(self, ins):
        ins.then_inc(self.sem, 1)
        self.n += 1
        self.eng.wait_ge(self.sem, self.offset + self.n)


def build(nc, t, out):
    with ExitStack() as ctx:
        def sb(name, shape, dt=F32):
            return ctx.enter_context(nc.sbuf_tensor(name, shape, dt))

        def sem(name):
            return ctx.enter_context(nc.semaphore(name))

        arena_at = -(-nc.sbuf_base // 32) * 32
        ctx.enter_context(nc.sbuf_tensor("arena", [P, SLOTS * SLAB + NT * ROW + 8], F32))

        def place(cols, at, name, dt):
            return nc.alloc_sbuf_tensor_at(name, [P, cols], dt, offset=arena_at + 4 * at)

        ring = place(SLOTS * SLAB, 0, "ring", F32)
        e_arrived = place(RAW_E * UNIT, 0, "e_arrived", F32)
        e_low = place(RAW_E * UNIT, 0, "e_low", F32R)
        e_high = place(2 * SLOTS * UNIT - RAW_E * UNIT, RAW_E * UNIT, "e_high", F32R)
        work_all = place(NT * ROW, SLOTS * SLAB, "work_all", F32)
        work_r = place(NT * ROW, SLOTS * SLAB, "work_r", F32R)
        hT_all = sb("hT_all", [P, 32 * S])
        h_all = sb("h_all", [P, NT * D])
        xT_all = sb("xT_all", [P, KD * S])
        xn_all = sb("xn_all", [P, NT * D])
        ident = sb("ident", [P, P])
        causal = sb("causal", [P, S])
        upto = sb("upto", [P, P])
        ones = sb("ones", [P, P])
        iota = sb("iota", [P, P])
        gains = sb("gains", [P, 74])
        w_forget = sb("w_forget", [P, KD, HEADS])
        w_router = sb("w_router", [P, KD, E])
        w_if = sb("w_if", [P, KD, 2 * ML_H])
        b_forget = sb("b_forget", [P, HEADS])
        b_if = sb("b_if", [P, 2 * ML_H])
        stats = sb("stats", [P, 368])
        routing = sb("routing", [P, 160])
        indices = sb("indices", [P, 2, 8], U32)
        rounds_i = sb("rounds_i", [P, 2], I32)
        pos_i = sb("pos_i", [P, NT], I32)
        turn_i = sb("turn_i", [P, NT * ROPE_HALF], I32)
        rope = sb("rope", [P, 8, NT * ROPE_HALF])

        G = [ctx.enter_context(nc.psum_tensor(f"G{i}", [P, BANK], F32)) for i in range(4)]
        SM = [ctx.enter_context(nc.psum_tensor(f"SM{i}", [P, BANK], F32)) for i in range(2)]
        T = [ctx.enter_context(nc.psum_tensor(f"T{i}", [P, BANK], F32)) for i in range(2)]

        hT = hT_all[:, :].rearrange("p (k s) -> p k s", s=S)
        work = work_all[:, :].rearrange("p (c n) -> p c n", c=NT)
        h = h_all[:, :].rearrange("p (c n) -> p c n", c=NT)
        xn = xn_all[:, :].rearrange("p (c n) -> p c n", c=NT)
        xT = xT_all[:, :].rearrange("p (k s) -> p k s", s=S)
        xT2 = hT[:, 0:KD, :]
        ws_raw = hT_all[:, 24 * S:24 * S + GROUPS * P].rearrange("p (g j) -> p g j", g=GROUPS)
        gain_rows = hT_all[0:74, 23 * S:23 * S + P]
        wsT = hT_all[:, 28 * S:28 * S + GROUPS * P]
        post_gain1 = work[:, 0, PROJ:PROJ + D]
        post_gain2 = work[:, 0, 0:D]

        def slot(j):
            return ring[:, j * SLAB:(j + 1) * SLAB]

        ss = stats[:, 0:2]
        rstd = stats[:, 2:4]
        vss = stats[:, 4:4 + NT * GROUPS]
        ss4 = stats[:, 20:24]
        head_ss = stats[:, 24:88]
        nmax = stats[:, 88:120]
        rowsum = stats[:, 120:152]
        rinv = stats[:, 152:184]
        rmax = stats[:, 184:216]
        expm = stats[:, 216:224]
        hss = stats[:, 224:232]
        tokf = stats[:, 232:234]
        variance = stats[:, 240:304]
        root = stats[:, 304:368]
        correction = stats[:, 88:152]

        GC = {"a": 0, "f": 8, "kv": 16, "b": 24, "m": 32, "pre2": 40, "mlp2": 48, "mix": 56, "bs": 64, "kq": 72}

        x_landed = sem("x_landed")
        params_landed = sem("params_landed")
        spatial_landed = sem("spatial_landed")
        consts_ready = sem("consts_ready")
        pool_step = sem("pool_step")
        vector_step = sem("vector_step")
        scalar_step = sem("scalar_step")
        gain_rows_ready = sem("gain_rows_ready")
        h_ready = sem("h_ready")
        variance_ready = sem("variance_ready")
        root_ready = sem("root_ready")
        hm_ready = sem("hm_ready")
        squares_ready = sem("squares_ready")
        xn_ready = sem("xn_ready")
        turned = sem("turned")
        turned_copied = [sem("turned_copied_v"), sem("turned_copied_s")]
        turned2 = sem("turned2")
        turned2_copied = [sem("turned2_copied_v"), sem("turned2_copied_s")]
        down_full = sem("down_full")
        spatial_ready = sem("spatial_ready")
        mixed_full = sem("mixed_full")
        mixed_read = sem("mixed_read")
        gated_ready = sem("gated_ready")
        silu_ready = sem("silu_ready")
        small_full = sem("small_full")
        z_ready = sem("z_ready")
        ez_ready = sem("ez_ready")
        ez1_ready = sem("ez1_ready")
        ln_ready = sem("ln_ready")
        logf_ready = sem("logf_ready")
        aug_ready = sem("aug_ready")
        gap_exp = sem("gap_exp")
        mask_ready = sem("mask_ready")
        rounds_ready = sem("rounds_ready")
        angle_ready = sem("angle_ready")
        sines_ready = sem("sines_ready")
        relu_ready = sem("relu_ready")
        relu2_ready = sem("relu2_ready")
        post_squares = sem("post_squares")
        post_landed = sem("post_landed")
        out_landed = sem("out_landed")

        class Phase:

            def __init__(self, name, slabs, slots, dmas=1, uses=2):
                self.name, self.slabs, self.slots, self.dmas, self.uses = name, slabs, slots, dmas, uses
                self.landed = [sem(f"{name}_landed{j}") for j in range(len(slots))]
                if uses:
                    self.full = sem(f"{name}_full")
                    self.done = sem(f"{name}_done")
                else:
                    self.used = sem(f"{name}_used")

        av = Phase("av", GROUPS, [0, 1])
        au = Phase("au", GROUPS, [2, 3], dmas=2)
        ao = Phase("ao", A_CHUNKS // 4, [4, 5], uses=0)
        fu = Phase("fu", FF_SLABS, [0, 1])
        fo = Phase("fo", FF_CHUNKS // 2, [2, 3], uses=0)
        kv = Phase("kv", 4, [4, 5])
        qg = Phase("qg", 4, [0, 1])
        bo = Phase("bo", 2, [4, 5], uses=0)
        pr = Phase("pr", PROJ // BANK, [0, 1])
        po = Phase("po", 2, [2, 3], uses=0)
        mu = Phase("mu", FF2_SLABS, [4, 5])
        md = Phase("md", FF2_SLABS, [0, 1], uses=0)

        class Attention:
            def __init__(self, name):
                self.full = sem(f"{name}_logits_full")
                self.max_ready = sem(f"{name}_max_ready")
                self.p_ready = sem(f"{name}_p_ready")
                self.out_full = sem(f"{name}_out_full")
                self.out_done = sem(f"{name}_out_done")

        att1, att2, mls = Attention("att1"), Attention("att2"), Attention("mlstm")
        weights_ready = sem("mlstm_weights_ready")
        out_gate_ready = sem("out_gate_ready")

        e_landed = [sem(f"expert_landed{j}") for j in range(RAW_E)]
        e_hi = sem("expert_hi")
        e_lo = sem("expert_lo")
        up_half_used = sem("up_half_used")
        up_full = sem("up_full")
        up_read = sem("up_read")
        e_silu_ready = sem("e_silu_ready")
        down_used = sem("down_used")
        y_full = sem("y_full")
        y_copied = [sem("y_copied_s"), sem("y_copied_v")]
        gather_full = sem("gather_full")
        gathered = [sem("gathered_s"), sem("gathered_v")]
        scatter_full = sem("scatter_full")
        scatter_added = sem("scatter_added")
        pick_ready = sem("pick_ready")
        route_ready = sem("route_ready")
        e_turned = sem("e_turned")
        e_turned_hi = sem("e_turned_hi")
        e_turned_lo = sem("e_turned_lo")

        y_sb = work_all[:, 0:D]
        routeT = work_all[:, 1024:1280]
        pick = work_all[:, 1280:1536].rearrange("p (c s) -> p c s", c=NT)
        route = work_all[:, 1536:1792].rearrange("p (c s) -> p c s", c=NT)
        e_silu = work_all[:, 1792:2304].rearrange("p (b n) -> p b n", b=2)
        e_hid = work_all[:, 2304:2816].rearrange("p (b n) -> p b n", b=2)
        e_hT_hi = work_r[:, 2816:3840].rearrange("p (b n) -> p b n", b=2)
        e_hT_lo = work_r[:, 3840:4864].rearrange("p (b n) -> p b n", b=2)
        xg_hi = work_r[:, 4864:4864 + KD * P]
        xg_lo = work_r[:, 5888:5888 + KD * P]

        COLS = 2 * E + 1
        logit = routing[:, 0:16].rearrange("p (c e) -> p c e", c=NT)
        top8 = routing[:, 16:32].rearrange("p (c e) -> p c e", c=NT)
        topi = routing[:, 32:48].rearrange("p (c e) -> p c e", c=NT)
        sel = routing[:, 48:64].rearrange("p (c e) -> p c e", c=NT)
        rank = routing[:, 64:64 + NT * COLS].rearrange("p (c e) -> p c e", c=NT)
        gate = routing[:, 100:100 + NT * COLS].rearrange("p (c e) -> p c e", c=NT)
        tmp8 = routing[:, 136:144]
        gap = routing[:, 144:146]
        g1 = routing[:, 146:148]
        g2 = routing[:, 148:150]
        total = routing[:, 150:151]
        roundsf = routing[:, 151:152]

        a_in = t["a_w_in"][0].rearrange("(k p) n -> p k n", p=P)
        a_out = t["a_w_out"][0].rearrange("(s k p) n -> s p k n", p=P, k=4)
        f_in = t["f_w_in"][0].rearrange("(k p) n -> p k n", p=P)
        f_out = t["f_w_out"][0].rearrange("(s k p) n -> s p k n", p=P, k=2)
        kv_w = t["kv_w"].rearrange("(k p) n -> p k n", p=P)
        b_in = t["b_w_in"][0].rearrange("(k p) n -> p k n", p=P)
        b_out = t["b_w_out"][0].rearrange("(s k p) n -> s p k n", p=P, k=4)
        m_in = t["m_w_in"][0].rearrange("e (k p) (b n) -> e p k b n", p=P, b=2)
        m_out = t["m_w_out"][0].rearrange("e (s k p) n -> e s p k n", p=P, k=2)
        w_in2 = t["w_in_2"][0].rearrange("(k p) n -> p k n", p=P)
        w_out2 = t["w_out_2"][0].rearrange("(s k p) n -> s p k n", p=P, k=4)
        w_up2 = t["w_up_2"][0].rearrange("(k p) n -> p k n", p=P)
        w_down2 = t["w_down_2"][0].rearrange("(s k p) n -> s p k n", p=P, k=4)

        def cols(j, n):
            return slot(j)[:, 0:KD * n].rearrange("p (k n) -> p k n", k=KD)

        def rows(j, k):
            return slot(j)[:, 0:k * D].rearrange("p (k n) -> p k n", k=k)

        last_scatter = sem("last_scatter")

        def running_sums(pe, x, n):
            nc.tensor.matmul(SM[1][:, 0:n], upto[:, :], x[:, 0, :], start=True, stop=True)
            nc.tensor.matmul(SM[1][:, n:2 * n], ones[:, :], x[:, 0, :], start=True, stop=False)
            return nc.tensor.matmul(SM[1][:, n:2 * n], upto[:, :], x[:, 1, :], start=False, stop=True)


        v_squared = sem("v_squared")
        gap_diff = sem("gap_diff")
        bsum_ready = sem("bsum_ready")

        def log_sigmoid(dve, V, steps, z, w, dst, ez_ready, ez1_ready, ln_ready, logf_ready, n, z_ready):
            dve.wait_ge(ez_ready, n)
            V.tensor_scalar(w, w, 1.0, None, ALU.add).then_inc(ez1_ready, 1)
            dve.wait_ge(ln_ready, n)
            dve.wait_ge(z_ready, n)
            V.scalar_tensor_tensor(out=dst, in0=z, scalar=0.0, in1=w, op0=ALU.min, op1=ALU.subtract).then_inc(logf_ready, 1)


        def softplus(eng, steps, z, w, z_ready, ez_ready, ez1_ready, ln_ready, n):
            eng.wait_ge(z_ready, n)
            steps.then(nc.scalar.activation(w, z, ACT.Abs))
            nc.scalar.activation(w, w, ACT.Exp, scale=-1.0).then_inc(ez_ready, 1)
            eng.wait_ge(ez1_ready, n)
            nc.scalar.activation(w, w, ACT.Ln).then_inc(ln_ready, 1)

        def e_consumed(eng, it, n):
            kind, s = ORDER[n // 2]
            if kind == "up":
                eng.wait_ge(up_full if n % 2 else up_half_used, it * UPS + (s + 1))
            elif n < UNITS - 1:
                eng.wait_ge(down_used, it * (2 * DOWNS - 1) + (2 * s + n % 2 + 1))
            else:
                eng.wait_ge(y_full, it * 2 + 2)

        def e_raw(n, memory):
            return memory[:, (n % RAW_E) * UNIT:(n % RAW_E + 1) * UNIT]

        def e_hi_unit(n):
            at = HI_AT[n % HI_E] - RAW_E
            return e_high[:, at * UNIT:(at + 1) * UNIT]

        def e_make_hi(act, it, n):
            act.wait_ge(e_landed[n % RAW_E], it * (32 * (UNITS // RAW_E)) + 32 * (n // RAW_E + 1))
            if n >= HI_E:
                e_consumed(act, it, n - HI_E)
            elif n >= LEAD:
                act.wait_ge(down_used, it * (2 * DOWNS - 1))
                act.wait_ge(y_full, it * 2)
            nc.scalar.copy(e_hi_unit(n), e_raw(n, e_arrived)).then_inc(e_hi, 1)

        def e_make_lo(dve, it, n):
            dve.wait_ge(e_hi, it * UNITS + (n + 1))
            nc.vector.tensor_tensor(e_raw(n, e_low), e_raw(n, e_arrived), e_hi_unit(n).bitcast(F32), ALU.subtract
                                    ).then_inc(e_lo, 1)

        def expert_hidden_free(eng, it, p):
            if p >= 2:
                eng.wait_ge(down_used, it * (2 * DOWNS - 1) + 2 * (p - 1))
            elif p == 0:
                eng.wait_ge(y_full, it * 2)
            else:
                eng.wait_ge(down_used, it * (2 * DOWNS - 1))

        def second_head_copy(copy, mul, g, bank):
            if g < 12:
                dst = hT[0:HD, 2 * g:2 * g + 2, :]
                src = bank[0:HD, :].rearrange("p (h s) -> p h s", h=2)
                if g < 4 or g >= 10:
                    return mul(dst, src, HD ** -0.5)
                return copy(dst, src)
            return copy(hT[0:2, 2 * g:2 * g + 2, :], bank[0:2, :].rearrange("p (h s) -> p h s", h=2))

        block = ctx.enter_context(nc.Block())

        @block.sync
        def _(sp):
            def stream(ph, load, handover):
                n = len(ph.slots)

                def used(i):
                    if ph.uses:
                        done = mixed_read if ph is au else ph.full
                        sp.wait_ge(done, (i + 1) * ph.uses)
                    else:
                        sp.wait_ge(ph.used, i + 1)

                for j in range(n):
                    handover(j)
                    load(j, j, ph.slots[j])
                whole = ph.slabs // n
                if whole > 1:
                    with sp.Fori(1, whole) as i:
                        for j in range(n):
                            used(i * n + (j - n))
                            load(i * n + j, j, ph.slots[j])
                for s in range(whole * n, ph.slabs):
                    used(s - n)
                    load(s, s % n, ph.slots[s % n])

            def plain(ph, src):
                def load(s, j, at):
                    sp.dma_start(cols(at, BANK), src[:, :, bass.ds(s * BANK, BANK)]).then_inc(ph.landed[j], 16)
                return load

            def down(ph, src, k):
                def load(s, j, at):
                    sp.dma_start(rows(at, k), src[bass.ds(s, 1)].rearrange("s p k n -> p (s k) n")).then_inc(ph.landed[j], 16)
                return load

            def load_v(s, j, at):
                sp.dma_start(cols(at, GDIM), a_in[:, :, bass.ds(s * GDIM + A_HALF, GDIM)]).then_inc(av.landed[j], 16)

            def load_u(s, j, at):
                sp.dma_start(cols(at, GDIM), a_in[:, :, bass.ds(s * GDIM, GDIM)]).then_inc(au.landed[j], 16)
                sp.dma_start(slot(at)[:, KD * GDIM:(KD + 1) * GDIM],
                             t["a_v_norm_g"][0:1, bass.ds(s * GDIM, GDIM)].to_broadcast([P, GDIM])
                             ).then_inc(au.landed[j], 16)

            def load_pair(s, j, at):
                sp.dma_start(slot(at).rearrange("p (k b n) -> p k b n", k=KD, b=2)[:, :, 0, :],
                             f_in[:, :, bass.ds(s * PAIR, PAIR)]).then_inc(fu.landed[j], 16)
                sp.dma_start(slot(at).rearrange("p (k b n) -> p k b n", k=KD, b=2)[:, :, 1, :],
                             f_in[:, :, bass.ds(s * PAIR + D_FF, PAIR)]).then_inc(fu.landed[j], 16)

            free = lambda j: None
            stream(av, load_v, free)
            stream(au, load_u, free)
            stream(ao, down(ao, a_out, 4), free)
            stream(fu, load_pair, lambda j: sp.wait_ge(av.full, 2 * av.slabs))
            stream(fo, down(fo, f_out, 2), lambda j: sp.wait_ge(mixed_read, 2 * au.slabs))
            stream(kv, plain(kv, kv_w), lambda j: sp.wait_ge(down_full, 4))
            stream(qg, plain(qg, b_in), lambda j: sp.wait_ge(fu.full, 2 * fu.slabs))
            stream(bo, down(bo, b_out, 4), lambda j: sp.wait_ge(kv.full, 2 * kv.slabs))

            def fill(e, n):
                kind, s = ORDER[n // 2]
                half = n % 2
                at = e_raw(n, e_arrived)
                for b in range(2):
                    if kind == "up":
                        sp.dma_start(at.rearrange("p (k b n) -> p k b n", k=4, b=2)[:, :, b, :],
                                     m_in[bass.ds(e, 1), :, 4 * half:4 * half + 4, b, s * PAIR:(s + 1) * PAIR
                                          ].rearrange("e p k n -> p (e k) n")).then_inc(e_landed[n % RAW_E], 16)
                    else:
                        sp.dma_start(at.rearrange("p (k n) -> p k n", k=2)[:, b:b + 1, :],
                                     m_out[bass.ds(e, 1), 2 * s + half, :, b:b + 1, :].rearrange("e p k n -> p (e k) n")
                                     ).then_inc(e_landed[n % RAW_E], 16)

            for n in range(UNITS):
                if n < 4:
                    sp.wait_ge(qg.full, 2 * qg.slabs)
                elif n < RAW_E:
                    sp.wait_ge(down_full, 8)
                else:
                    e_consumed(sp, 0, n - RAW_E)
                fill(0, n)

            def expert_loop(before, count, expert):
                with sp.Fori(0, count) as i:
                    for n in range(UNITS):
                        if n < RAW_E:
                            e_consumed(sp, i + before, n - RAW_E + UNITS)
                        else:
                            e_consumed(sp, i + (before + 1), n - RAW_E)
                        fill(i + expert, n)

            expert_loop(0, E - 1, 1)
            sp.wait_ge(rounds_ready, 1)
            last = sp.value_load(rounds_i[0:1, 1:2], min_val=E - 1, max_val=2 * E - 1)
            with sp.If(last > E - 1):
                expert_loop(E - 1, E, 0)

            for n in range(LEAD):
                e_consumed(sp, last, n - RAW_E + UNITS)
                fill(0, n)

            def after_experts(j):
                if j == 0:
                    sp.wait_ge(e_lo, last * UNITS + (UNITS + LEAD))
                e_consumed(sp, last, UNITS - RAW_E + 2 * j + 1 if j < 3 else UNITS - 1)
                if j >= 3:
                    sp.wait_ge(e_lo, last * UNITS + (UNITS + LEAD))

            stream(pr, plain(pr, w_in2), lambda j: after_experts(pr.slots[j]))
            stream(po, down(po, w_out2, 4), lambda j: after_experts(3))
            stream(mu, plain(mu, w_up2), lambda j: after_experts(3))
            stream(md, down(md, w_down2, 4), lambda j: sp.wait_ge(pr.full, 2 * pr.slabs))
            for c in range(NT):
                sp.wait_ge(h_ready, 22 + 2 * c)
                sp.dma_start(out[0, c * P:(c + 1) * P, :], h[:, c, :]).then_inc(out_landed, 16)
            sp.wait_ge(out_landed, 32)

        @block.gpsimd
        def _(pool):
            steps = Steps(pool, pool_step)
            steps.then(nc.gpsimd.memset(ident[:, :], 0.0))
            nc.gpsimd.affine_select(out=ident[:, :], in_=ident[:, :], compare_op=ALU.not_equal, fill=1.0, base=0,
                                    pattern=[[-1, P]], channel_multiplier=1).then_inc(consts_ready, 1)
            steps.then(nc.gpsimd.memset(ones[:, :], 1.0))
            nc.gpsimd.affine_select(out=upto[:, :], in_=ones[:, :], compare_op=ALU.is_ge, fill=0.0, base=0,
                                    pattern=[[1, P]], channel_multiplier=-1).then_inc(consts_ready, 1)
            steps.then(nc.gpsimd.memset(causal[:, :], 0.0))
            nc.gpsimd.affine_select(out=causal[:, :], in_=causal[:, :], compare_op=ALU.is_ge, fill=MASKED, base=P,
                                    pattern=[[-1, S]], channel_multiplier=1).then_inc(consts_ready, 1)
            nc.gpsimd.iota(iota[:, :], pattern=[[1, P]], base=0, channel_multiplier=0,
                           allow_small_or_imprecise_dtypes=True).then_inc(consts_ready, 1)
            inv = (np.float32(ROPE_THETA) ** (-np.arange(0, 2 * ROPE_HALF, 2, dtype=np.float32) / np.float32(2 * ROPE_HALF)))
            for f in range(ROPE_HALF):
                ins = nc.gpsimd.memset(rope[:, 0, f:f + 1], float(inv[f]))
            ins.then_inc(consts_ready, 1)

        @block.scalar
        def _(act):
            steps = Steps(act, scalar_step)
            roots = [0]

            def take_root(w):
                roots[0] += 1
                act.wait_ge(variance_ready, roots[0])
                nc.scalar.activation(root[:, 0:w], variance[:, 0:w], ACT.Sqrt).then_inc(root_ready, 1)

            act.dma_start(h, t["x"][0].rearrange("(c p) n -> p c n", p=P)).then_inc(x_landed, 16)
            act.wait_ge(gain_rows_ready, 1)
            row = lambda name, n: gain_rows[GC[name]:GC[name] + n, :]
            n_params = 0
            for name, src in (("a", t["a_norm_g"][0]), ("f", t["f_norm_g"][0]), ("kv", t["kv_norm_g"]),
                              ("b", t["b_norm_g"][0]), ("m", t["m_norm_g"][0]), ("pre2", t["g_mix_pre_2"][0]),
                              ("mlp2", t["g_mlp_pre_2"][0])):
                act.dma_start(row(name, KD), src.rearrange("(k p) -> k p", p=P)).then_inc(params_landed, 16)
            act.dma_start(gain_rows[GC["mix"] + 4:GC["mix"] + 8, :],
                          t["g_mlstm_out_2"][0].rearrange("(k p) -> k p", p=P)).then_inc(params_landed, 16)
            act.dma_start(row("bs", GROUPS), t["a_b_spatial"][0]).then_inc(params_landed, 16)
            act.dma_start(gain_rows[GC["kq"]:GC["kq"] + 1, 0:HD], t["k_norm_g"].rearrange("(a n) -> a n", a=1)
                          ).then_inc(params_landed, 16)
            act.dma_start(gain_rows[GC["kq"] + 1:GC["kq"] + 2, 0:HD], t["q_norm_g"]).then_inc(params_landed, 16)
            act.dma_start(ws_raw, t["a_w_spatial"][0].rearrange("g i j -> i g j")).then_inc(spatial_landed, 16)
            act.dma_start(w_forget[:, :, :], kv_w[:, :, 2 * D:2 * D + HEADS]).then_inc(params_landed, 16)
            act.dma_start(w_router[:, :, :], t["m_w_router"][0].rearrange("(k p) n -> p k n", p=P)
                          ).then_inc(params_landed, 16)
            act.dma_start(w_if[:, :, :], w_in2[:, :, PROJ:PROJ + 2 * ML_H]).then_inc(params_landed, 16)
            act.dma_start(b_forget[:, :], t["kv_b_f"].rearrange("(a n) -> a n", a=1).to_broadcast([P, HEADS])
                          ).then_inc(params_landed, 16)
            act.dma_start(b_if[:, 0:ML_H], t["b_igate_2"].to_broadcast([P, ML_H])).then_inc(params_landed, 16)
            act.dma_start(b_if[:, ML_H:2 * ML_H], t["b_fgate_2"].to_broadcast([P, ML_H])).then_inc(params_landed, 16)
            act.dma_start(pos_i[:, :], t["positions_2"][0].rearrange("(c p) -> p c", p=P),
                          allow_slow_non_contiguous=True).then_inc(params_landed, 16)

            def squares():
                for c in range(NT):
                    nc.scalar.activation(xn[:, c, :], h[:, c, :], ACT.Square, accum_out=ss[:, c:c + 1]).then_inc(squares_ready, 1)

            def odd_turn(tf, tc, g, copy):
                act.wait_ge(tf, g + 1)
                copy(T[1]).then_inc(tc[1], 1)

            def norm_copies(tf, tc, base, outs):
                for j in (1, 3):
                    def copy(bank, j=j):
                        for dst, gc in outs:
                            for k in (2 * j, 2 * j + 1):
                                src = bank[:, (k % 2) * S:(k % 2 + 1) * S]
                                if gc is None:
                                    ins = nc.scalar.copy(dst[:, k, :], src)
                                else:
                                    ins = nc.scalar.mul(dst[:, k, :], src, gains[:, gc + k:gc + k + 1])
                        return ins
                    odd_turn(tf, tc, base + j, copy)

            act.wait_ge(x_landed, 16)
            squares()
            take_root(NT)
            base = 2
            act.wait_ge(turned, 2)
            nc.scalar.copy(wsT[:, 0:BANK], T[1][:, :])
            nc.scalar.copy(wsT[:, BANK:2 * BANK], G[3][:, :]).then_inc(turned_copied[1], 1)
            act.wait_ge(turned_copied[0], 1)
            norm_copies(turned, turned_copied, base, [(xT, GC["a"])])
            base += 4

            def gelu_v(i, j, c):
                n = i * 4 + 2 * j + c
                act.wait_ge(av.full, n + 1)
                nc.scalar.activation(work[:, c, bass.ds(i * (2 * GDIM) + j * GDIM, GDIM)], G[2 * j + c][:, 0:GDIM],
                                     ACT.Gelu).then_inc(av.done, 1)

            with act.Fori(0, av.slabs // 2) as i:
                for j in range(2):
                    for c in range(NT):
                        gelu_v(i, j, c)
            take_root(NT)
            for n in range(2 * au.slabs + 1):
                s, c = n // 2, n % 2
                if n < 2 * au.slabs:
                    act.wait_ge(au.full, n + 1)
                    if n >= 2:
                        act.wait_ge(gated_ready, n - 1)
                    nc.scalar.activation(xn[:, c, 0:GDIM], G[n % 4][:, 0:GDIM], ACT.Gelu).then_inc(au.done, 1)
                m = n - 1
                if m >= 0 and m % 2 == 1:
                    odd_turn(turned, turned_copied, base + m, lambda bank: nc.scalar.copy(
                        hT[:, GCH * (m // 2):GCH * (m // 2 + 1), P:2 * P],
                        bank[:, 0:GDIM].rearrange("p (k s) -> p k s", k=GCH)))
            base += 2 * au.slabs

            def norm(ready, outs, tf, tc, base):
                for c in range(NT):
                    act.wait_ge(h_ready, ready + 2 * c + 2)
                    nc.scalar.activation(xn[:, c, :], h[:, c, :], ACT.Square, accum_out=ss[:, c:c + 1]).then_inc(squares_ready, 1)
                take_root(NT)
                norm_copies(tf, tc, base, outs)

            norm(0, [(xT, GC["f"])], turned, turned_copied, base)
            base += 4

            def silu(n, j, c, first):
                act.wait_ge(fu.full, n + 1)
                if not first:
                    act.wait_ge(fu.done, n - 1)
                nc.scalar.activation(xn[:, c, 0:PAIR], G[2 * j + c][:, 0:PAIR], ACT.Silu).then_inc(silu_ready, 1)

            def hidden_odd(m, s):
                odd_turn(turned, turned_copied, m + base, lambda bank: nc.scalar.copy(
                    hT[:, bass.ds(s * 2, 2), P:2 * P], bank[:, 0:2 * P].rearrange("p (k s) -> p k s", k=2)))

            def ffn_body(i, first):
                for j in range(2):
                    for c in range(NT):
                        silu(i * 4 + (2 * j + c), j, c, first and j == 0)
                        if c == 0 and not (first and j == 0):
                            hidden_odd(i * 4 + (2 * j - 1), i * 2 + (j - 1))

            ffn_body(0, True)
            with act.Fori(1, fu.slabs // 2) as i:
                ffn_body(i, False)
            last = 2 * (fu.slabs - 1)
            silu(last, 0, 0, False)
            hidden_odd(last - 1, fu.slabs - 2)
            silu(last + 1, 0, 1, False)
            hidden_odd(last + 1, fu.slabs - 1)
            base += 2 * fu.slabs

            norm(4, [(xT, GC["kv"]), (xT2, GC["b"])], turned, turned_copied, base)
            base += 4
            for ph in (kv, qg):
                for n in range(2 * ph.slabs):
                    s, c = n // 2, n % 2
                    act.wait_ge(ph.full, n + 1)
                    if s < 2:
                        at = KA if ph is kv else QA
                        dst = work[:, c, at + 8 * s * AUG:at + 8 * (s + 1) * AUG].rearrange("p (h e) -> p h e", e=AUG)[:, :, 0:HD]
                        nc.scalar.copy(dst, G[n % 4][:, :].rearrange("p (h e) -> p h e", e=HD)).then_inc(ph.done, 1)
                    elif ph is kv:
                        nc.scalar.copy(work[:, c, VA + (s - 2) * BANK:VA + (s - 1) * BANK], G[n % 4][:, :]).then_inc(ph.done, 1)
                    else:
                        nc.scalar.activation(work[:, c, GA + (s - 2) * BANK:GA + (s - 1) * BANK], G[n % 4][:, :],
                                             ACT.Sigmoid).then_inc(ph.done, 1)
                if ph is kv:
                    softplus(act, steps, xn[:, 1, 512:512 + 32], xn[:, 1, 544:544 + 32], z_ready, ez_ready, ez1_ready, ln_ready, 1)
            take_root(2 * 2 * HEADS)
            for g in range(16):
                if g % 2:
                    odd_turn(turned, turned_copied, base + g, lambda bank: nc.scalar.mul(
                        hT[0:AUG, 2 * g:2 * g + 2, :], bank[0:AUG, :].rearrange("p (h s) -> p h s", h=2),
                        gains[0:AUG, GC["kq"] + g // 8:GC["kq"] + g // 8 + 1]))
            base += 16

            def attention(att, units, tf, tc, base):
                for u in range(units + 2):
                    if u < units:
                        nk = P * (u % 2 + 1)
                        act.wait_ge(att.max_ready, u + 1)
                        if u >= 4:
                            act.wait_ge(tf, base + u - 3)
                        nc.scalar.activation(xn_all[:, (u % 4) * S:(u % 4) * S + nk], G[u % 4][:, 0:nk], ACT.Exp,
                                             bias=nmax[:, u:u + 1], accum_out=rowsum[:, u:u + 1]).then_inc(att.p_ready, 1)
                    w = u - 2
                    if w >= 0 and w % 2:
                        if w >= 4:
                            act.wait_ge(att.out_full, w - 3)
                        odd_turn(tf, tc, base + w, lambda bank: nc.scalar.copy(
                            xT_all[:, (w % 4) * S:(w % 4 + 1) * S], bank[:, 0:S]))

            attention(att1, 2 * HEADS, turned, turned_copied, base)
            base += 2 * HEADS
            norm_copies(turned, turned_copied, base, [(xT, None)])
            base += 4

            norm(8, [(xT, GC["m"])], turned, turned_copied, base)
            base += 4
            act.wait_ge(gap_diff, 2)
            nc.scalar.activation(gap, gap, ACT.Exp).then_inc(gap_exp, 1)

            def gather_copy(it):
                for half in range(2):
                    act.wait_ge(gather_full, it * 2 + (half + 1))
                    for k in range(4 * half, 4 * half + 4):
                        ins = nc.scalar.mul(xg_hi[:, k * P:(k + 1) * P], G[2 + half][:, (k % 4) * P:(k % 4 + 1) * P],
                                            gains[:, GC["m"] + k:GC["m"] + k + 1])
                ins.then_inc(gathered[0], 1)

            def e_turn(it, what):
                g = TURN_OF[what]
                act.wait_ge(e_turned, it * len(TURNS) + g + 1)
                if what == "route":
                    ins = nc.scalar.copy(routeT, T[1][:, 0:2 * P])
                else:
                    expert_hidden_free(act, it, what)
                    ins = nc.scalar.copy(e_hT_hi[:, what % 2, :], T[g % 2][:, :])
                ins.then_inc(e_turned_hi, 1)

            for n in range(LEAD):
                e_make_hi(act, 0, n)
            gather_copy(0)
            act.wait_ge(rounds_ready, 1)
            rounds = act.value_load(rounds_i[0:1, 0:1], min_val=1, max_val=2)
            with act.Fori(0, rounds * E) as it:
                for m, (kind, s) in enumerate(ORDER):
                    if m == len(ORDER) - 1:
                        gather_copy(it + 1)
                        e_turn(it, DOWNS - 1)
                    for n in (2 * m + LEAD, 2 * m + LEAD + 1):
                        e_make_hi(act, it, n)
                    if kind == "up":
                        act.wait_ge(up_full, it * UPS + s + 1)
                        act.wait_ge(up_read, it * UPS + s + 1)
                        nc.scalar.activation(e_silu[:, s % 2, :], G[s % 2][:, 0:PAIR], ACT.Silu).then_inc(e_silu_ready, 1)
                        if s == 4:
                            e_turn(it, "route")
                        if s % 2 == 0 and s >= 2:
                            e_turn(it, s // 2 - 1)
                act.wait_ge(y_full, it * 2 + 1)
                act.wait_ge(scatter_full, it * 4)
                nc.scalar.copy(y_sb[:, 0:BANK], SM[0][:, :]).then_inc(y_copied[0], 1)

            base = 0
            norm(12, [(xT, GC["pre2"])], turned2, turned2_copied, base)
            act.dma_start(post_gain1, t["g_mix_post_2"].to_broadcast([P, D])).then_inc(post_landed, 16)
            base += 4

            def project(i):
                for j in range(2):
                    for c in range(NT):
                        act.wait_ge(pr.full, i * 4 + (2 * j + c + 1))
                        nc.scalar.copy(work[:, c, bass.ds(i * (2 * BANK) + j * BANK, BANK)], G[2 * j + c][:, :]
                                       ).then_inc(pr.done, 1)

            with act.Fori(0, pr.slabs // 2) as i:
                project(i)
            softplus(act, steps, xn[:, 1, 512:512 + 8], xn[:, 1, 544:544 + 8], z_ready, ez_ready, ez1_ready, ln_ready, 2)
            act.wait_ge(angle_ready, 1)
            nc.scalar.activation(rope[:, 5:7, :], rope[:, 3:5, :], ACT.Sin).then_inc(sines_ready, 1)
            act.wait_ge(pr.done, 2 * pr.slabs)
            for c in range(NT):
                ins = nc.scalar.activation(work[:, c, MO:MO + ML_H * ML_V], work[:, c, MO:MO + ML_H * ML_V], ACT.Sigmoid)
            ins.then_inc(out_gate_ready, 1)
            for g in range(16):
                if g % 2:
                    odd_turn(turned2, turned2_copied, base + g, lambda bank: second_head_copy(nc.scalar.copy, nc.scalar.mul, g, bank))
            base += 16
            attention(att2, 2 * ATT_H, turned2, turned2_copied, base)
            base += 2 * ATT_H
            for u in range(2 * ML_H + 2):
                if u < 2 * ML_H:
                    nk = P * (u % 2 + 1)
                    act.wait_ge(mls.max_ready, u + 1)
                    if u >= 4:
                        act.wait_ge(turned2, base + u - 3)
                    nc.scalar.activation(xn_all[:, (u % 4) * S:(u % 4) * S + nk], G[u % 4][:, 0:nk], ACT.Exp,
                                         bias=nmax[:, u:u + 1])
                    nc.scalar.activation(expm[:, u:u + 1], nmax[:, u:u + 1], ACT.Exp).then_inc(mls.p_ready, 1)
                w = u - 2
                if w >= 0 and w % 2:
                    if w >= 4:
                        act.wait_ge(mls.out_full, w - 3)
                    odd_turn(turned2, turned2_copied, base + w, lambda bank: nc.scalar.copy(
                        xT_all[:, (w % 4) * S:(w % 4 + 1) * S], bank[:, 0:S]))
            base += 2 * ML_H
            take_root(2 * ML_H)
            norm_copies(turned2, turned2_copied, base, [(xT, GC["mix"])])
            base += 4

            def post_norm_squares(full):
                for b in range(4):
                    act.wait_ge(down_full, full + b + 1)
                    nc.scalar.activation(xn[:, b // 2, (b % 2) * BANK:(b % 2 + 1) * BANK], G[b][:, :], ACT.Square,
                                         accum_out=ss4[:, b:b + 1]).then_inc(post_squares, 1)

            post_norm_squares(12)
            take_root(NT)
            act.dma_start(post_gain2, t["g_mlp_post_2"].to_broadcast([P, D])).then_inc(post_landed, 16)

            norm(16, [(xT, GC["mlp2"])], turned2, turned2_copied, base)
            base += 4

            def relu(n, j, c, first):
                act.wait_ge(mu.full, n + 1)
                if not first:
                    act.wait_ge(relu2_ready, n - 1)
                nc.scalar.activation(xn[:, c, 0:BANK], G[2 * j + c][:, :], ACT.Relu).then_inc(mu.done, 1)

            def squared_odd(m, s):
                odd_turn(turned2, turned2_copied, m + base, lambda bank: nc.scalar.copy(
                    hT[:, bass.ds(s * 4, 4), P:2 * P], bank[:, :].rearrange("p (k s) -> p k s", k=4)))

            def mlp_body(i, first):
                for j in range(2):
                    for c in range(NT):
                        relu(i * 4 + (2 * j + c), j, c, first and j == 0)
                        if c == 0 and not (first and j == 0):
                            squared_odd(i * 4 + (2 * j - 1), i * 2 + (j - 1))

            mlp_body(0, True)
            with act.Fori(1, mu.slabs // 2) as i:
                mlp_body(i, False)
            squared_odd(2 * mu.slabs - 1, mu.slabs - 1)
            post_norm_squares(16)
            take_root(NT)

        @block.tensor
        def _(pe):
            def turn(tf, tc, g, blocks):
                if not isinstance(g, int) or g >= 2:
                    pe.wait_ge(tc[par(g)], half(g))
                at = 0
                for src in blocks:
                    k = src.shape[-1]
                    ins = nc.tensor.transpose(T[par(g)][0:k, at:at + P], src, ident[:, :])
                    at += P
                ins.then_inc(tf, 1)

            def par(g):
                return g % 2 if isinstance(g, int) else g.par

            def half(g):
                return g // 2 if isinstance(g, int) else g.half

            class G_:

                def __init__(self, half, par):
                    self.half, self.par = half, par

            def copied(tc, groups):
                pe.wait_ge(tc[0], (groups + 1) // 2)
                pe.wait_ge(tc[1], groups // 2)

            def norm_turns(tf, tc, base, src):
                for j in range(4):
                    turn(tf, tc, base + j, [src[:, c, k * P:(k + 1) * P] for k in (2 * j, 2 * j + 1) for c in range(NT)])

            def chunks(bank, x, c, w, n):
                for k in range(KD):
                    ins = nc.tensor.matmul(bank[:, 0:n], x[:, k, c * P:(c + 1) * P], w[:, k, :], start=(k == 0), stop=(k == KD - 1))
                return ins

            def use(ph, i, j, c, first, x, n):
                if not first:
                    pe.wait_ge(ph.done, i * 4 + (2 * j + c - 3))
                if c == 0:
                    pe.wait_ge(ph.landed[j], i * (16 * ph.dmas) + 16 * ph.dmas)
                chunks(G[2 * j + c], x, c, cols(ph.slots[j], n), n).then_inc(ph.full, 1)

            def down(ph, lhs, k_per, ready):
                n_k = ph.slabs * k_per
                for s in range(ph.slabs):
                    pe.wait_ge(ph.landed[s % 2], 16 * (s // 2 + 1))
                    w = rows(ph.slots[s % 2], k_per)
                    for kk in range(k_per):
                        k = s * k_per + kk
                        ready(k)
                        for c in range(NT):
                            for b in range(2):
                                ins = nc.tensor.matmul(G[2 * c + b][:, :], lhs(k, c), w[:, kk, b * BANK:(b + 1) * BANK],
                                                       start=(k == 0), stop=(k == n_k - 1))
                                if k == n_k - 1:
                                    ins.then_inc(down_full, 1)
                    if s < ph.slabs - 1:
                        ins.then_inc(ph.used, 1)

            hidden = lambda k, c: hT[:, k, c * P:(c + 1) * P]
            from_xT = lambda k, c: xT[:, k, c * P:(c + 1) * P]
            tf, tc = turned, turned_copied

            pe.wait_ge(consts_ready, 5)
            pe.wait_ge(params_landed, 16 * 18)
            nc.tensor.transpose(T[0][:, 0:74], gain_rows[:, :], ident[0:74, 0:74]).then_inc(turned, 1)
            pe.wait_ge(spatial_ready, 1)
            for g in range(GROUPS):
                bank = T[1] if g < 4 else G[3]
                ins = nc.tensor.transpose(bank[:, (g % 4) * P:(g % 4 + 1) * P], ws_raw[:, g, :], ident[:, :])
            ins.then_inc(turned, 1)
            pe.wait_ge(xn_ready, 2)
            base = 2
            norm_turns(tf, tc, base, xn)
            base += 4
            copied(tc, base)
            for j in range(2):
                for c in range(NT):
                    use(av, 0, j, c, True, xT, GDIM)
            with pe.Fori(1, av.slabs // 2) as i:
                for j in range(2):
                    for c in range(NT):
                        use(av, i, j, c, False, xT, GDIM)
            pe.wait_ge(av.done, 2 * av.slabs)
            for n in range(2 * au.slabs + 1):
                s, c = n // 2, n % 2
                if n < 2 * au.slabs:
                    use(au, s // 2, s % 2, c, n < 4, xT, GDIM)
                    if n == 0:
                        pe.wait_ge(spatial_ready, 2)
                    if n >= 2:
                        pe.wait_ge(mixed_read, n - 1)
                    nc.tensor.matmul(SM[c][:, 0:GDIM], work[:, c, A_HALF + s * P:A_HALF + (s + 1) * P],
                                     work[:, c, s * GDIM:(s + 1) * GDIM], start=True, stop=True).then_inc(mixed_full, 1)
                m = n - 1
                if m >= 0:
                    pe.wait_ge(gated_ready, m + 1)
                    turn(tf, tc, base + m, [xn[:, m % 2, GDIM + k * P:GDIM + (k + 1) * P] for k in range(GCH)])
            pe.wait_ge(au.done, 2 * au.slabs)

            def chunk_ready(base, per, tc):
                def ready(k):
                    if k % per == 0:
                        for c in range(NT):
                            pe.wait_ge(tc[c], base // 2 + k // per + 1)
                return ready

            down(ao, hidden, 4, chunk_ready(base, GCH, tc))
            base += 2 * au.slabs

            pe.wait_ge(xn_ready, 4)
            norm_turns(tf, tc, base, xn)
            base += 4
            copied(tc, base)
            pe.wait_ge(h_ready, 4)

            def hidden_turn(m, g):
                pe.wait_ge(fu.done, m + 1)
                turn(tf, tc, g, [xn[:, par(g), PAIR + k * P:PAIR + (k + 1) * P] for k in range(2)])

            def ffn_use(i, j, c, first):
                if not first:
                    pe.wait_ge(fu.done, i * 4 + (2 * j + c - 3))
                if c == 0:
                    pe.wait_ge(fu.landed[j], i * 32 + 32)
                chunks(G[2 * j + c], xT, c, cols(fu.slots[j], BANK), BANK).then_inc(fu.full, 1)

            def ffn_body(i, first, base):
                for j in range(2):
                    for c in range(NT):
                        ffn_use(i, j, c, first)
                        n = 2 * j + c
                        if not (first and n == 0):
                            g = G_(i * 2 + ((n - 1) // 2 + base // 2), (n - 1) % 2)
                            hidden_turn(i * 4 + (n - 1), g)

            ffn_body(0, True, base)
            with pe.Fori(1, fu.slabs // 2) as i:
                ffn_body(i, False, base)
            for c in range(NT):
                n = 2 * (fu.slabs - 1) + c
                ffn_use(fu.slabs // 2, 0, c, False)
                hidden_turn(n - 1, base + n - 1)
            hidden_turn(n, base + n)
            pe.wait_ge(fu.done, 2 * fu.slabs)
            down(fo, hidden, 2, chunk_ready(base, 2, tc))
            base += 2 * fu.slabs

            pe.wait_ge(xn_ready, 6)
            norm_turns(tf, tc, base, xn)
            base += 4
            copied(tc, base)
            pe.wait_ge(h_ready, 8)
            for ph, x in ((kv, xT), (qg, xT2)):
                if ph is qg:
                    pe.wait_ge(kv.done, 2 * kv.slabs)
                for s in range(ph.slabs):
                    for c in range(NT):
                        use(ph, s // 2, s % 2, c, s < 2, x, BANK)
                if ph is kv:
                    for c in range(NT):
                        ins = chunks(SM[0][:, c * HEADS:(c + 1) * HEADS], xT, c, w_forget, HEADS)
                    ins.then_inc(small_full, 1)
            pe.wait_ge(logf_ready, 1)
            running_sums(pe, xn[:, 1, 576:576 + 32].rearrange("p (c n) -> p c n", c=NT), HEADS).then_inc(small_full, 1)
            pe.wait_ge(aug_ready, 1)
            for g in range(16):
                at = (KA if g < 8 else QA) + 2 * (g % 8) * AUG
                turn(tf, tc, base + g, [work[:, c, at + e * AUG:at + (e + 1) * AUG] for e in range(2) for c in range(NT)])
            base += 16
            copied(tc, base)
            pe.wait_ge(qg.done, 2 * qg.slabs)

            def attention(att, units, qT, kT, v, width, tf, tc, base, extra=None):
                for u in range(units + 3):
                    if u < units:
                        hd, q = u // 2, u % 2
                        nk = P * (q + 1)
                        if u >= 4:
                            pe.wait_ge(att.p_ready if extra is None else weights_ready, u - 3)
                        if extra is None:
                            nc.tensor.matmul(G[u % 4][:, 0:nk], qT(hd)[:, q * P:(q + 1) * P], kT(hd)[:, 0:nk],
                                             start=True, stop=True).then_inc(att.full, 1)
                        else:
                            extra(u, hd, q, nk).then_inc(att.full, 1)
                    w = u - 2
                    if 0 <= w < units:
                        pe.wait_ge(att.p_ready if extra is None else weights_ready, w + 1)
                        turn(tf, tc, base + w, [xn_all[:, (w % 4) * S + k * P:(w % 4) * S + (k + 1) * P]
                                                for k in range(w % 2 + 1)])
                    w = u - 3
                    if 0 <= w < units:
                        g = base + w
                        pe.wait_ge(tc[g % 2], g // 2 + 1)
                        if w >= 2:
                            pe.wait_ge(att.out_done, w - 1)
                        for k in range(w % 2 + 1):
                            ins = nc.tensor.matmul(SM[w % 2][:, 0:width], xT_all[:, (w % 4) * S + k * P:(w % 4) * S + (k + 1) * P],
                                                   v(w // 2, k), start=(k == 0), stop=(k == w % 2))
                        ins.then_inc(att.out_full, 1)

            attention(att1, 2 * HEADS, lambda hd: hT[0:AUG, HEADS + hd, :], lambda hd: hT[0:AUG, hd, :],
                      lambda hd, k: work[:, k, VA + hd * HD:VA + (hd + 1) * HD], HD, tf, tc, base)
            base += 2 * HEADS
            pe.wait_ge(att1.out_done, 2 * HEADS)
            norm_turns(tf, tc, base, work[:, :, GA:GA + D])
            base += 4
            copied(tc, base)
            down(bo, from_xT, 4, lambda k: None)

            pe.wait_ge(xn_ready, 8)
            norm_turns(tf, tc, base, xn)
            base += 4
            copied(tc, base)
            for c in range(NT):
                ins = chunks(SM[0][:, c * E:(c + 1) * E], xT, c, w_router, E)
            ins.then_inc(small_full, 1)
            pe.wait_ge(mask_ready, 1)
            running_sums(pe, sel, E)
            nc.tensor.matmul(SM[1][:, 2 * E:3 * E], ones[:, :], sel[:, 0, :], start=True, stop=False)
            nc.tensor.matmul(SM[1][:, 2 * E:3 * E], ones[:, :], sel[:, 1, :], start=False, stop=True).then_inc(small_full, 1)

            def gather(it):
                pe.wait_ge(pick_ready, it + 1)
                for k in range(KD):
                    for c in range(NT):
                        ins = nc.tensor.matmul(G[2 + k // 4][:, (k % 4) * P:(k % 4 + 1) * P], xn[:, c, k * P:(k + 1) * P],
                                               pick[:, c, :], start=(c == 0), stop=(c == NT - 1))
                    if k % 4 == 3:
                        ins.then_inc(gather_full, 1)

            def scatter(added, added_before, full):
                for c in range(NT):
                    for b in range(2):
                        if c:
                            pe.wait_ge(added, added_before + b + 1)
                        ins = nc.tensor.matmul(G[2 + b][:, :], routeT[:, c * P:(c + 1) * P], y_sb[:, b * BANK:(b + 1) * BANK],
                                               start=True, stop=True)
                        ins.then_inc(full, 1)

            def e_turn(it, what):
                g = TURN_OF[what]
                if what == "route":
                    pe.wait_ge(route_ready, it + 1)
                    blocks = [route[:, c, :] for c in range(NT)]
                else:
                    pe.wait_ge(up_read, it * UPS + 2 * what + 4)
                    blocks = [e_hid[:, b, k * P:(k + 1) * P] for b in range(2) for k in range(2)]
                if g == 3:
                    pe.wait_ge(e_turned_hi, it * len(TURNS) + 2)
                else:
                    pe.wait_ge(e_turned_lo, it * DOWNS + (0 if g < 2 else 1 if g == 2 else g - 2))
                for n, src in enumerate(blocks):
                    ins = nc.tensor.transpose(T[g % 2][:, n * P:(n + 1) * P], src, ident[:, :])
                ins.then_inc(e_turned, 1)

            def three_products(bank, x_hi, x_lo, w_hi, w_lo, start, stop):
                nc.tensor.matmul(bank, x_hi, w_hi, start=start, stop=False)
                nc.tensor.matmul(bank, x_hi, w_lo, start=False, stop=False)
                return nc.tensor.matmul(bank, x_lo, w_hi, start=False, stop=stop)

            gather(0)
            pe.wait_ge(rounds_ready, 1)
            rounds = pe.value_load(rounds_i[0:1, 0:1], min_val=1, max_val=2)
            with pe.Fori(0, rounds * E) as it:
                for q in range(2):
                    pe.wait_ge(gathered[q], it + 1)
                for m, (kind, s) in enumerate(ORDER):
                    if kind == "up":
                        pe.wait_ge(up_read, it * UPS + s + 1)
                        for part in range(2):
                            n = 2 * m + part
                            pe.wait_ge(e_lo, it * UNITS + (n + 1))
                            for kk in range(4):
                                k = 4 * part + kk
                                at = slice(kk * BANK, (kk + 1) * BANK)
                                ins = three_products(G[s % 2][:, :], xg_hi[:, k * P:(k + 1) * P], xg_lo[:, k * P:(k + 1) * P],
                                                     e_hi_unit(n)[:, at], e_raw(n, e_low)[:, at], k == 0, k == KD - 1)
                            ins.then_inc(up_full if part else up_half_used, 1)
                        if s == 1:
                            for b in range(2):
                                pe.wait_ge(y_copied[b], it + 1)
                            scatter(scatter_added, it * 4, scatter_full)
                        if s == 4:
                            e_turn(it, "route")
                        if s % 2 == 0 and s >= 2:
                            e_turn(it, s // 2 - 1)
                    else:
                        if s == DOWNS - 1:
                            pe.wait_ge(scatter_added, it * 4 + 4)
                            gather(it + 1)
                            e_turn(it, DOWNS - 1)
                            pe.wait_ge(e_turned_hi, it * len(TURNS) + (TURN_OF["route"] + 1))
                        pe.wait_ge(e_turned_lo, it * DOWNS + (s + 1))
                        for part in range(2):
                            n = 2 * m + part
                            final = s == DOWNS - 1 and part == 1
                            pe.wait_ge(e_lo, it * UNITS + (n + 1))
                            for kk in range(2):
                                k = 2 * part + kk
                                for b in range(2):
                                    at = slice(kk * D + b * BANK, kk * D + (b + 1) * BANK)
                                    ins = three_products(SM[b][:, :], e_hT_hi[:, s % 2, k * P:(k + 1) * P],
                                                         e_hT_lo[:, s % 2, k * P:(k + 1) * P], e_hi_unit(n)[:, at],
                                                         e_raw(n, e_low)[:, at], s == 0 and k == 0, final and kk == 1)
                                    if final and kk == 1:
                                        ins.then_inc(y_full, 1)
                            if not final:
                                ins.then_inc(down_used, 1)
            for b in range(2):
                pe.wait_ge(y_copied[b], rounds * E + 1)
                pe.wait_ge(gathered[b], rounds * E + 1)
            scatter(h_ready, 12, last_scatter)

            tf, tc = turned2, turned2_copied
            base = 0
            pe.wait_ge(e_turned_lo, rounds * (E * DOWNS))
            pe.wait_ge(xn_ready, 10)
            norm_turns(tf, tc, base, xn)
            base += 4
            copied(tc, base)
            for j in range(2):
                for c in range(NT):
                    use(pr, 0, j, c, True, xT, BANK)
            with pe.Fori(1, pr.slabs // 2) as i:
                for j in range(2):
                    for c in range(NT):
                        use(pr, i, j, c, False, xT, BANK)
            for c in range(NT):
                ins = chunks(SM[0][:, c * 2 * ML_H:(c + 1) * 2 * ML_H], xT, c, w_if, 2 * ML_H)
            ins.then_inc(small_full, 1)
            pe.wait_ge(logf_ready, 2)
            running_sums(pe, xn[:, 1, 576:576 + 8].rearrange("p (c n) -> p c n", c=NT), ML_H).then_inc(small_full, 1)
            pe.wait_ge(aug_ready, 2)
            pe.wait_ge(pr.done, 2 * pr.slabs)
            for g in range(16):
                if g < 12:
                    at = g * 2 * HD if g < 8 else MQ + (g - 8) * 2 * HD
                    blocks = [work[:, c, at + e * HD:at + (e + 1) * HD] for e in range(2) for c in range(NT)]
                else:
                    at = 640 + 2 * (2 * (g - 12))
                    blocks = [xn[:, 1, at + 2 * e + 16 * c:at + 2 * e + 16 * c + 2] for e in range(2) for c in range(NT)]
                turn(tf, tc, base + g, blocks)
            base += 16
            copied(tc, base)
            attention(att2, 2 * ATT_H, lambda hd: hT[0:HD, hd, :], lambda hd: hT[0:HD, ATT_H + hd, :],
                      lambda hd, k: work[:, k, V2 + hd * HD:V2 + (hd + 1) * HD], HD, tf, tc, base)
            base += 2 * ATT_H
            pe.wait_ge(att2.out_done, 2 * ATT_H)

            def mlstm_scores(u, hd, q, nk):
                nc.tensor.matmul(G[u % 4][:, 0:nk], hT[0:2, 24 + hd, q * P:(q + 1) * P], hT[0:2, 28 + hd, 0:nk],
                                 start=True, stop=True)
                return nc.tensor.matmul(G[u % 4][:, S:S + nk], hT[0:HD, 16 + hd, q * P:(q + 1) * P],
                                        hT[0:HD, 20 + hd, 0:nk], start=True, stop=True)

            attention(mls, 2 * ML_H, None, None, lambda hd, k: work[:, k, MV + hd * ML_V:MV + (hd + 1) * ML_V],
                      ML_V, tf, tc, base, extra=mlstm_scores)
            base += 2 * ML_H
            pe.wait_ge(hm_ready, 2 * ML_H)
            norm_turns(tf, tc, base, work[:, :, 0:D])
            base += 4
            copied(tc, base)
            down(po, from_xT, 4, lambda k: None)

            pe.wait_ge(xn_ready, 12)
            norm_turns(tf, tc, base, xn)
            base += 4
            copied(tc, base)
            pe.wait_ge(h_ready, 20)

            def squared_turn(m, g):
                pe.wait_ge(relu2_ready, m + 1)
                turn(tf, tc, g, [xn[:, par(g), BANK + k * P:BANK + (k + 1) * P] for k in range(4)])

            def mlp_body(i, first, base):
                for j in range(2):
                    for c in range(NT):
                        use(mu, i, j, c, first, xT, BANK)
                        n = 2 * j + c
                        if not (first and n == 0):
                            squared_turn(i * 4 + (n - 1), G_(i * 2 + ((n - 1) // 2 + base // 2), (n - 1) % 2))

            mlp_body(0, True, base)
            with pe.Fori(1, mu.slabs // 2) as i:
                mlp_body(i, False, base)
            squared_turn(2 * mu.slabs - 1, base + 2 * mu.slabs - 1)
            pe.wait_ge(mu.done, 2 * mu.slabs)
            down(md, hidden, 4, chunk_ready(base, 4, tc))

        @block.vector
        def _(dve):
            V = nc.vector
            steps = Steps(dve, vector_step)
            roots = [0]
            tf, tc = turned, turned_copied

            def even_turn(tf, tc, g, copy):
                dve.wait_ge(tf, g + 1)
                copy(T[0]).then_inc(tc[0], 1)

            def norm_copies(tf, tc, base, outs):
                for j in (0, 2):
                    def copy(bank, j=j):
                        for dst, gc in outs:
                            for k in (2 * j, 2 * j + 1):
                                src = bank[:, (k % 2) * S:(k % 2 + 1) * S]
                                if gc is None:
                                    ins = V.tensor_copy(dst[:, k, :], src)
                                else:
                                    ins = V.tensor_scalar(dst[:, k, :], src, gains[:, gc + k:gc + k + 1], None, ALU.mult)
                        return ins
                    even_turn(tf, tc, base + j, copy)

            def inverse_rms(dst, src, n):
                w = src.shape[-1]
                roots[0] += 1
                V.tensor_scalar(variance[:, 0:w], src, 1.0 / n, EPS, ALU.mult, ALU.add).then_inc(variance_ready, 1)
                dve.wait_ge(root_ready, roots[0])
                steps.then(V.reciprocal(dst, root[:, 0:w]))
                c = correction[:, 0:w]
                steps.then(V.tensor_tensor(c, dst, dst, ALU.mult))
                steps.then(V.tensor_tensor(c, c, variance[:, 0:w], ALU.mult))
                steps.then(V.tensor_scalar(c, c, -0.5, 1.5, ALU.mult, ALU.add))
                steps.then(V.tensor_tensor(dst, dst, c, ALU.mult))

            def norm(nth, tf, tc, base, outs):
                dve.wait_ge(squares_ready, 2 * nth)
                inverse_rms(rstd, ss, D)
                for c in range(NT):
                    V.tensor_scalar(xn[:, c, :], h[:, c, :], rstd[:, c:c + 1], None, ALU.mult).then_inc(xn_ready, 1)
                norm_copies(tf, tc, base, outs)

            def add_down(full):
                for b in range(4):
                    dve.wait_ge(down_full, full + b + 1)
                    dst = h[:, b // 2, (b % 2) * BANK:(b % 2 + 1) * BANK]
                    V.tensor_tensor(dst, dst, G[b][:, :], ALU.add).then_inc(h_ready, 1)

            V.memset(gain_rows[:, :], 1.0).then_inc(gain_rows_ready, 1)
            dve.wait_ge(spatial_landed, 16)
            V.memset(ws_raw[0:64, :, 64:128], 0.0).then_inc(spatial_ready, 1)
            dve.wait_ge(turned, 1)
            steps.then(V.tensor_copy(gains[:, :], T[0][:, 0:74]))
            V.tensor_scalar(gains[0:HD, GC["kq"] + 1:GC["kq"] + 2], gains[0:HD, GC["kq"] + 1:GC["kq"] + 2], HD ** -0.5, None,
                            ALU.mult).then_inc(tc[0], 1)
            base = 2
            dve.wait_ge(tc[0], 1)
            norm(1, tf, tc, base, [(xT, GC["a"])])
            base += 4

            for n in range(2 * av.slabs):
                s, c = n // 2, n % 2
                dve.wait_ge(av.done, n + 1)
                if n >= 2:
                    dve.wait_ge(v_squared, n - 1)
                v = work[:, c, s * GDIM:(s + 1) * GDIM]
                V.tensor_tensor_reduce(out=xn[:, c, GDIM:2 * GDIM], in0=v, in1=v, scale=1.0, scalar=0.0, op0=ALU.mult,
                                       op1=ALU.add, accum_out=vss[:, c * GROUPS + s:c * GROUPS + s + 1]).then_inc(v_squared, 1)
            dve.wait_ge(v_squared, 2 * av.slabs)
            dve.wait_ge(tc[1], 1)
            for c in range(NT):
                steps.then(V.tensor_reduce(ss[:, c:c + 1], vss[:, c * GROUPS:(c + 1) * GROUPS], AX_X, ALU.add))
            inverse_rms(rstd, ss, A_HALF)
            for c in range(NT):
                ins = V.tensor_scalar(work[:, c, A_HALF:A_HALF + GROUPS * P], wsT, rstd[:, c:c + 1], None, ALU.mult)
            ins.then_inc(spatial_ready, 1)
            for n in range(2 * au.slabs + 1):
                s, c = n // 2, n % 2
                m = n - 1
                if m >= 0 and m % 2 == 0:
                    even_turn(tf, tc, base + m, lambda bank: V.tensor_copy(
                        hT[:, GCH * (m // 2):GCH * (m // 2 + 1), 0:P], bank[:, 0:GDIM].rearrange("p (k s) -> p k s", k=GCH)))
                if n < 2 * au.slabs:
                    at = slot(au.slots[s % 2])[:, KD * GDIM:(KD + 1) * GDIM]
                    dve.wait_ge(au.landed[s % 2], 32 * (s // 2 + 1))
                    dve.wait_ge(mixed_full, n + 1)
                    if n >= 2:
                        dve.wait_ge(tf, base + n - 1)
                    mixed = xn[:, c, GDIM:2 * GDIM]
                    V.tensor_tensor(mixed, SM[c][:, 0:GDIM], at, ALU.mult).then_inc(mixed_read, 1)
                    dve.wait_ge(mixed_read, n + 1)
                    dve.wait_ge(au.done, n + 1)
                    V.scalar_tensor_tensor(out=mixed, in0=mixed, scalar=gains[:, GC["bs"] + s:GC["bs"] + s + 1],
                                           in1=xn[:, c, 0:GDIM], op0=ALU.add, op1=ALU.mult).then_inc(gated_ready, 1)
            base += 2 * au.slabs
            add_down(0)

            norm(2, tf, tc, base, [(xT, GC["f"])])
            base += 4

            def gated(n, j, c, first, turned_before):
                dve.wait_ge(silu_ready, n + 1)
                if not first:
                    dve.wait_ge(tf, turned_before)
                V.tensor_tensor(xn[:, c, PAIR:2 * PAIR], xn[:, c, 0:PAIR], G[2 * j + c][:, PAIR:2 * PAIR], ALU.mult
                                ).then_inc(fu.done, 1)

            def hidden_even(g, s):
                even_turn(tf, tc, g, lambda bank: V.tensor_copy(
                    hT[:, bass.ds(s * 2, 2), 0:P], bank[:, 0:2 * P].rearrange("p (k s) -> p k s", k=2)))

            def ffn_body(i, first):
                for j in range(2):
                    for c in range(NT):
                        if c == 1:
                            hidden_even(i * 4 + (2 * j + base), i * 2 + j)
                        gated(i * 4 + (2 * j + c), j, c, first and j == 0, i * 4 + (2 * j + c - 1 + base))

            ffn_body(0, True)
            with dve.Fori(1, fu.slabs // 2) as i:
                ffn_body(i, False)
            last = 2 * (fu.slabs - 1)
            gated(last, 0, 0, False, last - 1 + base)
            hidden_even(last + base, fu.slabs - 1)
            gated(last + 1, 0, 1, False, last + base)
            base += 2 * fu.slabs
            add_down(4)

            norm(3, tf, tc, base, [(xT, GC["kv"]), (xT2, GC["b"])])
            base += 4
            heads = lambda c, at: work[:, c, at:at + HEADS * AUG].rearrange("p (h e) -> p h e", e=AUG)
            z = xn[:, 1, 512:544].rearrange("p (c n) -> p c n", c=NT)
            soft = xn[:, 1, 544:576].rearrange("p (c n) -> p c n", c=NT)
            logf = xn[:, 1, 576:608].rearrange("p (c n) -> p c n", c=NT)
            dve.wait_ge(tf, base)
            for which, (ph, at) in enumerate(((kv, KA), (qg, QA))):
                for c in range(NT):
                    V.memset(heads(c, at)[:, :, HD + 1 - which:HD + 2 - which], 1.0)
                for n in range(4):
                    s, c = n // 2, n % 2
                    dve.wait_ge(ph.done, n + 1)
                    x = heads(c, at)[:, 8 * s:8 * (s + 1), 0:HD]
                    sq = xn[:, 0, 0:BANK].rearrange("p (h e) -> p h e", e=HD)
                    steps.then(V.tensor_tensor(sq, x, x, ALU.mult))
                    steps.then(V.tensor_reduce(head_ss[:, c * 32 + which * 16 + 8 * s:c * 32 + which * 16 + 8 * (s + 1)],
                                               sq, AX_X, ALU.add))
                if which == 0:
                    dve.wait_ge(small_full, 1)
                    for c in range(NT):
                        ins = V.tensor_tensor(z[:, c, :], SM[0][:, c * HEADS:(c + 1) * HEADS], b_forget[:, :], ALU.add)
                    ins.then_inc(z_ready, 1)
                    log_sigmoid(dve, V, steps, xn[:, 1, 512:544], xn[:, 1, 544:576], xn[:, 1, 576:608],
                                ez_ready, ez1_ready, ln_ready, logf_ready, 1, z_ready)
            inverse_rms(head_ss, head_ss, HD)
            for which, at in enumerate((KA, QA)):
                for c in range(NT):
                    x = heads(c, at)[:, :, 0:HD]
                    r = head_ss[:, c * 32 + which * 16:c * 32 + (which + 1) * 16]
                    V.tensor_tensor(x, x, r.rearrange("p (h e) -> p h e", e=1).to_broadcast([P, HEADS, HD]), ALU.mult)
            dve.wait_ge(small_full, 2)
            for c in range(NT):
                cum = SM[1][:, c * HEADS:(c + 1) * HEADS].rearrange("p (h e) -> p h e", e=1)
                V.tensor_scalar(heads(c, KA)[:, :, HD:HD + 1], cum, -1.0, None, ALU.mult)
                ins = V.tensor_copy(heads(c, QA)[:, :, HD + 1:HD + 2], cum)
            ins.then_inc(aug_ready, 1)
            for g in range(0, 16, 2):
                even_turn(tf, tc, base + g, lambda bank: V.tensor_scalar(
                    hT[0:AUG, 2 * g:2 * g + 2, :], bank[0:AUG, :].rearrange("p (h s) -> p h s", h=2),
                    gains[0:AUG, GC["kq"] + g // 8:GC["kq"] + g // 8 + 1], None, ALU.mult))
            base += 16

            def attention(att, units, dst, gate_of, tf, tc, base):
                for u in range(units + 3):
                    if u < units:
                        q = u % 2
                        nk = P * (q + 1)
                        dve.wait_ge(att.full, u + 1)
                        steps.then(V.tensor_tensor_reduce(out=G[u % 4][:, 0:nk], in0=G[u % 4][:, 0:nk], in1=causal[:, P * (1 - q):S],
                                                          scale=1.0, scalar=MASKED, op0=ALU.add, op1=ALU.max,
                                                          accum_out=rmax[:, u:u + 1]))
                        V.tensor_scalar(nmax[:, u:u + 1], rmax[:, u:u + 1], -1.0, None, ALU.mult).then_inc(att.max_ready, 1)
                    w = u - 2
                    if 0 <= w < units and w % 2 == 0:
                        if w >= 4:
                            dve.wait_ge(att.out_full, w - 3)
                        even_turn(tf, tc, base + w, lambda bank: V.tensor_copy(xT_all[:, (w % 4) * S:(w % 4) * S + P], bank[:, 0:P]))
                    w = u - 3
                    if 0 <= w < units:
                        hd, q = w // 2, w % 2
                        dve.wait_ge(att.p_ready, w + 1)
                        steps.then(V.reciprocal(rinv[:, w:w + 1], rowsum[:, w:w + 1]))
                        dve.wait_ge(att.out_full, w + 1)
                        if gate_of is None:
                            V.tensor_scalar(dst(hd, q), SM[q][:, 0:HD], rinv[:, w:w + 1], None, ALU.mult).then_inc(att.out_done, 1)
                        else:
                            V.scalar_tensor_tensor(out=dst(hd, q), in0=SM[q][:, 0:HD], scalar=rinv[:, w:w + 1],
                                                   in1=gate_of(hd, q), op0=ALU.mult, op1=ALU.mult).then_inc(att.out_done, 1)

            gated_out = lambda hd, q: work[:, q, GA + hd * HD:GA + (hd + 1) * HD]
            dve.wait_ge(qg.done, 2 * qg.slabs)
            attention(att1, 2 * HEADS, gated_out, gated_out, tf, tc, base)
            base += 2 * HEADS
            norm_copies(tf, tc, base, [(xT, None)])
            base += 4
            add_down(8)

            norm(4, tf, tc, base, [(xT, GC["m"])])
            base += 4
            for c in range(NT):
                steps.then(V.memset(rank[:, c, 2 * E:COLS], -1000.0))
            V.memset(y_sb, 0.0).then_inc(y_copied[0], 1)
            V.memset(routeT, 0.0).then_inc(y_copied[1], 1)
            dve.wait_ge(small_full, 3)
            steps.then(V.tensor_copy(routing[:, 0:2 * E], SM[0][:, 0:2 * E]))
            for c in range(NT):
                steps.then(V.max(top8[:, c, :], logit[:, c, :]))
                steps.then(V.max_index(indices[:, c, :], top8[:, c, :], logit[:, c, :]))
                steps.then(V.tensor_copy(topi[:, c, :], indices[:, c, :]))
                V.tensor_tensor(gap[:, c:c + 1], top8[:, c, 1:2], top8[:, c, 0:1], ALU.subtract).then_inc(gap_diff, 1)
            dve.wait_ge(gap_exp, 1)
            steps.then(V.tensor_scalar(g1, gap, 1.0, None, ALU.add))
            steps.then(V.reciprocal(g1, g1))
            steps.then(V.tensor_tensor(g2, gap, g1, ALU.mult))
            for c in range(NT):
                steps.then(V.tensor_scalar(sel[:, c, :], iota[:, 0:E], topi[:, c, 0:1], None, ALU.is_equal))
                steps.then(V.tensor_scalar(tmp8, iota[:, 0:E], topi[:, c, 1:2], None, ALU.is_equal))
                steps.then(V.tensor_scalar(gate[:, c, 0:E], sel[:, c, :], g1[:, c:c + 1], None, ALU.mult))
                steps.then(V.scalar_tensor_tensor(out=gate[:, c, 0:E], in0=tmp8, scalar=g2[:, c:c + 1], in1=gate[:, c, 0:E],
                                                  op0=ALU.mult, op1=ALU.add))
                steps.then(V.tensor_tensor(sel[:, c, :], sel[:, c, :], tmp8, ALU.add))
                steps.then(V.tensor_copy(gate[:, c, E:2 * E], gate[:, c, 0:E]))
            V.memset(gate[:, :, 2 * E:COLS], 0.0).then_inc(mask_ready, 1)
            dve.wait_ge(small_full, 4)
            for c in range(NT):
                steps.then(V.tensor_tensor(rank[:, c, 0:E], sel[:, c, :], SM[1][:, c * E:(c + 1) * E], ALU.mult))
                steps.then(V.tensor_scalar(rank[:, c, 0:E], rank[:, c, 0:E], -1.0, None, ALU.add))
                steps.then(V.tensor_scalar(rank[:, c, E:2 * E], rank[:, c, 0:E], float(-P), None, ALU.add))
            steps.then(V.tensor_reduce(total, SM[1][:, 2 * E:3 * E], AX_X, ALU.max))
            steps.then(V.tensor_scalar(roundsf, total, float(P), 1.0, ALU.is_gt, ALU.add))
            steps.then(V.tensor_copy(rounds_i[:, 0:1], roundsf))
            steps.then(V.tensor_scalar(roundsf, roundsf, float(E), -1.0, ALU.mult, ALU.add))
            V.tensor_copy(rounds_i[:, 1:2], roundsf).then_inc(rounds_ready, 1)

            def make_pick(it):
                for c in range(NT):
                    ins = V.tensor_scalar(pick[:, c, :], iota[:, :], rank[:, c, bass.ds(it, 1)], None, ALU.is_equal)
                ins.then_inc(pick_ready, 1)

            def make_route(it):
                for c in range(NT):
                    ins = V.tensor_scalar(route[:, c, :], iota[:, :], rank[:, c, bass.ds(it, 1)],
                                          gate[:, c, bass.ds(it, 1)], ALU.is_equal, ALU.mult)
                ins.then_inc(route_ready, 1)

            def gather_copy(it):
                dve.wait_ge(gathered[0], it + 1)
                for k in range(KD):
                    ins = V.scalar_tensor_tensor(out=xg_lo[:, k * P:(k + 1) * P], in0=G[2 + k // 4][:, (k % 4) * P:(k % 4 + 1) * P],
                                                 scalar=gains[:, GC["m"] + k:GC["m"] + k + 1],
                                                 in1=xg_hi[:, k * P:(k + 1) * P].bitcast(F32), op0=ALU.mult, op1=ALU.subtract)
                ins.then_inc(gathered[1], 1)

            def e_turn(it, p):
                g = TURN_OF[p]
                dve.wait_ge(e_turned_hi, it * len(TURNS) + g + 1)
                expert_hidden_free(dve, it, p)
                V.tensor_tensor(e_hT_lo[:, p % 2, :], T[g % 2][:, :], e_hT_hi[:, p % 2, :].bitcast(F32), ALU.subtract
                                ).then_inc(e_turned_lo, 1)

            make_pick(0)
            for n in range(LEAD):
                e_make_lo(dve, 0, n)
            gather_copy(0)
            dve.wait_ge(rounds_ready, 1)
            rounds = dve.value_load(rounds_i[0:1, 0:1], min_val=1, max_val=2)
            V.memset(tmp8, 0.0).then_inc(up_read, 2)
            with dve.Fori(0, rounds * E) as it:
                make_route(it)
                for m, (kind, s) in enumerate(ORDER):
                    if m == len(ORDER) - 1:
                        gather_copy(it + 1)
                        e_turn(it, DOWNS - 1)
                    for n in (2 * m + LEAD, 2 * m + LEAD + 1):
                        e_make_lo(dve, it, n)
                    if kind == "down":
                        continue
                    dve.wait_ge(e_silu_ready, it * UPS + s + 1)
                    if s >= 2:
                        dve.wait_ge(e_turned, it * len(TURNS) + TURN_OF[s // 2 - 1] + 1)
                    else:
                        dve.wait_ge(e_turned, it * len(TURNS))
                    V.tensor_tensor(e_hid[:, s % 2, :], e_silu[:, s % 2, :], G[s % 2][:, PAIR:2 * PAIR], ALU.mult
                                    ).then_inc(up_read, 1)
                    if s == 1:
                        for c in range(NT):
                            for b in range(2):
                                dve.wait_ge(scatter_full, it * 4 + 2 * c + b + 1)
                                dst = h[:, c, b * BANK:(b + 1) * BANK]
                                V.tensor_tensor(dst, dst, G[2 + b][:, :], ALU.add).then_inc(scatter_added, 1)
                    if s == 3:
                        make_pick(it + 1)
                    if s % 2 == 0 and s >= 2:
                        e_turn(it, s // 2 - 1)
                dve.wait_ge(y_full, it * 2 + 2)
                dve.wait_ge(scatter_full, it * 4 + 4)
                V.tensor_copy(y_sb[:, BANK:2 * BANK], SM[1][:, :]).then_inc(y_copied[1], 1)
            for c in range(NT):
                for b in range(2):
                    dve.wait_ge(last_scatter, 2 * c + b + 1)
                    dst = h[:, c, b * BANK:(b + 1) * BANK]
                    V.tensor_tensor(dst, dst, G[2 + b][:, :], ALU.add).then_inc(h_ready, 1)

            tf, tc = turned2, turned2_copied
            base = 0
            flat = lambda n: rope[:, n, :]
            steps.then(V.tensor_copy(tokf, pos_i[:, :]))
            for c in range(NT):
                steps.then(V.tensor_scalar(rope[:, 1, c * ROPE_HALF:(c + 1) * ROPE_HALF], rope[:, 0, 0:ROPE_HALF],
                                           tokf[:, c:c + 1], None, ALU.mult))
            steps.then(V.tensor_scalar(flat(2), flat(1), 1.0 / (2 * math.pi), None, ALU.mult))
            steps.then(V.tensor_copy(turn_i[:, :], flat(2)))
            steps.then(V.tensor_copy(flat(2), turn_i[:, :]))
            c1 = 6.28125
            c2 = float(np.float32(round((2 * math.pi - c1) * 2 ** 20) / 2 ** 20))
            c3 = 2 * math.pi - c1 - c2
            steps.then(V.tensor_copy(flat(3), flat(1)))
            for part in (c1, c2, c3):
                steps.then(V.scalar_tensor_tensor(out=flat(3), in0=flat(2), scalar=-part, in1=flat(3), op0=ALU.mult, op1=ALU.add))
            steps.then(V.tensor_scalar(flat(3), flat(3), 3.1415925, -3.1415925, ALU.min, ALU.max))
            steps.then(V.tensor_scalar(flat(4), flat(3), -1.0, None, ALU.mult))
            steps.then(V.tensor_tensor(flat(4), flat(4), flat(3), ALU.min))
            V.tensor_scalar(flat(4), flat(4), math.pi / 2, None, ALU.add).then_inc(angle_ready, 1)

            norm(5, tf, tc, base, [(xT, GC["pre2"])])
            base += 4
            dve.wait_ge(tf, base)
            dve.wait_ge(small_full, 5)
            z2 = xn[:, 1, 512:520].rearrange("p (c n) -> p c n", c=NT)
            gi = xn[:, 1, 608:616].rearrange("p (c n) -> p c n", c=NT)
            for c in range(NT):
                V.tensor_tensor(gi[:, c, :], SM[0][:, 2 * ML_H * c:2 * ML_H * c + ML_H], b_if[:, 0:ML_H], ALU.add)
                ins = V.tensor_tensor(z2[:, c, :], SM[0][:, 2 * ML_H * c + ML_H:2 * ML_H * (c + 1)], b_if[:, ML_H:2 * ML_H], ALU.add)
            ins.then_inc(z_ready, 1)
            log_sigmoid(dve, V, steps, xn[:, 1, 512:520], xn[:, 1, 544:552], xn[:, 1, 576:584],
                        ez_ready, ez1_ready, ln_ready, logf_ready, 2, z_ready)
            dve.wait_ge(pr.done, 8)
            dve.wait_ge(sines_ready, 1)
            tmp = [xn[:, 0, n * P:(n + 1) * P].rearrange("p (h e) -> p h e", e=ROPE_HALF) for n in range(4)]
            for c in range(NT):
                qk = work[:, c, 0:2 * ATT_H * HD].rearrange("p (h e) -> p h e", e=HD)
                x1, x2 = qk[:, :, 0:ROPE_HALF], qk[:, :, ROPE_HALF:2 * ROPE_HALF]
                table = lambda n: rope[:, n:n + 1, c * ROPE_HALF:(c + 1) * ROPE_HALF].to_broadcast([P, 2 * ATT_H, ROPE_HALF])
                V.tensor_tensor(tmp[0], x1, table(6), ALU.mult)
                V.tensor_tensor(tmp[1], x2, table(5), ALU.mult)
                V.tensor_tensor(tmp[2], x2, table(6), ALU.mult)
                steps.then(V.tensor_tensor(tmp[3], x1, table(5), ALU.mult))
                V.tensor_tensor(x1, tmp[0], tmp[1], ALU.subtract)
                steps.then(V.tensor_tensor(x2, tmp[2], tmp[3], ALU.add))
            dve.wait_ge(small_full, 6)
            two = xn[:, 1, 640:672].rearrange("p (c w h e) -> p c w h e", c=NT, w=2, e=2)
            steps.then(V.memset(xn[:, 1, 640:672], 1.0))
            steps.then(V.tensor_copy(xn[:, 1, 616:624], SM[1][:, 0:2 * ML_H]))
            for c in range(NT):
                B = xn[:, 1, 616 + ML_H * c:616 + ML_H * (c + 1)].rearrange("p (h e) -> p h e", e=1)
                V.tensor_copy(two[:, c, 0, :, 0:1], B)
                ins = V.tensor_tensor(two[:, c, 1, :, 1:2], gi[:, c, :].rearrange("p (h e) -> p h e", e=1), B, ALU.subtract)
            ins.then_inc(aug_ready, 1)
            bsum = head_ss[:, 0:8]
            V.tensor_copy(bsum, xn[:, 1, 616:624]).then_inc(bsum_ready, 1)
            for g in range(0, 16, 2):
                even_turn(tf, tc, base + g, lambda bank: second_head_copy(
                    V.tensor_copy, lambda o, i_, s_: V.tensor_scalar(o, i_, s_, None, ALU.mult), g, bank))
            base += 16
            attention(att2, 2 * ATT_H, lambda hd, q: work[:, q, hd * HD:(hd + 1) * HD], None, tf, tc, base)
            base += 2 * ATT_H

            dve.wait_ge(bsum_ready, 1)
            dve.wait_ge(out_gate_ready, 1)
            for u in range(2 * ML_H + 3):
                if u < 2 * ML_H:
                    hd, q = u // 2, u % 2
                    nk = P * (q + 1)
                    dve.wait_ge(mls.full, u + 1)
                    steps.then(V.tensor_tensor_reduce(out=G[u % 4][:, 0:nk], in0=G[u % 4][:, 0:nk], in1=causal[:, P * (1 - q):S],
                                                      scale=1.0, scalar=MASKED, op0=ALU.add, op1=ALU.max,
                                                      accum_out=rmax[:, u:u + 1]))
                    steps.then(V.tensor_tensor(rmax[:, u:u + 1], rmax[:, u:u + 1], bsum[:, q * ML_H + hd:q * ML_H + hd + 1], ALU.max))
                    V.tensor_scalar(nmax[:, u:u + 1], rmax[:, u:u + 1], -1.0, None, ALU.mult).then_inc(mls.max_ready, 1)
                    dve.wait_ge(mls.p_ready, u + 1)
                    e_buf = xn_all[:, (u % 4) * S:(u % 4) * S + nk]
                    V.tensor_tensor_reduce(out=e_buf, in0=G[u % 4][:, S:S + nk], in1=e_buf, scale=1.0, scalar=0.0,
                                           op0=ALU.mult, op1=ALU.add, accum_out=rowsum[:, u:u + 1]).then_inc(weights_ready, 1)
                w = u - 2
                if 0 <= w < 2 * ML_H and w % 2 == 0:
                    if w >= 4:
                        dve.wait_ge(mls.out_full, w - 3)
                    even_turn(tf, tc, base + w, lambda bank: V.tensor_copy(xT_all[:, (w % 4) * S:(w % 4) * S + P], bank[:, 0:P]))
                w = u - 3
                if 0 <= w < 2 * ML_H:
                    hd, q = w // 2, w % 2
                    steps.then(V.tensor_scalar(rinv[:, w:w + 1], rowsum[:, w:w + 1], -1.0, None, ALU.mult))
                    steps.then(V.tensor_tensor(rinv[:, w:w + 1], rinv[:, w:w + 1], rowsum[:, w:w + 1], ALU.max))
                    steps.then(V.tensor_tensor(rinv[:, w:w + 1], rinv[:, w:w + 1], expm[:, w:w + 1], ALU.max))
                    steps.then(V.reciprocal(rinv[:, w:w + 1], rinv[:, w:w + 1]))
                    dve.wait_ge(mls.out_full, w + 1)
                    dst = work[:, q, 512 + hd * ML_V:512 + (hd + 1) * ML_V]
                    junk = xn[:, 1, 0:ML_V]
                    V.tensor_scalar(dst, SM[q][:, 0:ML_V], rinv[:, w:w + 1], None, ALU.mult).then_inc(mls.out_done, 1)
                    dve.wait_ge(mls.out_done, w + 1)
                    steps.then(V.tensor_tensor_reduce(out=junk, in0=dst, in1=dst, scale=1.0, scalar=0.0, op0=ALU.mult,
                                                      op1=ALU.add, accum_out=hss[:, w:w + 1]))
            inverse_rms(hss, hss, ML_V)
            for w in range(2 * ML_H):
                hd, q = w // 2, w % 2
                dst = work[:, q, 512 + hd * ML_V:512 + (hd + 1) * ML_V]
                V.scalar_tensor_tensor(out=dst, in0=dst, scalar=hss[:, w:w + 1],
                                       in1=work[:, q, MO + hd * ML_V:MO + (hd + 1) * ML_V],
                                       op0=ALU.mult, op1=ALU.mult).then_inc(hm_ready, 1)
            base += 2 * ML_H
            norm_copies(tf, tc, base, [(xT, GC["mix"])])
            base += 4

            def post_norm(nth, gain, ready):
                dve.wait_ge(post_squares, 4 * nth)
                dve.wait_ge(post_landed, 16 * nth)
                for c in range(NT):
                    steps.then(V.tensor_tensor(ss[:, c:c + 1], ss4[:, 2 * c:2 * c + 1], ss4[:, 2 * c + 1:2 * c + 2], ALU.add))
                inverse_rms(rstd, ss, D)
                for b in range(4):
                    c, at = b // 2, (b % 2) * BANK
                    steps.then(V.scalar_tensor_tensor(out=xn[:, c, at:at + BANK], in0=G[b][:, :], scalar=rstd[:, c:c + 1],
                                                      in1=gain[:, at:at + BANK], op0=ALU.mult, op1=ALU.mult))
                    dst = h[:, c, at:at + BANK]
                    V.tensor_tensor(dst, dst, xn[:, c, at:at + BANK], ALU.add).then_inc(h_ready, 1)

            post_norm(1, post_gain1, 16)

            norm(6, tf, tc, base, [(xT, GC["mlp2"])])
            base += 4

            def squared(n, c, first, turned_before):
                dve.wait_ge(mu.done, n + 1)
                if not first:
                    dve.wait_ge(tf, turned_before)
                V.tensor_tensor(xn[:, c, BANK:2 * BANK], xn[:, c, 0:BANK], xn[:, c, 0:BANK], ALU.mult).then_inc(relu2_ready, 1)

            def squared_even(g, s):
                even_turn(tf, tc, g, lambda bank: V.tensor_copy(
                    hT[:, bass.ds(s * 4, 4), 0:P], bank[:, :].rearrange("p (k s) -> p k s", k=4)))

            def mlp_body(i, first):
                for j in range(2):
                    for c in range(NT):
                        if c == 1:
                            squared_even(i * 4 + (2 * j + base), i * 2 + j)
                        squared(i * 4 + (2 * j + c), c, first and j == 0, i * 4 + (2 * j + c - 1 + base))

            mlp_body(0, True)
            with dve.Fori(1, mu.slabs // 2) as i:
                mlp_body(i, False)
            post_norm(2, post_gain2, 20)


_INS = ["x", "a_norm_g", "a_w_in", "a_v_norm_g", "a_w_spatial", "a_b_spatial", "a_w_out", "f_norm_g", "f_w_in",
        "f_w_out", "kv_norm_g", "kv_w", "kv_b_f", "k_norm_g", "b_norm_g", "b_w_in", "q_norm_g", "b_w_out", "m_norm_g",
        "m_w_router", "m_w_in", "m_w_out", "positions_2", "g_mix_pre_2", "w_in_2", "b_igate_2", "b_fgate_2",
        "g_mlstm_out_2", "w_out_2", "g_mix_post_2", "g_mlp_pre_2", "w_up_2", "w_down_2", "g_mlp_post_2"]


def kernel(**inputs):
    import concourse.bacc as bacc
    from concourse.bass_utils import run_bass_kernel_spmd as run

    nc = bacc.Bacc("TRN2", target_bir_lowering=False, num_devices=1)
    arrays, args = {}, {}
    for name in _INS:
        a = np.ascontiguousarray(inputs[name])
        arrays[f"in_{name}_dram"] = a
        args[name] = nc.dram_tensor(f"in_{name}_dram", a.shape, mybir.dt.from_np(a.dtype), kind="ExternalInput").ap()
    out = nc.dram_tensor("out_0_dram", (1, S, D), F32, kind="ExternalOutput").ap()
    build(nc, args, out)
    r = run(nc, [arrays], core_ids=[0])
    return r.results[0]["out_0_dram"]
```

```python
from contextlib import ExitStack
import math

import numpy as np

import concourse.bass as bass
from concourse import mybir

ALU = mybir.AluOpType
ACT = mybir.ActivationFunctionType
F32 = mybir.dt.float32
I32 = mybir.dt.int32
U32 = mybir.dt.uint32
F32R = mybir.dt.float32r
AX_X = mybir.AxisListType.X

P = 128
S = 256
NT = S // P
D = 1024
KD = D // P
BANK = 512
SLAB = KD * BANK
SLOTS = 7
EPS = 1e-6
MASKED = -1e30

A_HALF = 3072
GROUPS = 8
GDIM = A_HALF // GROUPS
GCH = GDIM // P
A_CHUNKS = A_HALF // P
D_FF = 2816
PAIR = BANK // 2
FF_SLABS = D_FF // PAIR
FF_CHUNKS = D_FF // P
HEADS = 16
HD = 64
AUG = HD + 2
KA, QA = 0, HEADS * AUG
VA, GA = 2 * HEADS * AUG, 2 * HEADS * AUG + D
ROW = GA + D
E = 8
D_EXP = 3584
UPS = D_EXP // PAIR
DOWNS = D_EXP // (4 * P)
ATT_H = 8
ML_H = 4
ML_V = 128
Q2, K2, V2, MQ, MK, MV, MO = 0, 512, 1024, 1536, 1792, 2048, 2560
PROJ = 3072
ROPE_HALF = 8
ROPE_THETA = 500000.0
D_FF2 = 4096
FF2_SLABS = D_FF2 // BANK
FF2_CHUNKS = D_FF2 // P

ORDER = [("up", 0), ("up", 1)]
for _p in range(DOWNS - 1):
    ORDER += [("up", 2 * _p + 2), ("up", 2 * _p + 3), ("down", _p)]
ORDER.append(("down", DOWNS - 1))
UNIT = SLAB // 2
UNITS = 2 * len(ORDER)
RAW_E = 2 * SLOTS
HI_ROUNDS = [5] * 6 + [4] * 3
HI_PLACE = [place for r in HI_ROUNDS for place in range(r)]
LEAD = 2
assert len(ORDER) == UPS + DOWNS and UNITS % RAW_E == 0 and len(HI_PLACE) == UNITS
TURNS = ["route" if _g == 1 else (_g if _g == 0 else _g - 1) for _g in range(DOWNS + 1)]
TURN_OF = {what: g for g, what in enumerate(TURNS)}


class Steps:

    def __init__(self, eng, sem):
        self.eng, self.sem, self.n, self.offset = eng, sem, 0, 0

    def then(self, ins):
        ins.then_inc(self.sem, 1)
        self.n += 1
        self.eng.wait_ge(self.sem, self.offset + self.n)


def build(nc, t, out):
    with ExitStack() as ctx:
        def sb(name, shape, dt=F32):
            return ctx.enter_context(nc.sbuf_tensor(name, shape, dt))

        def sem(name):
            return ctx.enter_context(nc.semaphore(name))

        arena_at = -(-nc.sbuf_base // 32) * 32
        ctx.enter_context(nc.sbuf_tensor("arena", [P, SLOTS * SLAB + NT * ROW + 32 * S + KD * S + 8], F32))

        def place(cols, at, name, dt):
            return nc.alloc_sbuf_tensor_at(name, [P, cols], dt, offset=arena_at + 4 * at)

        ring = place(SLOTS * SLAB, 0, "ring", F32)
        half_ring = RAW_E // 2 * UNIT
        e_arrived = [place(half_ring, b * half_ring, f"e_arrived{b}", F32) for b in range(2)]
        e_low = [place(half_ring, b * half_ring, f"e_low{b}", F32R) for b in range(2)]
        dense_raw = place(4 * SLAB, 0, "dense_raw", F32)
        dense_low = place(4 * SLAB, 0, "dense_low", F32R)
        dense_high = place(2 * SLAB, 4 * SLAB, "dense_high", F32R)
        xT_lo_all = place(KD * S, 6 * SLAB, "xT_lo_all", F32R)
        work_all = place(NT * ROW, SLOTS * SLAB, "work_all", F32)
        work_r = place(NT * ROW, SLOTS * SLAB, "work_r", F32R)
        hT_at = SLOTS * SLAB + NT * ROW
        hT_all = place(32 * S, hT_at, "hT_all", F32)
        hT_hi_all = place(32 * S, hT_at, "hT_hi_all", F32R)
        xT_all = place(KD * S, hT_at + 32 * S, "xT_all", F32)
        xT_hi_all = place(KD * S, hT_at + 32 * S, "xT_hi_all", F32R)
        e_high = place(5 * UNIT, hT_at, "e_high", F32R)
        assert 5 * UNIT == 32 * S + KD * S
        h_all = sb("h_all", [P, NT * D])
        xn_all = sb("xn_all", [P, NT * D])
        ident = sb("ident", [P, P])
        causal = sb("causal", [P, S])
        upto = sb("upto", [P, P])
        ones = sb("ones", [P, P])
        iota = sb("iota", [P, P])
        gains = sb("gains", [P, 74])
        w_forget = sb("w_forget", [P, KD, HEADS])
        w_router = sb("w_router", [P, KD, E])
        w_if = sb("w_if", [P, KD, 2 * ML_H])
        b_forget = sb("b_forget", [P, HEADS])
        b_if = sb("b_if", [P, 2 * ML_H])
        stats = sb("stats", [P, 368])
        routing = sb("routing", [P, 160])
        indices = sb("indices", [P, 2, 8], U32)
        rounds_i = sb("rounds_i", [P, 2], I32)
        pos_i = sb("pos_i", [P, NT], I32)
        turn_i = sb("turn_i", [P, NT * ROPE_HALF], I32)
        rope = sb("rope", [P, 8, NT * ROPE_HALF])

        G = [ctx.enter_context(nc.psum_tensor(f"G{i}", [P, BANK], F32)) for i in range(4)]
        SM = [ctx.enter_context(nc.psum_tensor(f"SM{i}", [P, BANK], F32)) for i in range(2)]
        T = [ctx.enter_context(nc.psum_tensor(f"T{i}", [P, BANK], F32)) for i in range(2)]

        hT = hT_all[:, :].rearrange("p (k s) -> p k s", s=S)
        work = work_all[:, :].rearrange("p (c n) -> p c n", c=NT)
        h = h_all[:, :].rearrange("p (c n) -> p c n", c=NT)
        xn = xn_all[:, :].rearrange("p (c n) -> p c n", c=NT)
        xT = xT_all[:, :].rearrange("p (k s) -> p k s", s=S)
        xT_hi = xT_hi_all[:, :].rearrange("p (k s) -> p k s", s=S)
        xT_lo = xT_lo_all[:, :].rearrange("p (k s) -> p k s", s=S)
        hT_hi = hT_hi_all[:, :].rearrange("p (k s) -> p k s", s=S)
        hT_lo = work_r[:, 0:32 * S].rearrange("p (k s) -> p k s", s=S)
        xT2 = hT[:, 0:KD, :]
        ws_raw = hT_all[:, 24 * S:24 * S + GROUPS * P].rearrange("p (g j) -> p g j", g=GROUPS)
        gain_rows = hT_all[0:74, 23 * S:23 * S + P]
        wsT = hT_all[:, 28 * S:28 * S + GROUPS * P]
        post_gain1 = work[:, 0, PROJ:PROJ + D]
        post_gain2 = ring[:, 6 * SLAB + KD * S:6 * SLAB + KD * S + D]

        def slot(j, memory=ring):
            return memory[:, j * SLAB:(j + 1) * SLAB]

        ss = stats[:, 0:2]
        rstd = stats[:, 2:4]
        vss = stats[:, 4:4 + NT * GROUPS]
        ss4 = stats[:, 20:24]
        head_ss = stats[:, 24:88]
        nmax = stats[:, 88:120]
        rowsum = stats[:, 120:152]
        rinv = stats[:, 152:184]
        rmax = stats[:, 184:216]
        expm = stats[:, 216:224]
        hss = stats[:, 224:232]
        tokf = stats[:, 232:234]
        variance = stats[:, 240:304]
        root = stats[:, 304:368]
        correction = stats[:, 88:152]

        GC = {"a": 0, "f": 8, "kv": 16, "b": 24, "m": 32, "pre2": 40, "mlp2": 48, "mix": 56, "bs": 64, "kq": 72}

        x_landed = sem("x_landed")
        params_landed = sem("params_landed")
        spatial_landed = sem("spatial_landed")
        consts_ready = sem("consts_ready")
        pool_step = sem("pool_step")
        vector_step = sem("vector_step")
        scalar_step = sem("scalar_step")
        gain_rows_ready = sem("gain_rows_ready")
        h_ready = sem("h_ready")
        variance_ready = sem("variance_ready")
        root_ready = sem("root_ready")
        hm_ready = sem("hm_ready")
        squares_ready = sem("squares_ready")
        xn_ready = sem("xn_ready")
        turned = sem("turned")
        turned_copied = [sem("turned_copied_v"), sem("turned_copied_s")]
        turned2 = sem("turned2")
        turned2_copied = [sem("turned2_copied_v"), sem("turned2_copied_s")]
        down_full = sem("down_full")
        spatial_ready = sem("spatial_ready")
        mixed_full = sem("mixed_full")
        mixed_read = sem("mixed_read")
        gated_ready = sem("gated_ready")
        silu_ready = sem("silu_ready")
        small_full = sem("small_full")
        z_ready = sem("z_ready")
        ez_ready = sem("ez_ready")
        ez1_ready = sem("ez1_ready")
        ln_ready = sem("ln_ready")
        logf_ready = sem("logf_ready")
        aug_ready = sem("aug_ready")
        gap_exp = sem("gap_exp")
        mask_ready = sem("mask_ready")
        rounds_ready = sem("rounds_ready")
        angle_ready = sem("angle_ready")
        sines_ready = sem("sines_ready")
        relu_ready = sem("relu_ready")
        relu2_ready = sem("relu2_ready")
        post_squares = sem("post_squares")
        post_landed = sem("post_landed")
        out_landed = sem("out_landed")

        class Phase:

            def __init__(self, name, slabs, slots, dmas=1, uses=2):
                self.name, self.slabs, self.slots, self.dmas, self.uses = name, slabs, slots, dmas, uses
                self.landed = [sem(f"{name}_landed{j}") for j in range(len(slots))]
                if uses:
                    self.full = sem(f"{name}_full")
                    self.done = sem(f"{name}_done")
                else:
                    self.used = sem(f"{name}_used")

        av = Phase("av", GROUPS, [0, 1])
        au = Phase("au", GROUPS, [2, 3], dmas=2)
        ao = Phase("ao", A_CHUNKS // 4, [0, 1], uses=0)
        fu = Phase("fu", FF_SLABS, [0, 1])
        fo = Phase("fo", FF_CHUNKS // 2, [2, 3], uses=0)
        kv = Phase("kv", 4, [4, 5])
        qg = Phase("qg", 4, [0, 1])
        bo = Phase("bo", 2, [4, 5], uses=0)
        pr = Phase("pr", PROJ // BANK, [0, 1])
        po = Phase("po", 2, [4, 5], uses=0)
        mu = Phase("mu", FF2_SLABS, [2, 3])
        md = Phase("md", FF2_SLABS, [0, 1], uses=0)

        dense_hi, dense_lo = sem("dense_hi"), sem("dense_lo")
        before = 0
        for ph, units, dmas in ((av, 2 * GROUPS, (1, 1)), (au, 2 * GROUPS, (2, 1)), (fu, 2 * FF_SLABS, (2, 2)),
                                (fo, FF_CHUNKS // 2, (1, 1)), (mu, 2 * FF2_SLABS, (1, 1)), (md, FF2_CHUNKS // 2, (1, 1))):
            ph.before = before
            before += units
            ph.landed = ph.landed + [sem(f"{ph.name}_landed{q}") for q in (2, 3)]
            if ph not in (fo, md):
                ph.half_used = sem(f"{ph.name}_half_used")
            ph.units, ph.dmas = units, dmas
            ph.width = GDIM if ph in (av, au) else BANK
        fo.turned_by, md.turned_by = fu.units % 4, mu.units % 4
        split_copied = sem("split_copied")

        def unit_place(ph, q, memory):
            at = ph.slots[q // 2] * SLAB + q % 2 * UNIT
            return memory[:, at:at + UNIT]

        def high_place(n):
            return dense_high[:, n * UNIT:(n + 1) * UNIT]

        def make_high(act, ph, i, q, to):
            dmas, n = ph.dmas[q % 2], 4 * ph.width
            act.wait_ge(ph.landed[q], i * (16 * dmas) + 16 * dmas)
            nc.scalar.copy(high_place(to)[:, 0:n], unit_place(ph, q, dense_raw)[:, 0:n]).then_inc(dense_hi, 1)

        def make_low(dve, ph, i, q, to):
            dve.wait_ge(dense_hi, i * 4 + (q + 1 + ph.before))
            n = 4 * ph.width
            nc.vector.tensor_tensor(unit_place(ph, q, dense_low)[:, 0:n], unit_place(ph, q, dense_raw)[:, 0:n],
                                    high_place(to)[:, 0:n].bitcast(F32), ALU.subtract).then_inc(dense_lo, 1)

        def up_units(make, eng, ph, i, j):
            for part in range(2):
                make(eng, ph, i, 2 * j + part, 2 * j + part)

        def down_units(make, eng, up, down, first, end):
            for u in range(first, end):
                if make is make_high:
                    if u >= 4:
                        eng.wait_ge(down.used, u - 3)
                    else:
                        eng.wait_ge(up.full, up.units - (2 if u < 2 else 0))
                make(eng, down, u // 4, u % 4, (down.turned_by + u) % 4)

        class Attention:
            def __init__(self, name):
                self.full = sem(f"{name}_logits_full")
                self.max_ready = sem(f"{name}_max_ready")
                self.p_ready = sem(f"{name}_p_ready")
                self.out_full = sem(f"{name}_out_full")
                self.out_done = sem(f"{name}_out_done")

        att1, att2, mls = Attention("att1"), Attention("att2"), Attention("mlstm")
        weights_ready = sem("mlstm_weights_ready")
        out_gate_ready = sem("out_gate_ready")

        e_landed = [sem(f"expert_landed{j}") for j in range(SLOTS)]
        e_hi = sem("expert_hi")
        e_lo = sem("expert_lo")
        up_half_used = sem("up_half_used")
        up_full = sem("up_full")
        up_read = sem("up_read")
        e_silu_ready = sem("e_silu_ready")
        down_used = sem("down_used")
        y_full = sem("y_full")
        y_copied = [sem("y_copied_s"), sem("y_copied_v")]
        gather_full = sem("gather_full")
        gathered = [sem("gathered_s"), sem("gathered_v")]
        scatter_full = sem("scatter_full")
        scatter_added = sem("scatter_added")
        pick_ready = sem("pick_ready")
        route_ready = sem("route_ready")
        e_turned = sem("e_turned")
        e_turned_hi = sem("e_turned_hi")
        e_turned_lo = sem("e_turned_lo")

        y_sb = work_all[:, 0:D]
        routeT = work_all[:, 1024:1280]
        pick = work_all[:, 1280:1536].rearrange("p (c s) -> p c s", c=NT)
        route = work_all[:, 1536:1792].rearrange("p (c s) -> p c s", c=NT)
        e_silu = work_all[:, 1792:2304].rearrange("p (b n) -> p b n", b=2)
        e_hid = work_all[:, 2304:2816].rearrange("p (b n) -> p b n", b=2)
        e_hT_hi = work_r[:, 2816:3840].rearrange("p (b n) -> p b n", b=2)
        e_hT_lo = work_r[:, 3840:4864].rearrange("p (b n) -> p b n", b=2)
        xg_hi = work_r[:, 4864:4864 + KD * P]
        xg_lo = work_r[:, 5888:5888 + KD * P]

        COLS = 2 * E + 1
        logit = routing[:, 0:16].rearrange("p (c e) -> p c e", c=NT)
        top8 = routing[:, 16:32].rearrange("p (c e) -> p c e", c=NT)
        topi = routing[:, 32:48].rearrange("p (c e) -> p c e", c=NT)
        sel = routing[:, 48:64].rearrange("p (c e) -> p c e", c=NT)
        rank = routing[:, 64:64 + NT * COLS].rearrange("p (c e) -> p c e", c=NT)
        gate = routing[:, 100:100 + NT * COLS].rearrange("p (c e) -> p c e", c=NT)
        tmp8 = routing[:, 136:144]
        gap = routing[:, 144:146]
        g1 = routing[:, 146:148]
        g2 = routing[:, 148:150]
        total = routing[:, 150:151]
        roundsf = routing[:, 151:152]

        a_in = t["a_w_in"][0].rearrange("(k p) n -> p k n", p=P)
        a_out = t["a_w_out"][0].rearrange("(s k p) n -> s p k n", p=P, k=4)
        f_out = t["f_w_out"][0].rearrange("(s k p) n -> s p k n", p=P, k=2)
        kv_w = t["kv_w"].rearrange("(k p) n -> p k n", p=P)
        b_in = t["b_w_in"][0].rearrange("(k p) n -> p k n", p=P)
        b_out = t["b_w_out"][0].rearrange("(s k p) n -> s p k n", p=P, k=4)
        m_in = t["m_w_in"][0].rearrange("e (k p) (b n) -> e p k b n", p=P, b=2)
        m_out = t["m_w_out"][0].rearrange("e (s k p) n -> e s p k n", p=P, k=2)
        w_in2 = t["w_in_2"][0].rearrange("(k p) n -> p k n", p=P)
        w_out2 = t["w_out_2"][0].rearrange("(s k p) n -> s p k n", p=P, k=4)
        w_up2 = t["w_up_2"][0].rearrange("(k p) n -> p k n", p=P)
        w_down2 = t["w_down_2"][0].rearrange("(s k p) n -> s p k n", p=P, k=2)

        def cols(j, n, memory=ring):
            return slot(j, memory)[:, 0:KD * n].rearrange("p (k n) -> p k n", k=KD)

        def rows(j, k, memory=ring):
            return slot(j, memory)[:, 0:k * D].rearrange("p (k n) -> p k n", k=k)

        last_scatter = sem("last_scatter")

        def running_sums(pe, x, n):
            nc.tensor.matmul(SM[1][:, 0:n], upto[:, :], x[:, 0, :], start=True, stop=True)
            nc.tensor.matmul(SM[1][:, n:2 * n], ones[:, :], x[:, 0, :], start=True, stop=False)
            return nc.tensor.matmul(SM[1][:, n:2 * n], upto[:, :], x[:, 1, :], start=False, stop=True)


        v_squared = sem("v_squared")
        gap_diff = sem("gap_diff")
        bsum_ready = sem("bsum_ready")

        def log_sigmoid(dve, V, steps, z, w, dst, ez_ready, ez1_ready, ln_ready, logf_ready, n, z_ready):
            dve.wait_ge(ez_ready, n)
            V.tensor_scalar(w, w, 1.0, None, ALU.add).then_inc(ez1_ready, 1)
            dve.wait_ge(ln_ready, n)
            dve.wait_ge(z_ready, n)
            V.scalar_tensor_tensor(out=dst, in0=z, scalar=0.0, in1=w, op0=ALU.min, op1=ALU.subtract).then_inc(logf_ready, 1)


        def softplus(eng, steps, z, w, z_ready, ez_ready, ez1_ready, ln_ready, n):
            eng.wait_ge(z_ready, n)
            steps.then(nc.scalar.activation(w, z, ACT.Abs))
            nc.scalar.activation(w, w, ACT.Exp, scale=-1.0).then_inc(ez_ready, 1)
            eng.wait_ge(ez1_ready, n)
            nc.scalar.activation(w, w, ACT.Ln).then_inc(ln_ready, 1)

        def e_consumed(eng, it, n):
            kind, s = ORDER[n // 2]
            if kind == "up":
                eng.wait_ge(up_full if n % 2 else up_half_used, it * UPS + (s + 1))
            elif n < UNITS - 1:
                eng.wait_ge(down_used, it * (2 * DOWNS - 1) + (2 * s + n % 2 + 1))
            else:
                eng.wait_ge(y_full, it * 2 + 2)

        def e_raw(n, memory):
            at = n % RAW_E % SLOTS
            return memory[n % RAW_E // SLOTS][:, at * UNIT:(at + 1) * UNIT]

        def e_hi_unit(n):
            at = HI_PLACE[n % UNITS]
            return e_high[:, at * UNIT:(at + 1) * UNIT]

        def e_make_hi(act, it, n):
            act.wait_ge(e_landed[n % RAW_E // 2], it * (64 * (UNITS // RAW_E)) + 64 * (n // RAW_E + 1))
            if n >= max(HI_ROUNDS):
                e_consumed(act, it, max(m for m in range(n) if HI_PLACE[m % UNITS] == HI_PLACE[n % UNITS]))
            elif n >= LEAD:
                act.wait_ge(down_used, it * (2 * DOWNS - 1))
                act.wait_ge(y_full, it * 2)
            nc.scalar.copy(e_hi_unit(n), e_raw(n, e_arrived)).then_inc(e_hi, 1)

        def e_make_lo(dve, it, n):
            dve.wait_ge(e_hi, it * UNITS + (n + 1))
            nc.vector.tensor_tensor(e_raw(n, e_low), e_raw(n, e_arrived), e_hi_unit(n).bitcast(F32), ALU.subtract
                                    ).then_inc(e_lo, 1)

        def expert_hidden_free(eng, it, p):
            if p >= 2:
                eng.wait_ge(down_used, it * (2 * DOWNS - 1) + 2 * (p - 1))
            elif p == 0:
                eng.wait_ge(y_full, it * 2)
            else:
                eng.wait_ge(down_used, it * (2 * DOWNS - 1))

        def second_head_copy(copy, mul, g, bank):
            if g < 12:
                dst = hT[0:HD, 2 * g:2 * g + 2, :]
                src = bank[0:HD, :].rearrange("p (h s) -> p h s", h=2)
                if g < 4 or g >= 10:
                    return mul(dst, src, HD ** -0.5)
                return copy(dst, src)
            return copy(hT[0:2, 2 * g:2 * g + 2, :], bank[0:2, :].rearrange("p (h s) -> p h s", h=2))

        block = ctx.enter_context(nc.Block())

        @block.sync
        def _(sp):
            def stream(ph, load, handover):
                n = len(ph.slots)

                def used(i):
                    if ph.uses:
                        sp.wait_ge(ph.full, (i + 1) * ph.uses)
                    else:
                        sp.wait_ge(ph.used, i + 1)

                for j in range(n):
                    handover(j)
                    load(j, j, ph.slots[j])
                whole = ph.slabs // n
                if whole > 1:
                    with sp.Fori(1, whole) as i:
                        for j in range(n):
                            used(i * n + (j - n))
                            load(i * n + j, j, ph.slots[j])
                for s in range(whole * n, ph.slabs):
                    used(s - n)
                    load(s, s % n, ph.slots[s % n])

            def plain(ph, src):
                def load(s, j, at):
                    sp.dma_start(cols(at, BANK), src[:, :, bass.ds(s * BANK, BANK)]).then_inc(ph.landed[j], 16)
                return load

            def down(ph, src, k):
                def load(s, j, at):
                    sp.dma_start(rows(at, k), src[bass.ds(s, 1)].rearrange("s p k n -> p (s k) n")).then_inc(ph.landed[j], 16)
                return load

            def stream_units(ph, load, handover):
                for q in range(4):
                    handover(q)
                    load(0, q)

                def used(i, q):
                    if ph in (fo, md):
                        sp.wait_ge(ph.used, i * 4 + (q - 3))
                    elif q % 2 == 0:
                        sp.wait_ge(ph.half_used, i * 2 + (q // 2 - 1))
                        if ph is au:
                            sp.wait_ge(mixed_read, i * 4 + (q - 2))
                    else:
                        sp.wait_ge(ph.full, i * 4 + (q - 3))

                with sp.Fori(1, ph.units // 4) as i:
                    for q in range(4):
                        used(i, q)
                        load(i, q)
                for u in range(ph.units // 4 * 4, ph.units):
                    used(u // 4, u % 4)
                    load(u // 4, u % 4)

            def load_half(ph, src, shift):
                def load(i, q):
                    n = ph.width
                    sp.dma_start(unit_place(ph, q, dense_raw)[:, 0:4 * n].rearrange("p (k n) -> p k n", k=4),
                                 src[:, 4 * (q % 2):4 * (q % 2) + 4, bass.ds(i * (2 * n) + (q // 2 * n + shift), n)]
                                 ).then_inc(ph.landed[q], 16)
                return load

            load_u_columns = load_half(au, a_in, 0)

            def load_u(i, q):
                load_u_columns(i, q)
                if q % 2 == 0:
                    sp.dma_start(unit_place(au, q, dense_raw)[:, 4 * GDIM:5 * GDIM],
                                 t["a_v_norm_g"][0:1, bass.ds(i * (2 * GDIM) + q // 2 * GDIM, GDIM)].to_broadcast([P, GDIM])
                                 ).then_inc(au.landed[q], 16)

            f_in_pairs = t["f_w_in"][0].rearrange("(k p) (b n) -> p k b n", p=P, b=2)

            def load_pair(i, q):
                for b in range(2):
                    sp.dma_start(unit_place(fu, q, dense_raw).rearrange("p (k b n) -> p k b n", k=4, b=2)[:, :, b, :],
                                 f_in_pairs[:, 4 * (q % 2):4 * (q % 2) + 4, b, bass.ds(i * (2 * PAIR) + q // 2 * PAIR, PAIR)]
                                 ).then_inc(fu.landed[q], 16)

            def load_rows(ph, src):
                def load(i, q):
                    sp.dma_start(unit_place(ph, q, dense_raw).rearrange("p (k n) -> p k n", k=2),
                                 src[bass.ds(i * 4 + q, 1)].rearrange("s p k n -> p (s k) n")).then_inc(ph.landed[q], 16)
                return load

            free = lambda j: None
            stream_units(av, load_half(av, a_in, A_HALF), free)
            stream_units(au, load_u, free)
            stream(ao, down(ao, a_out, 4), lambda j: sp.wait_ge(av.full, 2 * av.slabs))
            stream_units(fu, load_pair, lambda q: sp.wait_ge(down_full, 4))
            def groups_done(q):
                sp.wait_ge(au.full, 2 * au.slabs)
                sp.wait_ge(mixed_read, 2 * au.slabs)

            stream_units(fo, load_rows(fo, f_out), groups_done)
            stream(kv, plain(kv, kv_w), lambda j: sp.wait_ge(down_full, 8))
            stream(qg, plain(qg, b_in), lambda j: sp.wait_ge(fu.full, 2 * fu.slabs))
            stream(bo, down(bo, b_out, 4), lambda j: sp.wait_ge(kv.full, 2 * kv.slabs))

            def fill(e, n):
                kind, s = ORDER[n // 2]
                half = n % 2
                at = e_raw(n, e_arrived)
                for b in range(2):
                    if kind == "up":
                        sp.dma_start(at.rearrange("p (k b n) -> p k b n", k=4, b=2)[:, :, b, :],
                                     m_in[bass.ds(e, 1), :, 4 * half:4 * half + 4, b, s * PAIR:(s + 1) * PAIR
                                          ].rearrange("e p k n -> p (e k) n")).then_inc(e_landed[n % RAW_E // 2], 16)
                    else:
                        sp.dma_start(at.rearrange("p (k n) -> p k n", k=2)[:, b:b + 1, :],
                                     m_out[bass.ds(e, 1), 2 * s + half, :, b:b + 1, :].rearrange("e p k n -> p (e k) n")
                                     ).then_inc(e_landed[n % RAW_E // 2], 16)

            for n in range(UNITS):
                if n < 4:
                    sp.wait_ge(qg.full, 2 * qg.slabs)
                elif n in (8, 9, 10, 11):
                    sp.wait_ge(down_full, 12)
                elif n < RAW_E:
                    sp.wait_ge(down_full, 8)
                else:
                    e_consumed(sp, 0, n - RAW_E)
                fill(0, n)

            def expert_loop(before, count, expert):
                with sp.Fori(0, count) as i:
                    for n in range(UNITS):
                        if n < RAW_E:
                            e_consumed(sp, i + before, n - RAW_E + UNITS)
                        else:
                            e_consumed(sp, i + (before + 1), n - RAW_E)
                        fill(i + expert, n)

            expert_loop(0, E - 1, 1)
            sp.wait_ge(rounds_ready, 1)
            last = sp.value_load(rounds_i[0:1, 1:2], min_val=E - 1, max_val=2 * E - 1)
            with sp.If(last > E - 1):
                expert_loop(E - 1, E, 0)

            for n in range(LEAD):
                e_consumed(sp, last, n - RAW_E + UNITS)
                fill(0, n)

            def after_experts():
                sp.wait_ge(h_ready, 13)

            stream(pr, plain(pr, w_in2), lambda j: after_experts())
            stream(po, down(po, w_out2, 4), lambda j: after_experts())
            stream_units(mu, load_half(mu, w_up2, 0), lambda q: after_experts())
            stream_units(md, load_rows(md, w_down2), lambda q: sp.wait_ge(pr.full, 2 * pr.slabs))
            for c in range(NT):
                sp.wait_ge(h_ready, 22 + 2 * c)
                sp.dma_start(out[0, c * P:(c + 1) * P, :], h[:, c, :]).then_inc(out_landed, 16)
            sp.wait_ge(out_landed, 32)

        @block.gpsimd
        def _(pool):
            steps = Steps(pool, pool_step)
            steps.then(nc.gpsimd.memset(ident[:, :], 0.0))
            nc.gpsimd.affine_select(out=ident[:, :], in_=ident[:, :], compare_op=ALU.not_equal, fill=1.0, base=0,
                                    pattern=[[-1, P]], channel_multiplier=1).then_inc(consts_ready, 1)
            steps.then(nc.gpsimd.memset(ones[:, :], 1.0))
            nc.gpsimd.affine_select(out=upto[:, :], in_=ones[:, :], compare_op=ALU.is_ge, fill=0.0, base=0,
                                    pattern=[[1, P]], channel_multiplier=-1).then_inc(consts_ready, 1)
            steps.then(nc.gpsimd.memset(causal[:, :], 0.0))
            nc.gpsimd.affine_select(out=causal[:, :], in_=causal[:, :], compare_op=ALU.is_ge, fill=MASKED, base=P,
                                    pattern=[[-1, S]], channel_multiplier=1).then_inc(consts_ready, 1)
            nc.gpsimd.iota(iota[:, :], pattern=[[1, P]], base=0, channel_multiplier=0,
                           allow_small_or_imprecise_dtypes=True).then_inc(consts_ready, 1)
            inv = (np.float32(ROPE_THETA) ** (-np.arange(0, 2 * ROPE_HALF, 2, dtype=np.float32) / np.float32(2 * ROPE_HALF)))
            for f in range(ROPE_HALF):
                ins = nc.gpsimd.memset(rope[:, 0, f:f + 1], float(inv[f]))
            ins.then_inc(consts_ready, 1)

        @block.scalar
        def _(act):
            steps = Steps(act, scalar_step)
            roots = [0]

            def take_root(w):
                roots[0] += 1
                act.wait_ge(variance_ready, roots[0])
                nc.scalar.activation(root[:, 0:w], variance[:, 0:w], ACT.Sqrt).then_inc(root_ready, 1)

            act.dma_start(h, t["x"][0].rearrange("(c p) n -> p c n", p=P)).then_inc(x_landed, 16)
            act.wait_ge(gain_rows_ready, 1)
            row = lambda name, n: gain_rows[GC[name]:GC[name] + n, :]
            n_params = 0
            for name, src in (("a", t["a_norm_g"][0]), ("f", t["f_norm_g"][0]), ("kv", t["kv_norm_g"]),
                              ("b", t["b_norm_g"][0]), ("m", t["m_norm_g"][0]), ("pre2", t["g_mix_pre_2"][0]),
                              ("mlp2", t["g_mlp_pre_2"][0])):
                act.dma_start(row(name, KD), src.rearrange("(k p) -> k p", p=P)).then_inc(params_landed, 16)
            act.dma_start(gain_rows[GC["mix"] + 4:GC["mix"] + 8, :],
                          t["g_mlstm_out_2"][0].rearrange("(k p) -> k p", p=P)).then_inc(params_landed, 16)
            act.dma_start(row("bs", GROUPS), t["a_b_spatial"][0]).then_inc(params_landed, 16)
            act.dma_start(gain_rows[GC["kq"]:GC["kq"] + 1, 0:HD], t["k_norm_g"].rearrange("(a n) -> a n", a=1)
                          ).then_inc(params_landed, 16)
            act.dma_start(gain_rows[GC["kq"] + 1:GC["kq"] + 2, 0:HD], t["q_norm_g"]).then_inc(params_landed, 16)
            act.dma_start(ws_raw, t["a_w_spatial"][0].rearrange("g i j -> i g j")).then_inc(spatial_landed, 16)
            act.dma_start(w_forget[:, :, :], kv_w[:, :, 2 * D:2 * D + HEADS]).then_inc(params_landed, 16)
            act.dma_start(w_router[:, :, :], t["m_w_router"][0].rearrange("(k p) n -> p k n", p=P)
                          ).then_inc(params_landed, 16)
            act.dma_start(w_if[:, :, :], w_in2[:, :, PROJ:PROJ + 2 * ML_H]).then_inc(params_landed, 16)
            act.dma_start(b_forget[:, :], t["kv_b_f"].rearrange("(a n) -> a n", a=1).to_broadcast([P, HEADS])
                          ).then_inc(params_landed, 16)
            act.dma_start(b_if[:, 0:ML_H], t["b_igate_2"].to_broadcast([P, ML_H])).then_inc(params_landed, 16)
            act.dma_start(b_if[:, ML_H:2 * ML_H], t["b_fgate_2"].to_broadcast([P, ML_H])).then_inc(params_landed, 16)
            act.dma_start(pos_i[:, :], t["positions_2"][0].rearrange("(c p) -> p c", p=P),
                          allow_slow_non_contiguous=True).then_inc(params_landed, 16)

            def squares():
                for c in range(NT):
                    nc.scalar.activation(xn[:, c, :], h[:, c, :], ACT.Square, accum_out=ss[:, c:c + 1]).then_inc(squares_ready, 1)

            def odd_turn(tf, tc, g, copy):
                act.wait_ge(tf, g + 1)
                copy(T[1]).then_inc(tc[1], 1)

            def norm_copies(tf, tc, base, outs):
                for j in (1, 3):
                    def copy(bank, j=j):
                        for dst, gc in outs:
                            for k in (2 * j, 2 * j + 1):
                                src = bank[:, (k % 2) * S:(k % 2 + 1) * S]
                                if gc is None:
                                    ins = nc.scalar.copy(dst[:, k, :], src)
                                else:
                                    ins = nc.scalar.mul(dst[:, k, :], src, gains[:, gc + k:gc + k + 1])
                        return ins
                    odd_turn(tf, tc, base + j, copy)

            act.wait_ge(x_landed, 16)
            squares()
            take_root(NT)
            base = 2
            act.wait_ge(turned, 2)
            nc.scalar.copy(wsT[:, 0:BANK], T[1][:, :])
            nc.scalar.copy(wsT[:, BANK:2 * BANK], G[3][:, :]).then_inc(turned_copied[1], 1)
            act.wait_ge(turned_copied[0], 1)
            up_units(make_high, act, av, 0, 0)

            def high_norm_copies(tf, base, gc):
                for j in range(4):
                    act.wait_ge(tf, base + j + 1)
                    for k in (2 * j, 2 * j + 1):
                        ins = nc.scalar.mul(xT_hi[:, k, :], T[j % 2][:, (k % 2) * S:(k % 2 + 1) * S], gains[:, gc + k:gc + k + 1])
                    ins.then_inc(split_copied, 1)

            high_norm_copies(turned, base, GC["a"])
            base += 4

            def gelu_v(i, j, c):
                n = i * 4 + 2 * j + c
                act.wait_ge(av.full, n + 1)
                nc.scalar.activation(work[:, c, bass.ds(i * (2 * GDIM) + j * GDIM, GDIM)], G[2 * j + c][:, 0:GDIM],
                                     ACT.Gelu).then_inc(av.done, 1)

            def v_slab(i, j, last=False):
                if last:
                    up_units(make_high, act, au, 0, 0)
                else:
                    up_units(make_high, act, av, i + j, 1 - j)
                for c in range(NT):
                    gelu_v(i, j, c)

            with act.Fori(0, av.slabs // 2 - 1) as i:
                for j in range(2):
                    v_slab(i, j)
            v_slab(av.slabs // 2 - 1, 0)
            v_slab(av.slabs // 2 - 1, 1, last=True)
            take_root(NT)

            def gated_odd(s):
                odd_turn(turned, turned_copied, base + 2 * s + 1, lambda bank: nc.scalar.copy(
                    hT[:, GCH * s:GCH * (s + 1), P:2 * P], bank[:, 0:GDIM].rearrange("p (k s) -> p k s", k=GCH)))

            for s in range(au.slabs):
                if s < au.slabs - 1:
                    up_units(make_high, act, au, (s + 1) // 2, (s + 1) % 2)
                if s:
                    gated_odd(s - 1)
                for c in range(NT):
                    n = 2 * s + c
                    act.wait_ge(au.full, n + 1)
                    if n >= 2:
                        act.wait_ge(gated_ready, n - 1)
                    nc.scalar.activation(xn[:, c, 0:GDIM], G[n % 4][:, 0:GDIM], ACT.Gelu).then_inc(au.done, 1)
            gated_odd(au.slabs - 1)
            base += 2 * au.slabs

            def norm(ready, outs, tf, tc, base, splits=None):
                for c in range(NT):
                    act.wait_ge(h_ready, ready + 2 * c + 2)
                    nc.scalar.activation(xn[:, c, :], h[:, c, :], ACT.Square, accum_out=ss[:, c:c + 1]).then_inc(squares_ready, 1)
                take_root(NT)
                if splits is None:
                    norm_copies(tf, tc, base, outs)
                else:
                    up_units(make_high, act, splits, 0, 0)
                    high_norm_copies(tf, base, outs[0][1])

            def hidden_high(tf, g, s, par, per):
                act.wait_ge(tf, g + 1)
                nc.scalar.copy(hT_hi[:, bass.ds(s * per, per), par * P:(par + 1) * P],
                               T[par][:, 0:per * P].rearrange("p (k s) -> p k s", k=per)).then_inc(split_copied, 1)

            norm(0, [(xT, GC["f"])], turned, turned_copied, base, splits=fu)
            base += 4

            def silu(n, j, c, first):
                act.wait_ge(fu.full, n + 1)
                if not first:
                    act.wait_ge(fu.done, n - 1)
                nc.scalar.activation(xn[:, c, 0:PAIR], G[2 * j + c][:, 0:PAIR], ACT.Silu).then_inc(silu_ready, 1)

            def ffn_slab(i, j, first, last=False):
                if last:
                    down_units(make_high, act, fu, fo, 0, 2)
                else:
                    up_units(make_high, act, fu, i + j, 1 - j)
                if not first:
                    for c in range(NT):
                        hidden_high(turned, i * 4 + (2 * j - 2 + c + base), i * 2 + (j - 1), c, 2)
                for c in range(NT):
                    silu(i * 4 + (2 * j + c), j, c, first)

            ffn_slab(0, 0, True)
            ffn_slab(0, 1, False)
            with act.Fori(1, fu.slabs // 2) as i:
                for j in range(2):
                    ffn_slab(i, j, False)
            ffn_slab(fu.slabs // 2, 0, False, last=True)
            for c in range(NT):
                hidden_high(turned, 2 * fu.slabs - 2 + c + base, fu.slabs - 1, c, 2)
            base += 2 * fu.slabs
            down_units(make_high, act, fu, fo, 2, fo.units)

            norm(4, [(xT, GC["kv"]), (xT2, GC["b"])], turned, turned_copied, base)
            base += 4
            for ph in (kv, qg):
                for n in range(2 * ph.slabs):
                    s, c = n // 2, n % 2
                    act.wait_ge(ph.full, n + 1)
                    if s < 2:
                        at = KA if ph is kv else QA
                        dst = work[:, c, at + 8 * s * AUG:at + 8 * (s + 1) * AUG].rearrange("p (h e) -> p h e", e=AUG)[:, :, 0:HD]
                        nc.scalar.copy(dst, G[n % 4][:, :].rearrange("p (h e) -> p h e", e=HD)).then_inc(ph.done, 1)
                    elif ph is kv:
                        nc.scalar.copy(work[:, c, VA + (s - 2) * BANK:VA + (s - 1) * BANK], G[n % 4][:, :]).then_inc(ph.done, 1)
                    else:
                        nc.scalar.activation(work[:, c, GA + (s - 2) * BANK:GA + (s - 1) * BANK], G[n % 4][:, :],
                                             ACT.Sigmoid).then_inc(ph.done, 1)
                if ph is kv:
                    softplus(act, steps, xn[:, 1, 512:512 + 32], xn[:, 1, 544:544 + 32], z_ready, ez_ready, ez1_ready, ln_ready, 1)
            take_root(2 * 2 * HEADS)
            for g in range(16):
                if g % 2:
                    odd_turn(turned, turned_copied, base + g, lambda bank: nc.scalar.mul(
                        hT[0:AUG, 2 * g:2 * g + 2, :], bank[0:AUG, :].rearrange("p (h s) -> p h s", h=2),
                        gains[0:AUG, GC["kq"] + g // 8:GC["kq"] + g // 8 + 1]))
            base += 16

            def attention(att, units, tf, tc, base):
                for u in range(units + 2):
                    if u < units:
                        nk = P * (u % 2 + 1)
                        act.wait_ge(att.max_ready, u + 1)
                        if u >= 4:
                            act.wait_ge(tf, base + u - 3)
                        nc.scalar.activation(xn_all[:, (u % 4) * S:(u % 4) * S + nk], G[u % 4][:, 0:nk], ACT.Exp,
                                             bias=nmax[:, u:u + 1], accum_out=rowsum[:, u:u + 1]).then_inc(att.p_ready, 1)
                    w = u - 2
                    if w >= 0 and w % 2:
                        if w >= 4:
                            act.wait_ge(att.out_full, w - 3)
                        odd_turn(tf, tc, base + w, lambda bank: nc.scalar.copy(
                            xT_all[:, (w % 4) * S:(w % 4 + 1) * S], bank[:, 0:S]))

            attention(att1, 2 * HEADS, turned, turned_copied, base)
            base += 2 * HEADS
            norm_copies(turned, turned_copied, base, [(xT, None)])
            base += 4

            norm(8, [(xT, GC["m"])], turned, turned_copied, base)
            base += 4
            act.wait_ge(gap_diff, 2)
            nc.scalar.activation(gap, gap, ACT.Exp).then_inc(gap_exp, 1)

            def gather_copy(it):
                for half in range(2):
                    act.wait_ge(gather_full, it * 2 + (half + 1))
                    for k in range(4 * half, 4 * half + 4):
                        ins = nc.scalar.mul(xg_hi[:, k * P:(k + 1) * P], G[2 + half][:, (k % 4) * P:(k % 4 + 1) * P],
                                            gains[:, GC["m"] + k:GC["m"] + k + 1])
                ins.then_inc(gathered[0], 1)

            def e_turn(it, what):
                g = TURN_OF[what]
                act.wait_ge(e_turned, it * len(TURNS) + g + 1)
                if what == "route":
                    ins = nc.scalar.copy(routeT, T[1][:, 0:2 * P])
                else:
                    expert_hidden_free(act, it, what)
                    ins = nc.scalar.copy(e_hT_hi[:, what % 2, :], T[g % 2][:, :])
                ins.then_inc(e_turned_hi, 1)

            for n in range(LEAD):
                e_make_hi(act, 0, n)
            gather_copy(0)
            act.wait_ge(rounds_ready, 1)
            rounds = act.value_load(rounds_i[0:1, 0:1], min_val=1, max_val=2)
            with act.Fori(0, rounds * E) as it:
                for m, (kind, s) in enumerate(ORDER):
                    if m == len(ORDER) - 1:
                        e_turn(it, DOWNS - 1)
                        gather_copy(it + 1)
                    for n in (2 * m + LEAD, 2 * m + LEAD + 1):
                        e_make_hi(act, it, n)
                    if kind == "up":
                        act.wait_ge(up_full, it * UPS + s + 1)
                        act.wait_ge(up_read, it * UPS + s + 1)
                        nc.scalar.activation(e_silu[:, s % 2, :], G[s % 2][:, 0:PAIR], ACT.Silu).then_inc(e_silu_ready, 1)
                        if s == 4:
                            e_turn(it, "route")
                        if s % 2 == 0 and s >= 2:
                            e_turn(it, s // 2 - 1)
                act.wait_ge(y_full, it * 2 + 1)
                act.wait_ge(scatter_full, it * 4)
                nc.scalar.copy(y_sb[:, 0:BANK], SM[0][:, :]).then_inc(y_copied[0], 1)

            base = 0
            norm(12, [(xT, GC["pre2"])], turned2, turned2_copied, base)
            act.dma_start(post_gain1, t["g_mix_post_2"].to_broadcast([P, D])).then_inc(post_landed, 16)
            base += 4

            def project(i):
                for j in range(2):
                    for c in range(NT):
                        act.wait_ge(pr.full, i * 4 + (2 * j + c + 1))
                        nc.scalar.copy(work[:, c, bass.ds(i * (2 * BANK) + j * BANK, BANK)], G[2 * j + c][:, :]
                                       ).then_inc(pr.done, 1)

            with act.Fori(0, pr.slabs // 2) as i:
                project(i)
            softplus(act, steps, xn[:, 1, 512:512 + 8], xn[:, 1, 544:544 + 8], z_ready, ez_ready, ez1_ready, ln_ready, 2)
            act.wait_ge(angle_ready, 1)
            nc.scalar.activation(rope[:, 5:7, :], rope[:, 3:5, :], ACT.Sin).then_inc(sines_ready, 1)
            act.wait_ge(pr.done, 2 * pr.slabs)
            for c in range(NT):
                ins = nc.scalar.activation(work[:, c, MO:MO + ML_H * ML_V], work[:, c, MO:MO + ML_H * ML_V], ACT.Sigmoid)
            ins.then_inc(out_gate_ready, 1)
            for g in range(16):
                if g % 2:
                    odd_turn(turned2, turned2_copied, base + g, lambda bank: second_head_copy(nc.scalar.copy, nc.scalar.mul, g, bank))
            base += 16
            attention(att2, 2 * ATT_H, turned2, turned2_copied, base)
            base += 2 * ATT_H
            for u in range(2 * ML_H + 2):
                if u < 2 * ML_H:
                    nk = P * (u % 2 + 1)
                    act.wait_ge(mls.max_ready, u + 1)
                    if u >= 4:
                        act.wait_ge(turned2, base + u - 3)
                    nc.scalar.activation(xn_all[:, (u % 4) * S:(u % 4) * S + nk], G[u % 4][:, 0:nk], ACT.Exp,
                                         bias=nmax[:, u:u + 1])
                    nc.scalar.activation(expm[:, u:u + 1], nmax[:, u:u + 1], ACT.Exp).then_inc(mls.p_ready, 1)
                w = u - 2
                if w >= 0 and w % 2:
                    if w >= 4:
                        act.wait_ge(mls.out_full, w - 3)
                    odd_turn(turned2, turned2_copied, base + w, lambda bank: nc.scalar.copy(
                        xT_all[:, (w % 4) * S:(w % 4 + 1) * S], bank[:, 0:S]))
            base += 2 * ML_H
            take_root(2 * ML_H)
            norm_copies(turned2, turned2_copied, base, [(xT, GC["mix"])])
            base += 4

            def post_norm_squares(full):
                for b in range(4):
                    act.wait_ge(down_full, full + b + 1)
                    nc.scalar.activation(xn[:, b // 2, (b % 2) * BANK:(b % 2 + 1) * BANK], G[b][:, :], ACT.Square,
                                         accum_out=ss4[:, b:b + 1]).then_inc(post_squares, 1)

            post_norm_squares(12)
            take_root(NT)
            act.dma_start(post_gain2, t["g_mlp_post_2"].to_broadcast([P, D])).then_inc(post_landed, 16)

            norm(16, [(xT, GC["mlp2"])], turned2, turned2_copied, base, splits=mu)
            base += 4

            def relu(n, j, c, first):
                act.wait_ge(mu.full, n + 1)
                if not first:
                    act.wait_ge(relu2_ready, n - 1)
                nc.scalar.activation(xn[:, c, 0:BANK], G[2 * j + c][:, :], ACT.Relu).then_inc(mu.done, 1)

            def mlp_slab(i, j, first, last=False):
                if last:
                    down_units(make_high, act, mu, md, 0, 2)
                else:
                    up_units(make_high, act, mu, i + j, 1 - j)
                if not first:
                    for c in range(NT):
                        hidden_high(turned2, i * 4 + (2 * j - 2 + c + base), i * 2 + (j - 1), c, 4)
                for c in range(NT):
                    relu(i * 4 + (2 * j + c), j, c, first)

            mlp_slab(0, 0, True)
            mlp_slab(0, 1, False)
            with act.Fori(1, mu.slabs // 2 - 1) as i:
                for j in range(2):
                    mlp_slab(i, j, False)
            mlp_slab(mu.slabs // 2 - 1, 0, False)
            mlp_slab(mu.slabs // 2 - 1, 1, False, last=True)
            for c in range(NT):
                hidden_high(turned2, 2 * mu.slabs - 2 + c + base, mu.slabs - 1, c, 4)
            down_units(make_high, act, mu, md, 2, md.units)
            post_norm_squares(16)
            take_root(NT)

        @block.tensor
        def _(pe):
            def turn(tf, tc, g, blocks):
                if not isinstance(g, int) or g >= 2:
                    pe.wait_ge(tc[par(g)], half(g))
                at = 0
                for src in blocks:
                    k = src.shape[-1]
                    ins = nc.tensor.transpose(T[par(g)][0:k, at:at + P], src, ident[:, :])
                    at += P
                ins.then_inc(tf, 1)

            def par(g):
                return g % 2 if isinstance(g, int) else g.par

            def half(g):
                return g // 2 if isinstance(g, int) else g.half

            class G_:

                def __init__(self, half, par):
                    self.half, self.par = half, par

            def copied(tc, groups):
                pe.wait_ge(tc[0], (groups + 1) // 2)
                pe.wait_ge(tc[1], groups // 2)

            def norm_turns(tf, tc, base, src):
                for j in range(4):
                    turn(tf, tc, base + j, [src[:, c, k * P:(k + 1) * P] for k in (2 * j, 2 * j + 1) for c in range(NT)])

            def chunks(bank, x, c, w, n):
                for k in range(KD):
                    ins = nc.tensor.matmul(bank[:, 0:n], x[:, k, c * P:(c + 1) * P], w[:, k, :], start=(k == 0), stop=(k == KD - 1))
                return ins

            def use(ph, i, j, c, first, x, n):
                if not first:
                    pe.wait_ge(ph.done, i * 4 + (2 * j + c - 3))
                if c == 0:
                    pe.wait_ge(ph.landed[j], i * (16 * ph.dmas) + 16 * ph.dmas)
                chunks(G[2 * j + c], x, c, cols(ph.slots[j], n), n).then_inc(ph.full, 1)

            def down(ph, lhs, k_per, ready):
                n_k = ph.slabs * k_per
                for s in range(ph.slabs):
                    pe.wait_ge(ph.landed[s % 2], 16 * (s // 2 + 1))
                    w = rows(ph.slots[s % 2], k_per)
                    for kk in range(k_per):
                        k = s * k_per + kk
                        ready(k)
                        for c in range(NT):
                            for b in range(2):
                                ins = nc.tensor.matmul(G[2 * c + b][:, :], lhs(k, c), w[:, kk, b * BANK:(b + 1) * BANK],
                                                       start=(k == 0), stop=(k == n_k - 1))
                                if k == n_k - 1:
                                    ins.then_inc(down_full, 1)
                    if s < ph.slabs - 1:
                        ins.then_inc(ph.used, 1)

            def three_products(bank, x_hi, x_lo, w_hi, w_lo, start, stop):
                nc.tensor.matmul(bank, x_hi, w_hi, start=start, stop=False)
                nc.tensor.matmul(bank, x_hi, w_lo, start=False, stop=False)
                return nc.tensor.matmul(bank, x_lo, w_hi, start=False, stop=stop)

            def split_use(ph, i, j, first, between):
                for part in range(2):
                    q = 2 * j + part
                    pe.wait_ge(dense_lo, i * 4 + (q + 1 + ph.before))
                    for c in range(NT):
                        if part == 0 and not first:
                            pe.wait_ge(ph.done, i * 4 + (2 * j + c - 3))
                        for kk in range(4):
                            k = 4 * part + kk
                            at = slice(kk * ph.width, (kk + 1) * ph.width)
                            ins = three_products(G[2 * j + c][:, 0:ph.width], xT_hi[:, k, c * P:(c + 1) * P],
                                                 xT_lo[:, k, c * P:(c + 1) * P], high_place(q)[:, at],
                                                 unit_place(ph, q, dense_low)[:, at], k == 0, k == KD - 1)
                        if part:
                            ins.then_inc(ph.full, 1)
                    if part == 0:
                        ins.then_inc(ph.half_used, 1)
                        between()

            def split_down(ph, ready):
                for u in range(ph.units):
                    pe.wait_ge(dense_lo, u + 1 + ph.before)
                    w_hi, w_lo = high_place((ph.turned_by + u) % 4), unit_place(ph, u % 4, dense_low)
                    for kk in range(2):
                        k = 2 * u + kk
                        ready(k)
                        for c in range(NT):
                            for b in range(2):
                                at = slice(kk * D + b * BANK, kk * D + (b + 1) * BANK)
                                ins = three_products(G[2 * c + b][:, :], hT_hi[:, k, c * P:(c + 1) * P],
                                                     hT_lo[:, k, c * P:(c + 1) * P], w_hi[:, at], w_lo[:, at],
                                                     k == 0, k == 2 * ph.units - 1)
                                if k == 2 * ph.units - 1:
                                    ins.then_inc(down_full, 1)
                    if u < ph.units - 1:
                        ins.then_inc(ph.used, 1)

            hidden = lambda k, c: hT[:, k, c * P:(c + 1) * P]
            from_xT = lambda k, c: xT[:, k, c * P:(c + 1) * P]
            tf, tc = turned, turned_copied

            pe.wait_ge(consts_ready, 5)
            pe.wait_ge(params_landed, 16 * 18)
            nc.tensor.transpose(T[0][:, 0:74], gain_rows[:, :], ident[0:74, 0:74]).then_inc(turned, 1)
            pe.wait_ge(spatial_ready, 1)
            for g in range(GROUPS):
                bank = T[1] if g < 4 else G[3]
                ins = nc.tensor.transpose(bank[:, (g % 4) * P:(g % 4 + 1) * P], ws_raw[:, g, :], ident[:, :])
            ins.then_inc(turned, 1)
            pe.wait_ge(xn_ready, 2)
            base = 2
            norm_turns(tf, tc, base, xn)
            base += 4
            copied(tc, base)
            nothing = lambda: None
            for j in range(2):
                split_use(av, 0, j, True, nothing)
            with pe.Fori(1, av.slabs // 2) as i:
                for j in range(2):
                    split_use(av, i, j, False, nothing)
            pe.wait_ge(av.done, 2 * av.slabs)

            def gated_turns(s):
                for c in range(NT):
                    m = 2 * s + c
                    pe.wait_ge(gated_ready, m + 1)
                    turn(tf, tc, base + m, [xn[:, c, GDIM + k * P:GDIM + (k + 1) * P] for k in range(GCH)])

            def mix(s):
                if s:
                    gated_turns(s - 1)
                else:
                    pe.wait_ge(spatial_ready, 2)
                for c in range(NT):
                    if s:
                        pe.wait_ge(mixed_read, 2 * s + c - 1)
                    nc.tensor.matmul(SM[c][:, 0:GDIM], work[:, c, A_HALF + s * P:A_HALF + (s + 1) * P],
                                     work[:, c, s * GDIM:(s + 1) * GDIM], start=True, stop=True).then_inc(mixed_full, 1)

            for s in range(au.slabs):
                split_use(au, s // 2, s % 2, s < 2, lambda: mix(s))
            gated_turns(au.slabs - 1)
            pe.wait_ge(au.done, 2 * au.slabs)

            def chunk_ready(base, per, tc):
                def ready(k):
                    if k % per == 0:
                        for c in range(NT):
                            pe.wait_ge(tc[c], base // 2 + k // per + 1)
                return ready

            down(ao, hidden, 4, chunk_ready(base, GCH, tc))
            base += 2 * au.slabs

            pe.wait_ge(xn_ready, 4)
            norm_turns(tf, tc, base, xn)
            base += 4
            copied(tc, base)
            pe.wait_ge(h_ready, 4)

            def hidden_turn(m, g):
                pe.wait_ge(fu.done, m + 1)
                turn(tf, tc, g, [xn[:, par(g), PAIR + k * P:PAIR + (k + 1) * P] for k in range(2)])

            def slab_before(turn_one, i, j, base):
                for c in range(NT):
                    turn_one(i * 4 + (2 * j - 2 + c), G_(i * 2 + (j - 1 + base // 2), c))

            def ffn_body(i, first, base):
                for j in range(2):
                    split_use(fu, i, j, first, lambda: first and j == 0 or slab_before(hidden_turn, i, j, base))

            ffn_body(0, True, base)
            with pe.Fori(1, fu.slabs // 2) as i:
                ffn_body(i, False, base)
            split_use(fu, fu.slabs // 2, 0, False, lambda: slab_before(hidden_turn, fu.slabs // 2, 0, base))
            pe.wait_ge(fu.done, 2 * fu.slabs)
            slab_before(hidden_turn, fu.slabs // 2, 1, base)
            split_down(fo, chunk_ready(base, 2, tc))
            base += 2 * fu.slabs

            pe.wait_ge(xn_ready, 6)
            norm_turns(tf, tc, base, xn)
            base += 4
            copied(tc, base)
            pe.wait_ge(h_ready, 8)
            for ph, x in ((kv, xT), (qg, xT2)):
                if ph is qg:
                    pe.wait_ge(kv.done, 2 * kv.slabs)
                for s in range(ph.slabs):
                    for c in range(NT):
                        use(ph, s // 2, s % 2, c, s < 2, x, BANK)
                if ph is kv:
                    for c in range(NT):
                        ins = chunks(SM[0][:, c * HEADS:(c + 1) * HEADS], xT, c, w_forget, HEADS)
                    ins.then_inc(small_full, 1)
            pe.wait_ge(logf_ready, 1)
            running_sums(pe, xn[:, 1, 576:576 + 32].rearrange("p (c n) -> p c n", c=NT), HEADS).then_inc(small_full, 1)
            pe.wait_ge(aug_ready, 1)
            for g in range(16):
                at = (KA if g < 8 else QA) + 2 * (g % 8) * AUG
                turn(tf, tc, base + g, [work[:, c, at + e * AUG:at + (e + 1) * AUG] for e in range(2) for c in range(NT)])
            base += 16
            copied(tc, base)
            pe.wait_ge(qg.done, 2 * qg.slabs)

            def attention(att, units, qT, kT, v, width, tf, tc, base, extra=None):
                for u in range(units + 3):
                    if u < units:
                        hd, q = u // 2, u % 2
                        nk = P * (q + 1)
                        if u >= 4:
                            pe.wait_ge(att.p_ready if extra is None else weights_ready, u - 3)
                        if extra is None:
                            nc.tensor.matmul(G[u % 4][:, 0:nk], qT(hd)[:, q * P:(q + 1) * P], kT(hd)[:, 0:nk],
                                             start=True, stop=True).then_inc(att.full, 1)
                        else:
                            extra(u, hd, q, nk).then_inc(att.full, 1)
                    w = u - 2
                    if 0 <= w < units:
                        pe.wait_ge(att.p_ready if extra is None else weights_ready, w + 1)
                        turn(tf, tc, base + w, [xn_all[:, (w % 4) * S + k * P:(w % 4) * S + (k + 1) * P]
                                                for k in range(w % 2 + 1)])
                    w = u - 3
                    if 0 <= w < units:
                        g = base + w
                        pe.wait_ge(tc[g % 2], g // 2 + 1)
                        if w >= 2:
                            pe.wait_ge(att.out_done, w - 1)
                        for k in range(w % 2 + 1):
                            ins = nc.tensor.matmul(SM[w % 2][:, 0:width], xT_all[:, (w % 4) * S + k * P:(w % 4) * S + (k + 1) * P],
                                                   v(w // 2, k), start=(k == 0), stop=(k == w % 2))
                        ins.then_inc(att.out_full, 1)

            attention(att1, 2 * HEADS, lambda hd: hT[0:AUG, HEADS + hd, :], lambda hd: hT[0:AUG, hd, :],
                      lambda hd, k: work[:, k, VA + hd * HD:VA + (hd + 1) * HD], HD, tf, tc, base)
            base += 2 * HEADS
            pe.wait_ge(att1.out_done, 2 * HEADS)
            norm_turns(tf, tc, base, work[:, :, GA:GA + D])
            base += 4
            copied(tc, base)
            down(bo, from_xT, 4, lambda k: None)

            pe.wait_ge(xn_ready, 8)
            norm_turns(tf, tc, base, xn)
            base += 4
            copied(tc, base)
            for c in range(NT):
                ins = chunks(SM[0][:, c * E:(c + 1) * E], xT, c, w_router, E)
            ins.then_inc(small_full, 1)
            pe.wait_ge(mask_ready, 1)
            running_sums(pe, sel, E)
            nc.tensor.matmul(SM[1][:, 2 * E:3 * E], ones[:, :], sel[:, 0, :], start=True, stop=False)
            nc.tensor.matmul(SM[1][:, 2 * E:3 * E], ones[:, :], sel[:, 1, :], start=False, stop=True).then_inc(small_full, 1)

            def gather(it):
                pe.wait_ge(pick_ready, it + 1)
                for k in range(KD):
                    for c in range(NT):
                        ins = nc.tensor.matmul(G[2 + k // 4][:, (k % 4) * P:(k % 4 + 1) * P], xn[:, c, k * P:(k + 1) * P],
                                               pick[:, c, :], start=(c == 0), stop=(c == NT - 1))
                    if k % 4 == 3:
                        ins.then_inc(gather_full, 1)

            def scatter(added, added_before, full, tiles):
                for c in tiles:
                    for b in range(2):
                        if c:
                            pe.wait_ge(added, added_before + b + 1)
                        ins = nc.tensor.matmul(G[2 + b][:, :], routeT[:, c * P:(c + 1) * P], y_sb[:, b * BANK:(b + 1) * BANK],
                                               start=True, stop=True)
                        ins.then_inc(full, 1)

            def e_turn(it, what):
                g = TURN_OF[what]
                if what == "route":
                    pe.wait_ge(route_ready, it + 1)
                    blocks = [route[:, c, :] for c in range(NT)]
                else:
                    pe.wait_ge(up_read, it * UPS + 2 * what + 4)
                    blocks = [e_hid[:, b, k * P:(k + 1) * P] for b in range(2) for k in range(2)]
                if g == 3:
                    pe.wait_ge(e_turned_hi, it * len(TURNS) + 2)
                else:
                    pe.wait_ge(e_turned_lo, it * DOWNS + (0 if g < 2 else 1 if g == 2 else g - 2))
                for n, src in enumerate(blocks):
                    ins = nc.tensor.transpose(T[g % 2][:, n * P:(n + 1) * P], src, ident[:, :])
                ins.then_inc(e_turned, 1)

            gather(0)
            pe.wait_ge(rounds_ready, 1)
            rounds = pe.value_load(rounds_i[0:1, 0:1], min_val=1, max_val=2)
            with pe.Fori(0, rounds * E) as it:
                for q in range(2):
                    pe.wait_ge(gathered[q], it + 1)
                for m, (kind, s) in enumerate(ORDER):
                    if kind == "up":
                        pe.wait_ge(up_read, it * UPS + s + 1)
                        for part in range(2):
                            n = 2 * m + part
                            pe.wait_ge(e_lo, it * UNITS + (n + 1))
                            for kk in range(4):
                                k = 4 * part + kk
                                at = slice(kk * BANK, (kk + 1) * BANK)
                                ins = three_products(G[s % 2][:, :], xg_hi[:, k * P:(k + 1) * P], xg_lo[:, k * P:(k + 1) * P],
                                                     e_hi_unit(n)[:, at], e_raw(n, e_low)[:, at], k == 0, k == KD - 1)
                            ins.then_inc(up_full if part else up_half_used, 1)
                        if s == 1:
                            for b in range(2):
                                pe.wait_ge(y_copied[b], it + 1)
                            scatter(scatter_added, it * 4, scatter_full, [0])
                        if s == 2:
                            scatter(scatter_added, it * 4, scatter_full, [1])
                        if s == 4:
                            e_turn(it, "route")
                        if s % 2 == 0 and s >= 2:
                            e_turn(it, s // 2 - 1)
                    else:
                        if s == DOWNS - 1:
                            e_turn(it, DOWNS - 1)
                            pe.wait_ge(scatter_added, it * 4 + 4)
                            gather(it + 1)
                            pe.wait_ge(e_turned_hi, it * len(TURNS) + (TURN_OF["route"] + 1))
                        pe.wait_ge(e_turned_lo, it * DOWNS + (s + 1))
                        for part in range(2):
                            n = 2 * m + part
                            final = s == DOWNS - 1 and part == 1
                            pe.wait_ge(e_lo, it * UNITS + (n + 1))
                            for kk in range(2):
                                k = 2 * part + kk
                                for b in range(2):
                                    at = slice(kk * D + b * BANK, kk * D + (b + 1) * BANK)
                                    ins = three_products(SM[b][:, :], e_hT_hi[:, s % 2, k * P:(k + 1) * P],
                                                         e_hT_lo[:, s % 2, k * P:(k + 1) * P], e_hi_unit(n)[:, at],
                                                         e_raw(n, e_low)[:, at], s == 0 and k == 0, final and kk == 1)
                                    if final and kk == 1:
                                        ins.then_inc(y_full, 1)
                            if not final:
                                ins.then_inc(down_used, 1)
            for b in range(2):
                pe.wait_ge(y_copied[b], rounds * E + 1)
                pe.wait_ge(gathered[b], rounds * E + 1)
            scatter(h_ready, 12, last_scatter, range(NT))

            tf, tc = turned2, turned2_copied
            base = 0
            pe.wait_ge(e_turned_lo, rounds * (E * DOWNS))
            pe.wait_ge(xn_ready, 10)
            norm_turns(tf, tc, base, xn)
            base += 4
            copied(tc, base)
            for j in range(2):
                for c in range(NT):
                    use(pr, 0, j, c, True, xT, BANK)
            with pe.Fori(1, pr.slabs // 2) as i:
                for j in range(2):
                    for c in range(NT):
                        use(pr, i, j, c, False, xT, BANK)
            for c in range(NT):
                ins = chunks(SM[0][:, c * 2 * ML_H:(c + 1) * 2 * ML_H], xT, c, w_if, 2 * ML_H)
            ins.then_inc(small_full, 1)
            pe.wait_ge(logf_ready, 2)
            running_sums(pe, xn[:, 1, 576:576 + 8].rearrange("p (c n) -> p c n", c=NT), ML_H).then_inc(small_full, 1)
            pe.wait_ge(aug_ready, 2)
            pe.wait_ge(pr.done, 2 * pr.slabs)
            for g in range(16):
                if g < 12:
                    at = g * 2 * HD if g < 8 else MQ + (g - 8) * 2 * HD
                    blocks = [work[:, c, at + e * HD:at + (e + 1) * HD] for e in range(2) for c in range(NT)]
                else:
                    at = 640 + 2 * (2 * (g - 12))
                    blocks = [xn[:, 1, at + 2 * e + 16 * c:at + 2 * e + 16 * c + 2] for e in range(2) for c in range(NT)]
                turn(tf, tc, base + g, blocks)
            base += 16
            copied(tc, base)
            attention(att2, 2 * ATT_H, lambda hd: hT[0:HD, hd, :], lambda hd: hT[0:HD, ATT_H + hd, :],
                      lambda hd, k: work[:, k, V2 + hd * HD:V2 + (hd + 1) * HD], HD, tf, tc, base)
            base += 2 * ATT_H
            pe.wait_ge(att2.out_done, 2 * ATT_H)

            def mlstm_scores(u, hd, q, nk):
                nc.tensor.matmul(G[u % 4][:, 0:nk], hT[0:2, 24 + hd, q * P:(q + 1) * P], hT[0:2, 28 + hd, 0:nk],
                                 start=True, stop=True)
                return nc.tensor.matmul(G[u % 4][:, S:S + nk], hT[0:HD, 16 + hd, q * P:(q + 1) * P],
                                        hT[0:HD, 20 + hd, 0:nk], start=True, stop=True)

            attention(mls, 2 * ML_H, None, None, lambda hd, k: work[:, k, MV + hd * ML_V:MV + (hd + 1) * ML_V],
                      ML_V, tf, tc, base, extra=mlstm_scores)
            base += 2 * ML_H
            pe.wait_ge(hm_ready, 2 * ML_H)
            norm_turns(tf, tc, base, work[:, :, 0:D])
            base += 4
            copied(tc, base)
            down(po, from_xT, 4, lambda k: None)

            pe.wait_ge(xn_ready, 12)
            norm_turns(tf, tc, base, xn)
            base += 4
            copied(tc, base)
            pe.wait_ge(h_ready, 20)

            def squared_turn(m, g):
                pe.wait_ge(relu2_ready, m + 1)
                turn(tf, tc, g, [xn[:, par(g), BANK + k * P:BANK + (k + 1) * P] for k in range(4)])

            def mlp_body(i, first, base):
                for j in range(2):
                    split_use(mu, i, j, first, lambda: first and j == 0 or slab_before(squared_turn, i, j, base))

            mlp_body(0, True, base)
            with pe.Fori(1, mu.slabs // 2) as i:
                mlp_body(i, False, base)
            slab_before(squared_turn, mu.slabs // 2, 0, base)
            pe.wait_ge(mu.done, 2 * mu.slabs)
            split_down(md, chunk_ready(base, 4, tc))

        @block.vector
        def _(dve):
            V = nc.vector
            steps = Steps(dve, vector_step)
            roots = [0]
            tf, tc = turned, turned_copied

            def even_turn(tf, tc, g, copy):
                dve.wait_ge(tf, g + 1)
                copy(T[0]).then_inc(tc[0], 1)

            def norm_copies(tf, tc, base, outs):
                for j in (0, 2):
                    def copy(bank, j=j):
                        for dst, gc in outs:
                            for k in (2 * j, 2 * j + 1):
                                src = bank[:, (k % 2) * S:(k % 2 + 1) * S]
                                if gc is None:
                                    ins = V.tensor_copy(dst[:, k, :], src)
                                else:
                                    ins = V.tensor_scalar(dst[:, k, :], src, gains[:, gc + k:gc + k + 1], None, ALU.mult)
                        return ins
                    even_turn(tf, tc, base + j, copy)

            def inverse_rms(dst, src, n):
                w = src.shape[-1]
                roots[0] += 1
                V.tensor_scalar(variance[:, 0:w], src, 1.0 / n, EPS, ALU.mult, ALU.add).then_inc(variance_ready, 1)
                dve.wait_ge(root_ready, roots[0])
                steps.then(V.reciprocal(dst, root[:, 0:w]))
                c = correction[:, 0:w]
                steps.then(V.tensor_tensor(c, dst, dst, ALU.mult))
                steps.then(V.tensor_tensor(c, c, variance[:, 0:w], ALU.mult))
                steps.then(V.tensor_scalar(c, c, -0.5, 1.5, ALU.mult, ALU.add))
                steps.then(V.tensor_tensor(dst, dst, c, ALU.mult))

            high_parts = [0]

            def norm(nth, tf, tc, base, outs, splits=None):
                dve.wait_ge(squares_ready, 2 * nth)
                inverse_rms(rstd, ss, D)
                for c in range(NT):
                    V.tensor_scalar(xn[:, c, :], h[:, c, :], rstd[:, c:c + 1], None, ALU.mult).then_inc(xn_ready, 1)
                if splits is None:
                    norm_copies(tf, tc, base, outs)
                    return
                up_units(make_low, dve, splits, 0, 0)
                (_, gc), = outs
                for j in range(4):
                    dve.wait_ge(split_copied, high_parts[0] + j + 1)
                    for k in (2 * j, 2 * j + 1):
                        ins = V.scalar_tensor_tensor(out=xT_lo[:, k, :], in0=T[j % 2][:, (k % 2) * S:(k % 2 + 1) * S],
                                                     scalar=gains[:, gc + k:gc + k + 1], in1=xT_hi[:, k, :].bitcast(F32),
                                                     op0=ALU.mult, op1=ALU.subtract)
                    ins.then_inc(tc[j % 2], 1)
                high_parts[0] += 4

            def hidden_low(tc, m, s, par, per):
                dve.wait_ge(split_copied, m + (high_parts[0] + 1))
                at = (bass.ds(s * per, per), slice(par * P, (par + 1) * P))
                V.tensor_tensor(hT_lo[:, at[0], at[1]], T[par][:, 0:per * P].rearrange("p (k s) -> p k s", k=per),
                                hT_hi[:, at[0], at[1]].bitcast(F32), ALU.subtract).then_inc(tc[par], 1)

            def add_down(full):
                for b in range(4):
                    dve.wait_ge(down_full, full + b + 1)
                    dst = h[:, b // 2, (b % 2) * BANK:(b % 2 + 1) * BANK]
                    V.tensor_tensor(dst, dst, G[b][:, :], ALU.add).then_inc(h_ready, 1)

            V.memset(gain_rows[:, :], 1.0).then_inc(gain_rows_ready, 1)
            dve.wait_ge(spatial_landed, 16)
            V.memset(ws_raw[0:64, :, 64:128], 0.0).then_inc(spatial_ready, 1)
            dve.wait_ge(turned, 1)
            steps.then(V.tensor_copy(gains[:, :], T[0][:, 0:74]))
            V.tensor_scalar(gains[0:HD, GC["kq"] + 1:GC["kq"] + 2], gains[0:HD, GC["kq"] + 1:GC["kq"] + 2], HD ** -0.5, None,
                            ALU.mult).then_inc(tc[0], 1)
            base = 2
            dve.wait_ge(tc[0], 1)
            norm(1, tf, tc, base, [(xT, GC["a"])], splits=av)
            base += 4

            for n in range(2 * av.slabs):
                s, c = n // 2, n % 2
                if c == 0:
                    if s < av.slabs - 1:
                        up_units(make_low, dve, av, (s + 1) // 2, (s + 1) % 2)
                    else:
                        up_units(make_low, dve, au, 0, 0)
                dve.wait_ge(av.done, n + 1)
                if n >= 2:
                    dve.wait_ge(v_squared, n - 1)
                v = work[:, c, s * GDIM:(s + 1) * GDIM]
                V.tensor_tensor_reduce(out=xn[:, c, GDIM:2 * GDIM], in0=v, in1=v, scale=1.0, scalar=0.0, op0=ALU.mult,
                                       op1=ALU.add, accum_out=vss[:, c * GROUPS + s:c * GROUPS + s + 1]).then_inc(v_squared, 1)
            dve.wait_ge(v_squared, 2 * av.slabs)
            dve.wait_ge(tc[1], 1)
            for c in range(NT):
                steps.then(V.tensor_reduce(ss[:, c:c + 1], vss[:, c * GROUPS:(c + 1) * GROUPS], AX_X, ALU.add))
            inverse_rms(rstd, ss, A_HALF)
            for c in range(NT):
                ins = V.tensor_scalar(work[:, c, A_HALF:A_HALF + GROUPS * P], wsT, rstd[:, c:c + 1], None, ALU.mult)
            ins.then_inc(spatial_ready, 1)
            def gated_even(s):
                even_turn(tf, tc, base + 2 * s, lambda bank: V.tensor_copy(
                    hT[:, GCH * s:GCH * (s + 1), 0:P], bank[:, 0:GDIM].rearrange("p (k s) -> p k s", k=GCH)))

            for s in range(au.slabs):
                if s < au.slabs - 1:
                    up_units(make_low, dve, au, (s + 1) // 2, (s + 1) % 2)
                if s:
                    gated_even(s - 1)
                at = unit_place(au, 2 * (s % 2), dense_raw)[:, 4 * GDIM:5 * GDIM]
                for c in range(NT):
                    n = 2 * s + c
                    dve.wait_ge(au.landed[2 * (s % 2)], 32 * (s // 2 + 1))
                    dve.wait_ge(mixed_full, n + 1)
                    if n >= 2:
                        dve.wait_ge(tf, base + n - 1)
                    mixed = xn[:, c, GDIM:2 * GDIM]
                    V.tensor_tensor(mixed, SM[c][:, 0:GDIM], at, ALU.mult).then_inc(mixed_read, 1)
                    dve.wait_ge(mixed_read, n + 1)
                    dve.wait_ge(au.done, n + 1)
                    V.scalar_tensor_tensor(out=mixed, in0=mixed, scalar=gains[:, GC["bs"] + s:GC["bs"] + s + 1],
                                           in1=xn[:, c, 0:GDIM], op0=ALU.add, op1=ALU.mult).then_inc(gated_ready, 1)
            gated_even(au.slabs - 1)
            base += 2 * au.slabs
            add_down(0)

            norm(2, tf, tc, base, [(xT, GC["f"])], splits=fu)
            base += 4

            def gated(n, j, c, first, turned_before):
                dve.wait_ge(silu_ready, n + 1)
                if not first:
                    dve.wait_ge(tf, turned_before)
                V.tensor_tensor(xn[:, c, PAIR:2 * PAIR], xn[:, c, 0:PAIR], G[2 * j + c][:, PAIR:2 * PAIR], ALU.mult
                                ).then_inc(fu.done, 1)

            def ffn_slab(i, j, first, last=False):
                if last:
                    down_units(make_low, dve, fu, fo, 0, 2)
                else:
                    up_units(make_low, dve, fu, i + j, 1 - j)
                for c in range(NT):
                    if not first:
                        hidden_low(tc, i * 4 + (2 * j - 2 + c), i * 2 + (j - 1), c, 2)
                for c in range(NT):
                    gated(i * 4 + (2 * j + c), j, c, first, i * 4 + (2 * j + c - 1 + base))

            ffn_slab(0, 0, True)
            ffn_slab(0, 1, False)
            with dve.Fori(1, fu.slabs // 2) as i:
                for j in range(2):
                    ffn_slab(i, j, False)
            ffn_slab(fu.slabs // 2, 0, False, last=True)
            for c in range(NT):
                hidden_low(tc, 2 * fu.slabs - 2 + c, fu.slabs - 1, c, 2)
            base += 2 * fu.slabs
            high_parts[0] += 2 * fu.slabs
            down_units(make_low, dve, fu, fo, 2, fo.units)
            add_down(4)

            norm(3, tf, tc, base, [(xT, GC["kv"]), (xT2, GC["b"])])
            base += 4
            heads = lambda c, at: work[:, c, at:at + HEADS * AUG].rearrange("p (h e) -> p h e", e=AUG)
            z = xn[:, 1, 512:544].rearrange("p (c n) -> p c n", c=NT)
            soft = xn[:, 1, 544:576].rearrange("p (c n) -> p c n", c=NT)
            logf = xn[:, 1, 576:608].rearrange("p (c n) -> p c n", c=NT)
            dve.wait_ge(tf, base)
            for which, (ph, at) in enumerate(((kv, KA), (qg, QA))):
                for c in range(NT):
                    V.memset(heads(c, at)[:, :, HD + 1 - which:HD + 2 - which], 1.0)
                for n in range(4):
                    s, c = n // 2, n % 2
                    dve.wait_ge(ph.done, n + 1)
                    x = heads(c, at)[:, 8 * s:8 * (s + 1), 0:HD]
                    sq = xn[:, 0, 0:BANK].rearrange("p (h e) -> p h e", e=HD)
                    steps.then(V.tensor_tensor(sq, x, x, ALU.mult))
                    steps.then(V.tensor_reduce(head_ss[:, c * 32 + which * 16 + 8 * s:c * 32 + which * 16 + 8 * (s + 1)],
                                               sq, AX_X, ALU.add))
                if which == 0:
                    dve.wait_ge(small_full, 1)
                    for c in range(NT):
                        ins = V.tensor_tensor(z[:, c, :], SM[0][:, c * HEADS:(c + 1) * HEADS], b_forget[:, :], ALU.add)
                    ins.then_inc(z_ready, 1)
                    log_sigmoid(dve, V, steps, xn[:, 1, 512:544], xn[:, 1, 544:576], xn[:, 1, 576:608],
                                ez_ready, ez1_ready, ln_ready, logf_ready, 1, z_ready)
            inverse_rms(head_ss, head_ss, HD)
            for which, at in enumerate((KA, QA)):
                for c in range(NT):
                    x = heads(c, at)[:, :, 0:HD]
                    r = head_ss[:, c * 32 + which * 16:c * 32 + (which + 1) * 16]
                    V.tensor_tensor(x, x, r.rearrange("p (h e) -> p h e", e=1).to_broadcast([P, HEADS, HD]), ALU.mult)
            dve.wait_ge(small_full, 2)
            for c in range(NT):
                cum = SM[1][:, c * HEADS:(c + 1) * HEADS].rearrange("p (h e) -> p h e", e=1)
                V.tensor_scalar(heads(c, KA)[:, :, HD:HD + 1], cum, -1.0, None, ALU.mult)
                ins = V.tensor_copy(heads(c, QA)[:, :, HD + 1:HD + 2], cum)
            ins.then_inc(aug_ready, 1)
            for g in range(0, 16, 2):
                even_turn(tf, tc, base + g, lambda bank: V.tensor_scalar(
                    hT[0:AUG, 2 * g:2 * g + 2, :], bank[0:AUG, :].rearrange("p (h s) -> p h s", h=2),
                    gains[0:AUG, GC["kq"] + g // 8:GC["kq"] + g // 8 + 1], None, ALU.mult))
            base += 16

            def attention(att, units, dst, gate_of, tf, tc, base):
                for u in range(units + 3):
                    if u < units:
                        q = u % 2
                        nk = P * (q + 1)
                        dve.wait_ge(att.full, u + 1)
                        steps.then(V.tensor_tensor_reduce(out=G[u % 4][:, 0:nk], in0=G[u % 4][:, 0:nk], in1=causal[:, P * (1 - q):S],
                                                          scale=1.0, scalar=MASKED, op0=ALU.add, op1=ALU.max,
                                                          accum_out=rmax[:, u:u + 1]))
                        V.tensor_scalar(nmax[:, u:u + 1], rmax[:, u:u + 1], -1.0, None, ALU.mult).then_inc(att.max_ready, 1)
                    w = u - 2
                    if 0 <= w < units and w % 2 == 0:
                        if w >= 4:
                            dve.wait_ge(att.out_full, w - 3)
                        even_turn(tf, tc, base + w, lambda bank: V.tensor_copy(xT_all[:, (w % 4) * S:(w % 4) * S + P], bank[:, 0:P]))
                    w = u - 3
                    if 0 <= w < units:
                        hd, q = w // 2, w % 2
                        dve.wait_ge(att.p_ready, w + 1)
                        steps.then(V.reciprocal(rinv[:, w:w + 1], rowsum[:, w:w + 1]))
                        dve.wait_ge(att.out_full, w + 1)
                        if gate_of is None:
                            V.tensor_scalar(dst(hd, q), SM[q][:, 0:HD], rinv[:, w:w + 1], None, ALU.mult).then_inc(att.out_done, 1)
                        else:
                            V.scalar_tensor_tensor(out=dst(hd, q), in0=SM[q][:, 0:HD], scalar=rinv[:, w:w + 1],
                                                   in1=gate_of(hd, q), op0=ALU.mult, op1=ALU.mult).then_inc(att.out_done, 1)

            gated_out = lambda hd, q: work[:, q, GA + hd * HD:GA + (hd + 1) * HD]
            dve.wait_ge(qg.done, 2 * qg.slabs)
            attention(att1, 2 * HEADS, gated_out, gated_out, tf, tc, base)
            base += 2 * HEADS
            norm_copies(tf, tc, base, [(xT, None)])
            base += 4
            add_down(8)

            norm(4, tf, tc, base, [(xT, GC["m"])])
            base += 4
            for c in range(NT):
                steps.then(V.memset(rank[:, c, 2 * E:COLS], -1000.0))
            V.memset(y_sb, 0.0).then_inc(y_copied[0], 1)
            V.memset(routeT, 0.0).then_inc(y_copied[1], 1)
            dve.wait_ge(small_full, 3)
            steps.then(V.tensor_copy(routing[:, 0:2 * E], SM[0][:, 0:2 * E]))
            for c in range(NT):
                steps.then(V.max(top8[:, c, :], logit[:, c, :]))
                steps.then(V.max_index(indices[:, c, :], top8[:, c, :], logit[:, c, :]))
                steps.then(V.tensor_copy(topi[:, c, :], indices[:, c, :]))
                V.tensor_tensor(gap[:, c:c + 1], top8[:, c, 1:2], top8[:, c, 0:1], ALU.subtract).then_inc(gap_diff, 1)
            dve.wait_ge(gap_exp, 1)
            steps.then(V.tensor_scalar(g1, gap, 1.0, None, ALU.add))
            steps.then(V.reciprocal(g1, g1))
            steps.then(V.tensor_tensor(g2, gap, g1, ALU.mult))
            for c in range(NT):
                steps.then(V.tensor_scalar(sel[:, c, :], iota[:, 0:E], topi[:, c, 0:1], None, ALU.is_equal))
                steps.then(V.tensor_scalar(tmp8, iota[:, 0:E], topi[:, c, 1:2], None, ALU.is_equal))
                steps.then(V.tensor_scalar(gate[:, c, 0:E], sel[:, c, :], g1[:, c:c + 1], None, ALU.mult))
                steps.then(V.scalar_tensor_tensor(out=gate[:, c, 0:E], in0=tmp8, scalar=g2[:, c:c + 1], in1=gate[:, c, 0:E],
                                                  op0=ALU.mult, op1=ALU.add))
                steps.then(V.tensor_tensor(sel[:, c, :], sel[:, c, :], tmp8, ALU.add))
                steps.then(V.tensor_copy(gate[:, c, E:2 * E], gate[:, c, 0:E]))
            V.memset(gate[:, :, 2 * E:COLS], 0.0).then_inc(mask_ready, 1)
            dve.wait_ge(small_full, 4)
            for c in range(NT):
                steps.then(V.tensor_tensor(rank[:, c, 0:E], sel[:, c, :], SM[1][:, c * E:(c + 1) * E], ALU.mult))
                steps.then(V.tensor_scalar(rank[:, c, 0:E], rank[:, c, 0:E], -1.0, None, ALU.add))
                steps.then(V.tensor_scalar(rank[:, c, E:2 * E], rank[:, c, 0:E], float(-P), None, ALU.add))
            steps.then(V.tensor_reduce(total, SM[1][:, 2 * E:3 * E], AX_X, ALU.max))
            steps.then(V.tensor_scalar(roundsf, total, float(P), 1.0, ALU.is_gt, ALU.add))
            steps.then(V.tensor_copy(rounds_i[:, 0:1], roundsf))
            steps.then(V.tensor_scalar(roundsf, roundsf, float(E), -1.0, ALU.mult, ALU.add))
            V.tensor_copy(rounds_i[:, 1:2], roundsf).then_inc(rounds_ready, 1)

            def make_pick(it):
                for c in range(NT):
                    ins = V.tensor_scalar(pick[:, c, :], iota[:, :], rank[:, c, bass.ds(it, 1)], None, ALU.is_equal)
                ins.then_inc(pick_ready, 1)

            def make_route(it):
                for c in range(NT):
                    ins = V.tensor_scalar(route[:, c, :], iota[:, :], rank[:, c, bass.ds(it, 1)],
                                          gate[:, c, bass.ds(it, 1)], ALU.is_equal, ALU.mult)
                ins.then_inc(route_ready, 1)

            def gather_copy(it):
                dve.wait_ge(gathered[0], it + 1)
                for k in range(KD):
                    ins = V.scalar_tensor_tensor(out=xg_lo[:, k * P:(k + 1) * P], in0=G[2 + k // 4][:, (k % 4) * P:(k % 4 + 1) * P],
                                                 scalar=gains[:, GC["m"] + k:GC["m"] + k + 1],
                                                 in1=xg_hi[:, k * P:(k + 1) * P].bitcast(F32), op0=ALU.mult, op1=ALU.subtract)
                ins.then_inc(gathered[1], 1)

            def e_turn(it, p):
                g = TURN_OF[p]
                dve.wait_ge(e_turned_hi, it * len(TURNS) + g + 1)
                expert_hidden_free(dve, it, p)
                V.tensor_tensor(e_hT_lo[:, p % 2, :], T[g % 2][:, :], e_hT_hi[:, p % 2, :].bitcast(F32), ALU.subtract
                                ).then_inc(e_turned_lo, 1)

            make_pick(0)
            for n in range(LEAD):
                e_make_lo(dve, 0, n)
            gather_copy(0)
            dve.wait_ge(rounds_ready, 1)
            rounds = dve.value_load(rounds_i[0:1, 0:1], min_val=1, max_val=2)
            V.memset(tmp8, 0.0).then_inc(up_read, 2)
            with dve.Fori(0, rounds * E) as it:
                make_route(it)
                for m, (kind, s) in enumerate(ORDER):
                    if m == len(ORDER) - 1:
                        e_turn(it, DOWNS - 1)
                        gather_copy(it + 1)
                    for n in (2 * m + LEAD, 2 * m + LEAD + 1):
                        e_make_lo(dve, it, n)
                    if kind == "down":
                        continue
                    dve.wait_ge(e_silu_ready, it * UPS + s + 1)
                    if s >= 2:
                        dve.wait_ge(e_turned, it * len(TURNS) + TURN_OF[s // 2 - 1] + 1)
                    else:
                        dve.wait_ge(e_turned, it * len(TURNS))
                    V.tensor_tensor(e_hid[:, s % 2, :], e_silu[:, s % 2, :], G[s % 2][:, PAIR:2 * PAIR], ALU.mult
                                    ).then_inc(up_read, 1)
                    if s in (1, 2):
                        for b in range(2):
                            dve.wait_ge(scatter_full, it * 4 + 2 * (s - 1) + b + 1)
                            dst = h[:, s - 1, b * BANK:(b + 1) * BANK]
                            V.tensor_tensor(dst, dst, G[2 + b][:, :], ALU.add).then_inc(scatter_added, 1)
                    if s == 3:
                        make_pick(it + 1)
                    if s % 2 == 0 and s >= 2:
                        e_turn(it, s // 2 - 1)
                dve.wait_ge(y_full, it * 2 + 2)
                dve.wait_ge(scatter_full, it * 4 + 4)
                V.tensor_copy(y_sb[:, BANK:2 * BANK], SM[1][:, :]).then_inc(y_copied[1], 1)
            for c in range(NT):
                for b in range(2):
                    dve.wait_ge(last_scatter, 2 * c + b + 1)
                    dst = h[:, c, b * BANK:(b + 1) * BANK]
                    V.tensor_tensor(dst, dst, G[2 + b][:, :], ALU.add).then_inc(h_ready, 1)

            tf, tc = turned2, turned2_copied
            base = 0
            flat = lambda n: rope[:, n, :]
            steps.then(V.tensor_copy(tokf, pos_i[:, :]))
            for c in range(NT):
                steps.then(V.tensor_scalar(rope[:, 1, c * ROPE_HALF:(c + 1) * ROPE_HALF], rope[:, 0, 0:ROPE_HALF],
                                           tokf[:, c:c + 1], None, ALU.mult))
            steps.then(V.tensor_scalar(flat(2), flat(1), 1.0 / (2 * math.pi), None, ALU.mult))
            steps.then(V.tensor_copy(turn_i[:, :], flat(2)))
            steps.then(V.tensor_copy(flat(2), turn_i[:, :]))
            c1 = 6.28125
            c2 = float(np.float32(round((2 * math.pi - c1) * 2 ** 20) / 2 ** 20))
            c3 = 2 * math.pi - c1 - c2
            steps.then(V.tensor_copy(flat(3), flat(1)))
            for part in (c1, c2, c3):
                steps.then(V.scalar_tensor_tensor(out=flat(3), in0=flat(2), scalar=-part, in1=flat(3), op0=ALU.mult, op1=ALU.add))
            steps.then(V.tensor_scalar(flat(3), flat(3), 3.1415925, -3.1415925, ALU.min, ALU.max))
            steps.then(V.tensor_scalar(flat(4), flat(3), -1.0, None, ALU.mult))
            steps.then(V.tensor_tensor(flat(4), flat(4), flat(3), ALU.min))
            V.tensor_scalar(flat(4), flat(4), math.pi / 2, None, ALU.add).then_inc(angle_ready, 1)

            norm(5, tf, tc, base, [(xT, GC["pre2"])])
            base += 4
            dve.wait_ge(tf, base)
            dve.wait_ge(small_full, 5)
            z2 = xn[:, 1, 512:520].rearrange("p (c n) -> p c n", c=NT)
            gi = xn[:, 1, 608:616].rearrange("p (c n) -> p c n", c=NT)
            for c in range(NT):
                V.tensor_tensor(gi[:, c, :], SM[0][:, 2 * ML_H * c:2 * ML_H * c + ML_H], b_if[:, 0:ML_H], ALU.add)
                ins = V.tensor_tensor(z2[:, c, :], SM[0][:, 2 * ML_H * c + ML_H:2 * ML_H * (c + 1)], b_if[:, ML_H:2 * ML_H], ALU.add)
            ins.then_inc(z_ready, 1)
            log_sigmoid(dve, V, steps, xn[:, 1, 512:520], xn[:, 1, 544:552], xn[:, 1, 576:584],
                        ez_ready, ez1_ready, ln_ready, logf_ready, 2, z_ready)
            dve.wait_ge(pr.done, 8)
            dve.wait_ge(sines_ready, 1)
            tmp = [xn[:, 0, n * P:(n + 1) * P].rearrange("p (h e) -> p h e", e=ROPE_HALF) for n in range(4)]
            for c in range(NT):
                qk = work[:, c, 0:2 * ATT_H * HD].rearrange("p (h e) -> p h e", e=HD)
                x1, x2 = qk[:, :, 0:ROPE_HALF], qk[:, :, ROPE_HALF:2 * ROPE_HALF]
                table = lambda n: rope[:, n:n + 1, c * ROPE_HALF:(c + 1) * ROPE_HALF].to_broadcast([P, 2 * ATT_H, ROPE_HALF])
                V.tensor_tensor(tmp[0], x1, table(6), ALU.mult)
                V.tensor_tensor(tmp[1], x2, table(5), ALU.mult)
                V.tensor_tensor(tmp[2], x2, table(6), ALU.mult)
                steps.then(V.tensor_tensor(tmp[3], x1, table(5), ALU.mult))
                V.tensor_tensor(x1, tmp[0], tmp[1], ALU.subtract)
                steps.then(V.tensor_tensor(x2, tmp[2], tmp[3], ALU.add))
            dve.wait_ge(small_full, 6)
            two = xn[:, 1, 640:672].rearrange("p (c w h e) -> p c w h e", c=NT, w=2, e=2)
            steps.then(V.memset(xn[:, 1, 640:672], 1.0))
            steps.then(V.tensor_copy(xn[:, 1, 616:624], SM[1][:, 0:2 * ML_H]))
            for c in range(NT):
                B = xn[:, 1, 616 + ML_H * c:616 + ML_H * (c + 1)].rearrange("p (h e) -> p h e", e=1)
                V.tensor_copy(two[:, c, 0, :, 0:1], B)
                ins = V.tensor_tensor(two[:, c, 1, :, 1:2], gi[:, c, :].rearrange("p (h e) -> p h e", e=1), B, ALU.subtract)
            ins.then_inc(aug_ready, 1)
            bsum = head_ss[:, 0:8]
            V.tensor_copy(bsum, xn[:, 1, 616:624]).then_inc(bsum_ready, 1)
            for g in range(0, 16, 2):
                even_turn(tf, tc, base + g, lambda bank: second_head_copy(
                    V.tensor_copy, lambda o, i_, s_: V.tensor_scalar(o, i_, s_, None, ALU.mult), g, bank))
            base += 16
            attention(att2, 2 * ATT_H, lambda hd, q: work[:, q, hd * HD:(hd + 1) * HD], None, tf, tc, base)
            base += 2 * ATT_H

            dve.wait_ge(bsum_ready, 1)
            dve.wait_ge(out_gate_ready, 1)
            for u in range(2 * ML_H + 3):
                if u < 2 * ML_H:
                    hd, q = u // 2, u % 2
                    nk = P * (q + 1)
                    dve.wait_ge(mls.full, u + 1)
                    steps.then(V.tensor_tensor_reduce(out=G[u % 4][:, 0:nk], in0=G[u % 4][:, 0:nk], in1=causal[:, P * (1 - q):S],
                                                      scale=1.0, scalar=MASKED, op0=ALU.add, op1=ALU.max,
                                                      accum_out=rmax[:, u:u + 1]))
                    steps.then(V.tensor_tensor(rmax[:, u:u + 1], rmax[:, u:u + 1], bsum[:, q * ML_H + hd:q * ML_H + hd + 1], ALU.max))
                    V.tensor_scalar(nmax[:, u:u + 1], rmax[:, u:u + 1], -1.0, None, ALU.mult).then_inc(mls.max_ready, 1)
                    dve.wait_ge(mls.p_ready, u + 1)
                    e_buf = xn_all[:, (u % 4) * S:(u % 4) * S + nk]
                    V.tensor_tensor_reduce(out=e_buf, in0=G[u % 4][:, S:S + nk], in1=e_buf, scale=1.0, scalar=0.0,
                                           op0=ALU.mult, op1=ALU.add, accum_out=rowsum[:, u:u + 1]).then_inc(weights_ready, 1)
                w = u - 2
                if 0 <= w < 2 * ML_H and w % 2 == 0:
                    if w >= 4:
                        dve.wait_ge(mls.out_full, w - 3)
                    even_turn(tf, tc, base + w, lambda bank: V.tensor_copy(xT_all[:, (w % 4) * S:(w % 4) * S + P], bank[:, 0:P]))
                w = u - 3
                if 0 <= w < 2 * ML_H:
                    hd, q = w // 2, w % 2
                    steps.then(V.tensor_scalar(rinv[:, w:w + 1], rowsum[:, w:w + 1], -1.0, None, ALU.mult))
                    steps.then(V.tensor_tensor(rinv[:, w:w + 1], rinv[:, w:w + 1], rowsum[:, w:w + 1], ALU.max))
                    steps.then(V.tensor_tensor(rinv[:, w:w + 1], rinv[:, w:w + 1], expm[:, w:w + 1], ALU.max))
                    steps.then(V.reciprocal(rinv[:, w:w + 1], rinv[:, w:w + 1]))
                    dve.wait_ge(mls.out_full, w + 1)
                    dst = work[:, q, 512 + hd * ML_V:512 + (hd + 1) * ML_V]
                    junk = xn[:, 1, 0:ML_V]
                    V.tensor_scalar(dst, SM[q][:, 0:ML_V], rinv[:, w:w + 1], None, ALU.mult).then_inc(mls.out_done, 1)
                    dve.wait_ge(mls.out_done, w + 1)
                    steps.then(V.tensor_tensor_reduce(out=junk, in0=dst, in1=dst, scale=1.0, scalar=0.0, op0=ALU.mult,
                                                      op1=ALU.add, accum_out=hss[:, w:w + 1]))
            inverse_rms(hss, hss, ML_V)
            for w in range(2 * ML_H):
                hd, q = w // 2, w % 2
                dst = work[:, q, 512 + hd * ML_V:512 + (hd + 1) * ML_V]
                V.scalar_tensor_tensor(out=dst, in0=dst, scalar=hss[:, w:w + 1],
                                       in1=work[:, q, MO + hd * ML_V:MO + (hd + 1) * ML_V],
                                       op0=ALU.mult, op1=ALU.mult).then_inc(hm_ready, 1)
            base += 2 * ML_H
            norm_copies(tf, tc, base, [(xT, GC["mix"])])
            base += 4

            def post_norm(nth, gain, ready):
                dve.wait_ge(post_squares, 4 * nth)
                dve.wait_ge(post_landed, 16 * nth)
                for c in range(NT):
                    steps.then(V.tensor_tensor(ss[:, c:c + 1], ss4[:, 2 * c:2 * c + 1], ss4[:, 2 * c + 1:2 * c + 2], ALU.add))
                inverse_rms(rstd, ss, D)
                for b in range(4):
                    c, at = b // 2, (b % 2) * BANK
                    steps.then(V.scalar_tensor_tensor(out=xn[:, c, at:at + BANK], in0=G[b][:, :], scalar=rstd[:, c:c + 1],
                                                      in1=gain[:, at:at + BANK], op0=ALU.mult, op1=ALU.mult))
                    dst = h[:, c, at:at + BANK]
                    V.tensor_tensor(dst, dst, xn[:, c, at:at + BANK], ALU.add).then_inc(h_ready, 1)

            post_norm(1, post_gain1, 16)

            norm(6, tf, tc, base, [(xT, GC["mlp2"])], splits=mu)
            base += 4

            def squared(n, c, first, turned_before):
                dve.wait_ge(mu.done, n + 1)
                if not first:
                    dve.wait_ge(tf, turned_before)
                V.tensor_tensor(xn[:, c, BANK:2 * BANK], xn[:, c, 0:BANK], xn[:, c, 0:BANK], ALU.mult).then_inc(relu2_ready, 1)

            def mlp_slab(i, j, first, last=False):
                if last:
                    down_units(make_low, dve, mu, md, 0, 2)
                else:
                    up_units(make_low, dve, mu, i + j, 1 - j)
                for c in range(NT):
                    if not first:
                        hidden_low(tc, i * 4 + (2 * j - 2 + c), i * 2 + (j - 1), c, 4)
                for c in range(NT):
                    squared(i * 4 + (2 * j + c), c, first, i * 4 + (2 * j + c - 1 + base))

            mlp_slab(0, 0, True)
            mlp_slab(0, 1, False)
            with dve.Fori(1, mu.slabs // 2 - 1) as i:
                for j in range(2):
                    mlp_slab(i, j, False)
            mlp_slab(mu.slabs // 2 - 1, 0, False)
            mlp_slab(mu.slabs // 2 - 1, 1, False, last=True)
            for c in range(NT):
                hidden_low(tc, 2 * mu.slabs - 2 + c, mu.slabs - 1, c, 4)
            down_units(make_low, dve, mu, md, 2, md.units)
            post_norm(2, post_gain2, 20)


_INS = ["x", "a_norm_g", "a_w_in", "a_v_norm_g", "a_w_spatial", "a_b_spatial", "a_w_out", "f_norm_g", "f_w_in",
        "f_w_out", "kv_norm_g", "kv_w", "kv_b_f", "k_norm_g", "b_norm_g", "b_w_in", "q_norm_g", "b_w_out", "m_norm_g",
        "m_w_router", "m_w_in", "m_w_out", "positions_2", "g_mix_pre_2", "w_in_2", "b_igate_2", "b_fgate_2",
        "g_mlstm_out_2", "w_out_2", "g_mix_post_2", "g_mlp_pre_2", "w_up_2", "w_down_2", "g_mlp_post_2"]


def kernel(**inputs):
    import concourse.bacc as bacc
    from concourse.bass_utils import run_bass_kernel_spmd as run

    nc = bacc.Bacc("TRN2", target_bir_lowering=False, num_devices=1)
    arrays, args = {}, {}
    for name in _INS:
        a = np.ascontiguousarray(inputs[name])
        arrays[f"in_{name}_dram"] = a
        args[name] = nc.dram_tensor(f"in_{name}_dram", a.shape, mybir.dt.from_np(a.dtype), kind="ExternalInput").ap()
    out = nc.dram_tensor("out_0_dram", (1, S, D), F32, kind="ExternalOutput").ap()
    build(nc, args, out)
    r = run(nc, [arrays], core_ids=[0])
    return r.results[0]["out_0_dram"]
```
